# Optimizing a Trainium2 kernel written in Bass

```python
import math
import jax, jax.numpy as jnp
from jax import lax
import numpy as np

D_MODEL = 1024
BATCH = 1
SEQ = 512
DEPTH = 1

DA_HEADS = 8
DA_DH = 64
DA_QK = DA_HEADS * 2 * DA_DH
DA_V = DA_HEADS * 2 * DA_DH
DA_QBLOCK = 128
ROPE_THETA = 10000.0

GDN_HEADS = 8
GDN_DK = 128
GDN_DV = 128
GDN_QK = GDN_HEADS * GDN_DK
GDN_VW = GDN_HEADS * GDN_DV
GDN_CONV_DIM = 2 * GDN_QK + GDN_VW
CONV_K = 5
GDN_CHUNK = 64

N_EXPERTS = 16
EXPERT_FF = 2048
CAP_FACTOR = 2

NORM_EPS = 1e-6
IN_WIDTH = 2 * DA_QK + DA_V + GDN_CONV_DIM + GDN_VW + 4 * GDN_HEADS + 2 * D_MODEL


def rmsnorm(t, w, eps=NORM_EPS):
    t32 = t.astype(jnp.float32)
    y = t32 * lax.rsqrt(jnp.mean(t32 * t32, axis=-1, keepdims=True) + eps)
    return (y * w.astype(jnp.float32)).astype(t.dtype)

def l2norm(t, eps=1e-6):
    t32 = t.astype(jnp.float32)
    return t32 * lax.rsqrt(jnp.sum(t32 * t32, axis=-1, keepdims=True) + eps)

def rope_tables(seq, dim):
    inv = ROPE_THETA ** (-jnp.arange(0, dim, 2, dtype=jnp.float32) / dim)
    ang = jnp.arange(seq, dtype=jnp.float32)[:, None] * inv[None, :]
    ang = jnp.concatenate([ang, ang], axis=-1)
    return jnp.cos(ang), jnp.sin(ang)

def apply_rope(t, cos, sin):
    half = t.shape[-1] // 2
    t32 = t.astype(jnp.float32)
    rot = jnp.concatenate([-t32[..., half:], t32[..., :half]], axis=-1)
    shp = (1, t.shape[1]) + (1,) * (t.ndim - 3) + (t.shape[-1],)
    return (t32 * cos.reshape(shp) + rot * sin.reshape(shp)).astype(t.dtype)

def diff_attention(q, k, v, lam):
    b, s, h, _, dh = q.shape
    nb = s // DA_QBLOCK
    scale = dh ** -0.5
    qb = jnp.moveaxis(q.reshape(b, nb, DA_QBLOCK, h, 2, dh), 1, 0)

    def block(qblk):
        sc = jnp.einsum('bqhtd,bkhtd->bhtqk', qblk, k).astype(jnp.float32) * scale
        pr = jax.nn.softmax(sc, axis=-1)
        pd = pr[:, :, 0] - lam * pr[:, :, 1]
        return jnp.einsum('bhqk,bkhe->bqhe', pd.astype(v.dtype), v)

    o = lax.map(block, qb)
    return jnp.moveaxis(o, 0, 1).reshape(b, s, h, v.shape[-1])

def gated_delta_rule_chunked(q, k, v, g, beta):
    b, s, h, dk = q.shape
    dv = v.shape[-1]
    n = s // GDN_CHUNK

    def chunks(t):
        t = t.astype(jnp.float32).reshape((b, n, GDN_CHUNK, h) + t.shape[3:])
        return jnp.moveaxis(t, 3, 1)

    q = chunks(q) * dk ** -0.5
    k = chunks(k)
    v = chunks(v)
    g = jnp.cumsum(chunks(g), axis=-1)
    beta = chunks(beta)

    incl = jnp.tril(jnp.ones((GDN_CHUNK, GDN_CHUNK), dtype=bool))
    strict = jnp.tril(jnp.ones((GDN_CHUNK, GDN_CHUNK), dtype=bool), k=-1)
    gdiff = g[..., :, None] - g[..., None, :]
    decay = jnp.where(incl, jnp.exp(jnp.where(incl, gdiff, 0.0)), 0.0)

    k_beta = k * beta[..., None]
    a_mat = jnp.where(strict, jnp.einsum('bhnid,bhnjd->bhnij', k_beta, k) * decay, 0.0)
    t_mat = a_mat + jnp.eye(GDN_CHUNK, dtype=jnp.float32)
    rhs = jnp.concatenate([v * beta[..., None], k_beta * jnp.exp(g)[..., None]], axis=-1)
    sol = lax.linalg.triangular_solve(t_mat, rhs, left_side=True, lower=True,
                                      unit_diagonal=True)
    u, w = sol[..., :dv], sol[..., dv:]

    qk = jnp.where(incl, jnp.einsum('bhnid,bhnjd->bhnij', q, k) * decay, 0.0)
    q_dec = q * jnp.exp(g)[..., None]
    k_dec = k * jnp.exp(g[..., -1:] - g)[..., None]
    g_last = jnp.exp(g[..., -1])

    def step(state, inp):
        qk_c, qd_c, kd_c, u_c, w_c, gl_c = inp
        v_new = u_c - jnp.einsum('bhcd,bhde->bhce', w_c, state)
        o_c = (jnp.einsum('bhcd,bhde->bhce', qd_c, state)
               + jnp.einsum('bhij,bhje->bhie', qk_c, v_new))
        state = state * gl_c[..., None, None] + jnp.einsum('bhcd,bhce->bhde', kd_c, v_new)
        return state, o_c

    xs = tuple(jnp.moveaxis(t, 2, 0) for t in (qk, q_dec, k_dec, u, w, g_last))
    state0 = jnp.zeros((b, h, dk, dv), jnp.float32)
    _, o = lax.scan(step, state0, xs)
    o = jnp.moveaxis(o, 0, 2)
    return jnp.moveaxis(o, 1, 3).reshape(b, s, h, dv)

def centred_depthwise_conv(t, w):
    c = t.shape[-1]
    pad = CONV_K // 2
    return lax.conv_general_dilated(
        t, w[:, None, :].astype(t.dtype), window_strides=(1,), padding=[(pad, pad)],
        dimension_numbers=('NWC', 'WIO', 'NWC'), feature_group_count=c)

def expert_choice_ffn(h, w_router, w_gate, w_up, w_down):
    b, s, d = h.shape
    cap = CAP_FACTOR * s // N_EXPERTS
    logits = jnp.einsum('bsd,de->bse', h, w_router).astype(jnp.float32)
    aff = jax.nn.softmax(logits, axis=-1)
    top_val, top_idx = lax.top_k(jnp.swapaxes(aff, 1, 2), cap)
    xs = jax.vmap(lambda hb, ib: hb[ib])(h, top_idx)
    gt = jnp.einsum('becd,edf->becf', xs, w_gate)
    up = jnp.einsum('becd,edf->becf', xs, w_up)
    ye = jnp.einsum('becf,efd->becd', jax.nn.silu(gt) * up, w_down)
    ye = ye * top_val[..., None].astype(ye.dtype)

    def scatter(yb, ib):
        return jnp.zeros((s, d), yb.dtype).at[ib.reshape(-1)].add(yb.reshape(-1, d))

    return jax.vmap(scatter)(ye, top_idx)

def first_inputs(seed: int = 0) -> dict:
    key = jax.random.key(seed)
    ks = jax.random.split(key, 32)
    f32 = jnp.float32

    def nrm(k, shape, scale):
        return jax.random.normal(k, shape, f32) * scale

    def gain(k, n):
        return 1.0 + 0.02 * jax.random.normal(k, (DEPTH, n), f32)

    def a_log(k):
        return jnp.log(jax.random.uniform(k, (DEPTH, GDN_HEADS), f32, 1.0, 16.0))

    def dt_bias(k):
        dt = jnp.exp(jax.random.uniform(k, (DEPTH, GDN_HEADS), f32,
                                        math.log(1e-3), math.log(1e-1)))
        return dt + jnp.log(-jnp.expm1(-dt))

    return {
        "x": nrm(ks[0], (BATCH, SEQ, D_MODEL), 1.0),
        "norm1_w": gain(ks[1], D_MODEL),
        "w_in": nrm(ks[2], (DEPTH, D_MODEL, IN_WIDTH), D_MODEL ** -0.5),
        "conv_w": nrm(ks[3], (DEPTH, CONV_K, GDN_CONV_DIM), CONV_K ** -0.5),
        "a_log_fwd": a_log(ks[4]),
        "dt_bias_fwd": dt_bias(ks[5]),
        "a_log_bwd": a_log(ks[6]),
        "dt_bias_bwd": dt_bias(ks[7]),
        "gdn_norm_w": gain(ks[8], GDN_DV),
        "lambda_q1": nrm(ks[9], (DEPTH, DA_DH), 0.1),
        "lambda_k1": nrm(ks[10], (DEPTH, DA_DH), 0.1),
        "lambda_q2": nrm(ks[11], (DEPTH, DA_DH), 0.1),
        "lambda_k2": nrm(ks[12], (DEPTH, DA_DH), 0.1),
        "subln_w": gain(ks[13], 2 * DA_DH),
        "w_proj_attn": nrm(ks[14], (DEPTH, DA_V, D_MODEL), DA_V ** -0.5),
        "w_proj_gdn": nrm(ks[15], (DEPTH, GDN_VW, D_MODEL), GDN_VW ** -0.5),
        "w_out": nrm(ks[16], (DEPTH, D_MODEL, D_MODEL), D_MODEL ** -0.5),
        "norm2_w": gain(ks[17], D_MODEL),
        "w_router": nrm(ks[18], (DEPTH, D_MODEL, N_EXPERTS), D_MODEL ** -0.5),
        "w_gate": nrm(ks[19], (DEPTH, N_EXPERTS, D_MODEL, EXPERT_FF), D_MODEL ** -0.5),
        "w_up": nrm(ks[20], (DEPTH, N_EXPERTS, D_MODEL, EXPERT_FF), D_MODEL ** -0.5),
        "w_down": nrm(ks[21], (DEPTH, N_EXPERTS, EXPERT_FF, D_MODEL), EXPERT_FF ** -0.5),
        "norm_f_w": 1.0 + 0.02 * jax.random.normal(ks[22], (D_MODEL,), f32),
    }

def first_block(x, norm1_w, w_in, conv_w, a_log_fwd, dt_bias_fwd, a_log_bwd, dt_bias_bwd,
              gdn_norm_w, lambda_q1, lambda_k1, lambda_q2, lambda_k2, subln_w,
              w_proj_attn, w_proj_gdn, w_out, norm2_w, w_router, w_gate, w_up, w_down,
              norm_f_w):
    b, s, _ = x.shape
    cos, sin = rope_tables(s, DA_DH)
    sizes = [DA_QK, DA_QK, DA_V, GDN_CONV_DIM, GDN_VW,
             GDN_HEADS, GDN_HEADS, GDN_HEADS, GDN_HEADS, D_MODEL, D_MODEL]
    split_at = [int(v) for v in np.cumsum(sizes)[:-1]]

    for l in range(DEPTH):
        lambda_init = 0.8 - 0.6 * math.exp(-0.3 * l)
        h = rmsnorm(x, norm1_w[l])
        p = jnp.einsum('bsd,dn->bsn', h, w_in[l])
        (qa, ka, va, qkv_g, z, a_f, a_b, b_f, b_b, gate_a, gate_g) = jnp.split(p, split_at, axis=-1)

        qa = apply_rope(qa.reshape(b, s, DA_HEADS, 2, DA_DH), cos, sin)
        ka = apply_rope(ka.reshape(b, s, DA_HEADS, 2, DA_DH), cos, sin)
        va = va.reshape(b, s, DA_HEADS, 2 * DA_DH)
        lam = (jnp.exp(jnp.sum(lambda_q1[l].astype(jnp.float32) * lambda_k1[l].astype(jnp.float32)))
               - jnp.exp(jnp.sum(lambda_q2[l].astype(jnp.float32) * lambda_k2[l].astype(jnp.float32)))
               + lambda_init)
        oa = diff_attention(qa, ka, va, lam)
        oa = rmsnorm(oa, subln_w[l]) * (1.0 - lambda_init)
        ya = jnp.einsum('bse,ed->bsd', oa.reshape(b, s, DA_V).astype(x.dtype), w_proj_attn[l])

        qkv_g = jax.nn.silu(centred_depthwise_conv(qkv_g, conv_w[l]))
        qg, kg, vg = jnp.split(qkv_g, [GDN_QK, 2 * GDN_QK], axis=-1)
        qg = l2norm(qg.reshape(b, s, GDN_HEADS, GDN_DK))
        kg = l2norm(kg.reshape(b, s, GDN_HEADS, GDN_DK))
        vg = vg.reshape(b, s, GDN_HEADS, GDN_DV).astype(jnp.float32)
        g_f = -jnp.exp(a_log_fwd[l].astype(jnp.float32)) * jax.nn.softplus(
            (a_f + dt_bias_fwd[l]).astype(jnp.float32))
        g_b = -jnp.exp(a_log_bwd[l].astype(jnp.float32)) * jax.nn.softplus(
            (a_b + dt_bias_bwd[l]).astype(jnp.float32))
        beta_f = jax.nn.sigmoid(b_f.astype(jnp.float32))
        beta_b = jax.nn.sigmoid(b_b.astype(jnp.float32))
        o_fwd = gated_delta_rule_chunked(qg, kg, vg, g_f, beta_f)
        flip = lambda t: jnp.flip(t, axis=1)
        o_bwd = flip(gated_delta_rule_chunked(flip(qg), flip(kg), flip(vg), flip(g_b), flip(beta_b)))
        og = rmsnorm(o_fwd + o_bwd, gdn_norm_w[l])
        og = og * jax.nn.silu(z.reshape(b, s, GDN_HEADS, GDN_DV).astype(jnp.float32))
        yg = jnp.einsum('bse,ed->bsd', og.reshape(b, s, GDN_VW).astype(x.dtype), w_proj_gdn[l])

        merged = jax.nn.sigmoid(gate_a) * ya + jax.nn.sigmoid(gate_g) * yg
        x = x + jnp.einsum('bsd,de->bse', merged, w_out[l])

        h2 = rmsnorm(x, norm2_w[l])
        x = x + expert_choice_ffn(h2, w_router[l], w_gate[l], w_up[l], w_down[l])

    return rmsnorm(x, norm_f_w)


CHUNK = 64
Q_BLOCK = 128

A_HEADS = 4
A_HEAD_DIM = 128
A_WIDTH = A_HEADS * A_HEAD_DIM
A_KV_RANK = 128
IDX_HEADS = 8
IDX_DIM = 64
TOPK_MAX = 256

B_HEADS = 4
B_KEY_DIM = 128
B_VAL_DIM = 128
B_WIDTH = B_HEADS * B_VAL_DIM
B_FORGET = B_HEADS * B_KEY_DIM

D_MIX = A_WIDTH + B_WIDTH

REL_BUCKETS = 32
REL_MAX_DIST = 256

DEEPNORM_ALPHA = (2.0 * DEPTH) ** 0.25
DEEPNORM_BETA = (8.0 * DEPTH) ** -0.25
LN_EPS = 1e-5
RMS_EPS = 1e-6

_SPLITS = (
    ('a_q', A_WIDTH),
    ('a_ckv', A_KV_RANK),
    ('a_iq', IDX_HEADS * IDX_DIM),
    ('a_ik', IDX_DIM),
    ('a_iw', IDX_HEADS),
    ('a_gate', A_WIDTH),
    ('b_q', B_FORGET),
    ('b_f', B_FORGET),
    ('b_i', B_WIDTH),
    ('b_gate', B_WIDTH),
)
D_IN_PROJ = int(sum(n for _, n in _SPLITS))
SPLIT_POINTS = tuple(int(v) for v in np.cumsum([n for _, n in _SPLITS])[:-1])


def _rms_norm(x, g):
    xf = x.astype(jnp.float32)
    y = xf * lax.rsqrt(jnp.mean(xf * xf, axis=-1, keepdims=True) + RMS_EPS)
    return (y * g.astype(jnp.float32)).astype(x.dtype)

def _layer_norm(x, g, b):
    xf = x.astype(jnp.float32)
    mu = jnp.mean(xf, axis=-1, keepdims=True)
    var = jnp.mean(jnp.square(xf - mu), axis=-1, keepdims=True)
    y = (xf - mu) * lax.rsqrt(var + LN_EPS) * g.astype(jnp.float32) + b.astype(jnp.float32)
    return y.astype(x.dtype)

def _t5_bucket(rel):
    nb = REL_BUCKETS // 2
    max_exact = nb // 2
    ret = jnp.where(rel > 0, nb, 0).astype(jnp.int32)
    n = jnp.abs(rel)
    nf = jnp.maximum(n, 1).astype(jnp.float32)
    large = max_exact + (jnp.log(nf / max_exact) / math.log(REL_MAX_DIST / max_exact)
                         * (nb - max_exact)).astype(jnp.int32)
    large = jnp.minimum(large, nb - 1)
    return ret + jnp.where(n < max_exact, n, large)

def _dsa_mixer(q, c, iq, ik, iw, w_uk, rel_bias):
    bsz, seq = q.shape[0], q.shape[1]
    k_sel = min(TOPK_MAX, seq // 4)
    n_blk = seq // Q_BLOCK
    q_lat = jnp.einsum('bshd,hdr->bshr', q, w_uk)
    scale = A_HEAD_DIM ** -0.5
    idx_scale = IDX_DIM ** -0.5
    w_scale = IDX_HEADS ** -0.5
    pos = jnp.arange(seq, dtype=jnp.int32)
    key_chunk = pos // CHUNK

    def blockify(t):
        return jnp.moveaxis(t.reshape(bsz, n_blk, Q_BLOCK, *t.shape[2:]), 1, 0)

    xs = (blockify(q_lat), blockify(iq), blockify(iw), pos.reshape(n_blk, Q_BLOCK))

    def one_block(args):
        ql, iqb, iwb, qpos = args
        q_chunk = qpos // CHUNK
        admissible = key_chunk[None, :] <= q_chunk[:, None]
        dots = jnp.einsum('bqhd,bsd->bqhs', iqb, ik) * idx_scale
        score = jnp.einsum('bqh,bqhs->bqs', iwb * w_scale, jax.nn.relu(dots))
        score = jnp.where(admissible[None], score.astype(jnp.float32), -jnp.inf)
        _, sel = lax.top_k(score, k_sel)
        valid = (sel // CHUNK) <= q_chunk[None, :, None]
        c_sel = jax.vmap(lambda cb, ib: cb[ib])(c, sel)
        bias = rel_bias[_t5_bucket(sel - qpos[None, :, None])]
        logits = (jnp.einsum('bqhr,bqkr->bqhk', ql, c_sel).astype(jnp.float32) * scale
                  + jnp.swapaxes(bias, -1, -2).astype(jnp.float32))
        logits = jnp.where(valid[:, :, None, :], logits, -jnp.inf)
        p = jax.nn.softmax(logits, axis=-1).astype(c.dtype)
        return jnp.einsum('bqhk,bqkr->bqhr', p, c_sel)

    o = lax.map(one_block, xs)
    return jnp.moveaxis(o, 0, 1).reshape(bsz, seq, A_HEADS, A_KV_RANK)

def _hgrn2_mixer(q, f_raw, v, lb):
    bsz, seq = q.shape[0], q.shape[1]
    n_chunk = seq // CHUNK
    q = jax.nn.silu(q.astype(jnp.float32))
    lbh = lb.reshape(B_HEADS, B_KEY_DIM).astype(jnp.float32)
    f = lbh + (1.0 - lbh) * jax.nn.sigmoid(f_raw.astype(jnp.float32))
    k = 1.0 - f
    log_f = jnp.log(f)

    def chunkify(t):
        return jnp.transpose(t.reshape(bsz, n_chunk, CHUNK, B_HEADS, t.shape[-1]), (1, 0, 3, 2, 4))

    qc, kc, vc = chunkify(q), chunkify(k), chunkify(v.astype(jnp.float32))
    bc = jnp.cumsum(chunkify(log_f), axis=3)
    causal = jnp.tril(jnp.ones((CHUNK, CHUNK), dtype=bool))

    def step(state, inp):
        qn, kn, vn, bn = inp
        diff = bn[:, :, :, None, :] - bn[:, :, None, :, :]
        decay = jnp.exp(jnp.where(causal[:, :, None], diff, -jnp.inf))
        scores = jnp.einsum('bhtk,bhsk,bhtsk->bhts', qn, kn, decay)
        o = (jnp.einsum('bhts,bhsv->bhtv', scores, vn)
             + jnp.einsum('bhtk,bhkv->bhtv', qn * jnp.exp(bn), state))
        b_last = bn[:, :, -1:, :]
        state = (jnp.exp(b_last[:, :, 0, :])[..., None] * state
                 + jnp.einsum('bhsk,bhsv->bhkv', kn * jnp.exp(b_last - bn), vn))
        return state, o

    s0 = jnp.zeros((bsz, B_HEADS, B_KEY_DIM, B_VAL_DIM), jnp.float32)
    _, o = lax.scan(step, s0, (qc, kc, vc, bc))
    return jnp.transpose(o, (1, 0, 3, 2, 4)).reshape(bsz, seq, B_HEADS, B_VAL_DIM)

def second_inputs(seed: int = 0) -> dict:
    key = jax.random.key(seed)
    ks = jax.random.split(key, 12)
    x = jax.random.normal(ks[0], (BATCH, SEQ, D_MODEL), jnp.float32)
    col_scale = jnp.concatenate([
        jnp.full((n,), DEEPNORM_BETA if name == 'b_i' else 1.0, jnp.float32) for name, n in _SPLITS])
    w_in = jax.random.normal(ks[1], (DEPTH, D_MODEL, D_IN_PROJ), jnp.float32) * (D_MODEL ** -0.5) * col_scale
    w_uk = jax.random.normal(ks[2], (DEPTH, A_HEADS, A_HEAD_DIM, A_KV_RANK), jnp.float32) * (A_HEAD_DIM ** -0.5)
    w_uv = (jax.random.normal(ks[3], (DEPTH, A_HEADS, A_KV_RANK, A_HEAD_DIM), jnp.float32)
            * (A_KV_RANK ** -0.5) * DEEPNORM_BETA)
    kv_norm_g = 1.0 + 0.05 * jax.random.normal(ks[4], (DEPTH, A_KV_RANK), jnp.float32)
    rel_bias = 0.2 * jax.random.normal(ks[5], (REL_BUCKETS, A_HEADS), jnp.float32)
    lb_logits = 0.5 * jax.random.normal(ks[6], (DEPTH + 1, B_FORGET), jnp.float32)
    hgrn_norm_g = 1.0 + 0.05 * jax.random.normal(ks[7], (DEPTH, B_WIDTH), jnp.float32)
    w_o = jax.random.normal(ks[8], (DEPTH, D_MIX, D_MODEL), jnp.float32) * (D_MIX ** -0.5) * DEEPNORM_BETA
    ln_g = 1.0 + 0.05 * jax.random.normal(ks[9], (DEPTH, D_MODEL), jnp.float32)
    ln_b = 0.02 * jax.random.normal(ks[10], (DEPTH, D_MODEL), jnp.float32)
    return {'x': x, 'w_in': w_in, 'w_uk': w_uk, 'w_uv': w_uv, 'kv_norm_g': kv_norm_g,
            'rel_bias': rel_bias, 'lb_logits': lb_logits, 'hgrn_norm_g': hgrn_norm_g,
            'w_o': w_o, 'ln_g': ln_g, 'ln_b': ln_b}

def second_block(x, w_in, w_uk, w_uv, kv_norm_g, rel_bias, lb_logits, hgrn_norm_g, w_o, ln_g, ln_b):
    bsz, seq, _ = x.shape
    lb_all = jnp.cumsum(jax.nn.softmax(lb_logits.astype(jnp.float32), axis=0), axis=0)
    for layer in range(DEPTH):
        h = jnp.einsum('bsd,dc->bsc', x, w_in[layer])
        a_q, a_ckv, a_iq, a_ik, a_iw, a_gate, b_q, b_f, b_i, b_gate = jnp.split(h, SPLIT_POINTS, axis=-1)

        c = _rms_norm(a_ckv, kv_norm_g[layer])
        o_lat = _dsa_mixer(a_q.reshape(bsz, seq, A_HEADS, A_HEAD_DIM), c,
                           a_iq.reshape(bsz, seq, IDX_HEADS, IDX_DIM), a_ik, a_iw,
                           w_uk[layer], rel_bias)
        o_a = jnp.einsum('bshr,hrv->bshv', o_lat, w_uv[layer]).reshape(bsz, seq, A_WIDTH)
        o_a = o_a * jax.nn.silu(a_gate)

        o_b = _hgrn2_mixer(b_q.reshape(bsz, seq, B_HEADS, B_KEY_DIM),
                           b_f.reshape(bsz, seq, B_HEADS, B_KEY_DIM),
                           b_i.reshape(bsz, seq, B_HEADS, B_VAL_DIM), lb_all[layer])
        o_b = _rms_norm(o_b, hgrn_norm_g[layer].reshape(B_HEADS, B_VAL_DIM)).reshape(bsz, seq, B_WIDTH)
        o_b = o_b.astype(x.dtype) * jax.nn.silu(b_gate)

        y = jnp.einsum('bsc,cd->bsd', jnp.concatenate([o_a.astype(x.dtype), o_b], axis=-1), w_o[layer])
        x = _layer_norm(DEEPNORM_ALPHA * x + y, ln_g[layer], ln_b[layer])
    return x


def setup_inputs(seed=0):
    out = dict(first_inputs(seed))
    for name, value in second_inputs(seed + 1).items():
        if name != "x":
            out[name + "_2"] = value
    return out


def reference(
    x, norm1_w, w_in, conv_w, a_log_fwd, dt_bias_fwd, a_log_bwd, dt_bias_bwd, gdn_norm_w,
    lambda_q1, lambda_k1, lambda_q2, lambda_k2, subln_w, w_proj_attn, w_proj_gdn, w_out,
    norm2_w, w_router, w_gate, w_up, w_down, norm_f_w, w_in_2, w_uk_2, w_uv_2, kv_norm_g_2,
    rel_bias_2, lb_logits_2, hgrn_norm_g_2, w_o_2, ln_g_2, ln_b_2,
):
    x = first_block(
        x, norm1_w, w_in, conv_w, a_log_fwd, dt_bias_fwd, a_log_bwd, dt_bias_bwd, gdn_norm_w,
        lambda_q1, lambda_k1, lambda_q2, lambda_k2, subln_w, w_proj_attn, w_proj_gdn, w_out,
        norm2_w, w_router, w_gate, w_up, w_down, norm_f_w,
    )
    return second_block(
        x, w_in_2, w_uk_2, w_uv_2, kv_norm_g_2, rel_bias_2, lb_logits_2, hgrn_norm_g_2, w_o_2,
        ln_g_2, ln_b_2,
    )


_drawn_inputs = setup_inputs


def setup_inputs(seed=0):
    import zlib

    import numpy as np

    out = dict(_drawn_inputs(seed))
    spreads = {}
    factors = {'gdn_norm_w': 5.323,
     'lambda_q1': 5.717,
     'lambda_k1': 8.0,
     'subln_w': 4.576,
     'norm2_w': 4.173,
     'norm_f_w': 2.734,
     'w_uk_2': 3.175,
     'kv_norm_g_2': 8.0,
     'rel_bias_2': 8.0,
     'lb_logits_2': 4.594,
     'hgrn_norm_g_2': 5.81,
     'ln_b_2': 2.87}
    for name, (base, spread) in spreads.items():
        noise = np.random.default_rng([zlib.crc32(name.encode()), seed]).standard_normal(out[name].shape)
        drawn = base * np.exp(spread * noise) if base else spread * noise
        out[name] = __import__('jax').numpy.asarray(drawn.astype(out[name].dtype))
    for name, factor in factors.items():
        out[name] = (out[name] * factor).astype(out[name].dtype)
    return out
```

```python
import math
from contextlib import ExitStack

import numpy as np
import concourse.bass as bass
from concourse import mybir

F32 = mybir.dt.float32
ALU = mybir.AluOpType
ACT = mybir.ActivationFunctionType
AX = mybir.AxisListType.X

P = 128
S = 512
NT = S // P
D = 1024
KD = D // P
HEADS = 8
EPS = 1e-6
LAMBDA_INIT = 0.8 - 0.6 * math.exp(0.0)
CONV_K = 5
NE = 16
FF = 2048
CAP = 2 * S // NE
SLAB = 4096
QA, KA, VA, QKVG, ZG, AB = 0, 1024, 2048, 3072, 6144, 7168
GATE_A, GATE_G = 7200, 8224
A_Q, A_CKV, A_IQ, A_IK, A_IW, A_GATE, B_Q, B_F, B_I, B_GATE = 0, 512, 640, 1152, 1216, 1224, 1736, 2248, 2760, 3272
LEVELS = [1, 2, 4, 8, 16, 32, 64]
NL = len(LEVELS)
TOPK = 128
BIG = 3.0e38
STRUCK = 3.2e38
ALPHA = 2.0 ** 0.25
REL = 640
T_ID, T_ONE, T_LE, T_GE, T_LOW = 0, 128, 256, 384, 512
T_UP = T_LOW + NL * P
T_IOTA = T_UP + NL * P
T_KEEP = T_IOTA + CAP
T_ROT = T_KEEP
T_COS = T_ROT + P
T_SIN = T_COS + S
T_BUCKET = T_SIN + S
T_ALL = T_BUCKET + REL


def shape_table():
    i, j = np.arange(P)[:, None], np.arange(P)[None, :]
    t = np.zeros((P, T_ALL), np.float32)
    t[:, T_ID:T_ID + P] = i == j
    t[:, T_ONE:T_ONE + P] = 1.0
    t[:, T_LE:T_LE + P] = i <= j
    t[:, T_GE:T_GE + P] = i >= j
    for n, s in enumerate(LEVELS):
        low = (i // (2 * s) == j // (2 * s)) & (i % (2 * s) >= s) & (j % (2 * s) < s)
        t[:, T_LOW + n * P:T_LOW + (n + 1) * P] = low
        t[:, T_UP + n * P:T_UP + (n + 1) * P] = low.T
    t[:, T_IOTA:T_IOTA + CAP] = np.arange(1, CAP + 1)
    rot = np.zeros((P, P), np.float32)
    for b in (0, 64):
        for m in range(32):
            rot[b + m + 32, b + m] = -1.0
            rot[b + m, b + m + 32] = 1.0
    t[:, T_ROT:T_ROT + P] = rot
    inv = np.float32(10000.0) ** (-np.arange(0, 64, 2, dtype=np.float32) / np.float32(64))
    ang = np.arange(S, dtype=np.float32)[None, :] * inv[np.arange(P) % 32][:, None]
    t[:, T_COS:T_COS + S] = np.cos(ang)
    t[:, T_SIN:T_SIN + S] = np.sin(ang)
    rel = np.arange(REL) - 511
    n = np.abs(rel)
    nf = np.maximum(n, 1).astype(np.float32)
    large = 8 + (np.log(nf / np.float32(8)) / np.float32(math.log(256 / 8)) * np.float32(8)).astype(np.int32)
    bucket = np.where(rel > 0, 16, 0) + np.where(n < 8, n, np.minimum(large, 15))
    for u in range(REL):
        t[bucket[u], T_BUCKET + u] = 1.0
    return t


LN_SUB, LN_DK, LN_EPS = 1, 2, 3
BIASES = (EPS, math.log(1.0 - LAMBDA_INIT), -0.5 * math.log(P), 1e-5)


class Chain:

    def __init__(self, eng, own, counts):
        self.eng, self.own, self.counts = eng, own, counts

    def __call__(self, ins, sem=None, last=True):
        sem = self.own if sem is None else sem
        ins.then_inc(sem, 1)
        key = id(sem)
        self.counts[key] = self.counts.get(key, 0) + 1
        if last:
            self.eng.wait_ge(sem, self.counts[key])


def build(nc, io, upto=99, dump=None):
    ctx = ExitStack()
    counts = {}
    with ctx:
        def sb(name, cols):
            return ctx.enter_context(nc.sbuf_tensor(name, [P, cols], F32))

        spent, cleared = [], []

        def sem(name):
            return cleared.pop(0) if cleared else ctx.enter_context(nc.semaphore(name))

        def clear_spent():
            with nc.Block() as block:
                @block.gpsimd
                def _(pool):
                    for s_ in spent:
                        pool.sem_clear(s_)
            for s_ in spent:
                counts.pop(id(s_), None)
            cleared.extend(spent)
            spent.clear()

        tab = sb("tab", T_KEEP)
        ident, ones = tab[:, T_ID:T_ID + P], tab[:, T_ONE:T_ONE + P]
        tri_le, tri_ge = tab[:, T_LE:T_LE + P], tab[:, T_GE:T_GE + P]
        low = [tab[:, T_LOW + n * P:T_LOW + (n + 1) * P] for n in range(NL)]
        up = [tab[:, T_UP + n * P:T_UP + (n + 1) * P] for n in range(NL)]
        iota = tab[:, T_IOTA:T_IOTA + CAP]
        X = sb("X", NT * D)
        HT = sb("HT", KD * S)
        SL = [sb(f"SL{i}", SLAB) for i in range(4)]
        R12 = sb("R12", 2 * SLAB)
        R = [None, R12[:, 0:SLAB], R12[:, SLAB:2 * SLAB]] + [sb(f"R{i}", SLAB) for i in range(3, 7)]
        wab_ = sb("wab", KD * 32)
        small = sb("small", 1100)
        x3 = X[:, :].rearrange("p (t d) -> p t d", t=NT)
        hT = HT[:, :].rearrange("p (k s) -> p k s", k=KD)
        at = [0]

        def take(n):
            at[0] += n
            assert at[0] <= 1100
            return small[:, at[0] - n:at[0]]

        convw = take(120)
        vcols = take(30)
        norm1c, sublnc, gdnc = vcols[:, 0:8], vcols[:, 16:17], vcols[:, 17:18]
        lbc, hgc = vcols[:, 18:26], vcols[:, 26:30]
        lam = take(4)
        stat = take(32)
        al = take(32)
        gg = take(64)
        beta = take(64)
        eG = take(64)
        G = take(64)
        nbeG = take(64)
        decs = take(64)
        gl = take(64)
        sa = take(64)
        sb_ = take(64)
        bias = take(len(BIASES))
        stat128 = take(128)
        aff = beta
        PS = [ctx.enter_context(nc.psum_tensor(f"PS{i}", [P, 512], F32)) for i in range(8)]

        dve_link, act_link, pool_link = sem("dve_link"), sem("act_link"), sem("pool_link")

        def V():
            return Chain(nc.vector, dve_link, counts)

        def A():
            return Chain(nc.scalar, act_link, counts)

        def G_():
            return Chain(nc.gpsimd, pool_link, counts)

        def bc(ap, n):
            return ap.unsqueeze(2).to_broadcast([P, ap.shape[1], n])

        def rsqrt(a, out, sums, scale, done, factor=0, eps=0):
            a(nc.scalar.activation(out, sums, ACT.Ln, scale=scale, bias=bias[:, eps:eps + 1]))
            a(nc.scalar.activation(out, out, ACT.Exp, scale=-0.5, bias=bias[:, factor:factor + 1] if factor else 0.0), done)

        slab_in = [sem(f"slab_in{i}") for i in range(8)]
        slab_n = [0] * 8
        SLB = SL + R[1:5]

        def load_slab(eng, slot, src, cols):
            k = src.shape[0] // P
            dst = SLB[slot][:, 0:k * cols].rearrange("p (k n) -> p k n", k=k)
            eng.dma_start(dst, src.rearrange("(k p) n -> p k n", p=P)).then_inc(slab_in[slot], 16)
            slab_n[slot] += 16
            return slab_in[slot], slab_n[slot]

        def slab(slot, k=KD, cols=512):
            return SLB[slot][:, 0:k * cols].rearrange("p (k n) -> p k n", k=k)

        tab_in, rows_in, x_in, bc_in = sem("tab_in"), sem("rows_in"), sem("x_in"), sem("bc_in")
        vec_t, h_ready, hT_done, hT_evac = sem("vec_t"), sem("h_ready"), sem("hT_done"), sem("hT_evac")
        bias_ready, rstd_ready = sem("bias_ready"), sem("rstd_ready")
        h_scaled, lam_dot = sem("h_scaled"), sem("lam_dot")
        rows = R[6]
        lamrow = R[6][:, 256:512].rearrange("p (a d) -> p a d", a=4)
        hn = R[1][:, :].rearrange("p (t d) -> p t d", t=NT)
        w_in = io["w_in"][0]
        with nc.Block() as block:
            @block.sync
            def _(sp):
                sp.dma_start(x3, io["x"][0].rearrange("(t p) d -> p t d", p=P)).then_inc(x_in, 16)
                sp.dma_start(tab[:, :], io["table"][:, 0:T_KEEP]).then_inc(tab_in, 16)
                sp.dma_start(R[5][:, 0:P + 2 * S], io["table"][:, T_ROT:T_BUCKET]).then_inc(tab_in, 16)
                for g in range(4):
                    load_slab(sp, g, w_in[:, g * 512:(g + 1) * 512], 512)

            @block.scalar
            def _(act):
                a = A()
                conv_rows = io["conv_w"][0].rearrange("t (c p) -> (t c) p", p=P)
                act.dma_start(rows[0:120, 0:P], conv_rows).then_inc(rows_in, 16)
                at_row = 0
                for name, n in (("norm1_w", 8), ("norm2_w", 8), ("subln_w", 1), ("gdn_norm_w", 1),
                                ("lb_logits_2", 8), ("hgrn_norm_g_2", 4)):
                    src = io[name]
                    src = src.rearrange("l (k p) -> (l k) p", p=P)
                    act.dma_start(rows[at_row:at_row + n, P:2 * P], src).then_inc(rows_in, 16)
                    at_row += n
                for i, name in enumerate(("lambda_q1", "lambda_k1", "lambda_q2", "lambda_k2")):
                    act.dma_start(lamrow[:, i, :], io[name].to_broadcast([P, 64])).then_inc(bc_in, 16)
                for i, name in enumerate(("a_log_fwd", "a_log_bwd", "dt_bias_fwd", "dt_bias_bwd")):
                    act.dma_start(al[:, 8 * i:8 * i + 8], io[name].to_broadcast([P, 8])).then_inc(bc_in, 16)
                act.wait_ge(x_in, 16)
                for t in range(NT):
                    a(nc.scalar.activation(hn[:, t, :], x3[:, t, :], ACT.Square, accum_out=stat[:, t:t + 1]),
                      h_ready)
                act.wait_ge(bias_ready, len(BIASES))
                rsqrt(a, stat[:, 8:12], stat[:, 0:4], 1.0 / D, rstd_ready)
                act.wait_ge(lam_dot, 2)
                a(nc.scalar.activation(lam[:, 2:4], lam[:, 0:2], ACT.Exp))
                act.wait_ge(vec_t, 1)
                a(nc.scalar.activation(convw, PS[6][:, 0:120], ACT.Copy))
                a(nc.scalar.activation(vcols, PS[7][:, 0:30], ACT.Copy))
                for k in range(KD):
                    act.wait_ge(hT_done, k + 1)
                    a(nc.scalar.activation(hT[:, k, :], PS[k % 4][:, :], ACT.Copy, scale=norm1c[:, k:k + 1]),
                      hT_evac)

            @block.gpsimd
            def _(pool):
                g = G_()
                for i, c in enumerate(BIASES):
                    g(nc.gpsimd.memset(bias[:, i:i + 1], c), bias_ready)

            @block.vector
            def _(dve):
                v = V()
                dve.wait_ge(rstd_ready, 1)
                for t in range(NT):
                    v(nc.vector.tensor_scalar(hn[:, t, :], x3[:, t, :], stat[:, 8 + t:9 + t], None, ALU.mult),
                      h_scaled)
                dve.wait_ge(bc_in, 16 * 8)
                for i in range(2):
                    v(nc.vector.tensor_tensor(lamrow[:, 2 * i, :], lamrow[:, 2 * i, :], lamrow[:, 2 * i + 1, :], ALU.mult))
                    v(nc.vector.reduce_sum(lam[:, i:i + 1], lamrow[:, 2 * i, :], AX), lam_dot)

            @block.tensor
            def _(pe):
                pe.wait_ge(tab_in, 32)
                pe.wait_ge(rows_in, 16 * 7)
                pe.transpose(PS[6][:, 0:120], rows[0:120, 0:P], ident[0:120, 0:120])
                pe.transpose(PS[7][:, 0:30], rows[0:30, P:2 * P], ident[0:30, 0:30]).then_inc(vec_t, 1)
                pe.wait_ge(h_scaled, NT)
                for k in range(KD):
                    if k >= 4:
                        pe.wait_ge(hT_evac, k - 3)
                    for t in range(NT):
                        m = pe.transpose(PS[k % 4][:, t * P:(t + 1) * P], hn[:, t, k * P:(k + 1) * P], ident)
                    m.then_inc(hT_done, 1)

        qz = [R[1][:, :].rearrange("p (h s) -> p h s", h=HEADS), R[2][:, :].rearrange("p (h s) -> p h s", h=HEADS)]
        kT = R[3][:, :].rearrange("p (h s) -> p h s", h=HEADS)
        va = R[4][:, :].rearrange("p (t d) -> p t d", t=NT)
        rot_m, cosT, sinT = R[5][:, 0:P], R[5][:, P:P + S], R[5][:, P + S:P + 2 * S]
        raw = [R[5][:, 1152 + i * S:1152 + (i + 1) * S] for i in range(2)]
        t1, t2 = R[5][:, 2176:2688], R[5][:, 2688:3200]
        proj_done, raw_ready, rot_done, rope_done, slab_used, va_evac = (
            sem("proj_done"), sem("raw_ready"), sem("rot_done"), sem("rope_done"), sem("slab_used"), sem("va_evac"))
        pad_zero = sem("pad_zero")
        NQK = 2 * HEADS
        with nc.Block() as block:
            @block.sync
            def _(sp):
                for g in range(4, 6):
                    sp.wait_ge(slab_used, g - 3)
                    load_slab(sp, g % 4, w_in[:, g * 512:(g + 1) * 512], 512)

            @block.tensor
            def _(pe):
                def rotate(u):
                    pe.wait_ge(raw_ready, u + 1)
                    if u >= 2:
                        pe.wait_ge(rope_done, u - 1)
                    pe.matmul(PS[4 + u % 2][:, :], rot_m, raw[u % 2], start=True, stop=True).then_inc(rot_done, 1)

                for u in range(NQK):
                    g, j = u // 4, u % 4
                    pe.wait_ge(slab_in[g % 4], 16 * (g // 4 + 1))
                    if u >= 4:
                        pe.wait_ge(raw_ready, u - 3)
                    for k in range(KD):
                        m = pe.matmul(PS[u % 4][:, :], slab(g % 4)[:, k, j * P:(j + 1) * P], hT[:, k, :],
                                      start=(k == 0), stop=(k == KD - 1))
                    m.then_inc(proj_done, 1)
                    if u >= 1:
                        rotate(u - 1)
                    if j == 3:
                        pe.wait_ge(rot_done, u)
                        pe.sem_inc(slab_used, 1)
                rotate(NQK - 1)
                for n in range(2):
                    pe.wait_ge(slab_in[n], 32)
                    for t in range(NT):
                        u = NT * n + t
                        b = u % 4
                        if u >= 4:
                            pe.wait_ge(va_evac, u - 3)
                        else:
                            pe.wait_ge(raw_ready, NQK)
                        for k in range(KD):
                            m = pe.matmul(PS[b][:, :], hT[:, k, t * P:(t + 1) * P], slab(n)[:, k, :],
                                          start=(k == 0), stop=(k == KD - 1))
                        m.then_inc(proj_done, 1)

            @block.scalar
            def _(act):
                a = A()
                for u in range(NQK):
                    act.wait_ge(proj_done, u + 1)
                    if u >= 2:
                        act.wait_ge(rope_done, u - 1)
                    a(nc.scalar.activation(raw[u % 2], PS[u % 4][:, :], ACT.Copy), raw_ready)
                for u in range(8):
                    n, t = u // NT, u % NT
                    act.wait_ge(proj_done, NQK + u + 1)
                    a(nc.scalar.activation(va[:, t, n * 512:(n + 1) * 512], PS[u % 4][:, :], ACT.Copy), va_evac)

            @block.gpsimd
            def _(pool):
                g = G_()
                g(nc.gpsimd.memset(R[1][64:128, :], 0.0), pad_zero)
                g(nc.gpsimd.memset(R[2][0:64, :], 0.0), pad_zero)

            @block.vector
            def _(dve):
                v = V()
                v(nc.vector.tensor_tensor(lam[:, 0:1], lam[:, 2:3], lam[:, 3:4], ALU.subtract))
                v(nc.vector.tensor_scalar(lam[:, 0:1], lam[:, 0:1], LAMBDA_INIT, None, ALU.add))
                for u in range(NQK):
                    dve.wait_ge(raw_ready, u + 1)
                    v(nc.vector.tensor_tensor(t1, raw[u % 2], cosT, ALU.mult))
                    dve.wait_ge(rot_done, u + 1)
                    v(nc.vector.tensor_tensor(t2, PS[4 + u % 2][:, :], sinT, ALU.mult))
                    if u < HEADS:
                        v(nc.vector.tensor_tensor(qz[0][0:64, u, :], t1[0:64, :], t2[0:64, :], ALU.add))
                        v(nc.vector.tensor_tensor(qz[1][64:128, u, :], t1[64:128, :], t2[64:128, :], ALU.add),
                          rope_done)
                    else:
                        v(nc.vector.tensor_tensor(kT[:, u - HEADS, :], t1, t2, ALU.add), rope_done)
        if upto == 1:
            return dump(locals())

        oaT = R[5][:, :].rearrange("p (h s) -> p h s", h=HEADS)
        r6 = R[6]
        p0 = [r6[:, 0:512], r6[:, 512:1024]]
        p1 = [r6[:, 1024:1536], r6[:, 1536:2048]]
        pd = [r6[:, 2048:2560], r6[:, 2560:3072]]
        pT = [r6[:, 3072:3584].rearrange("p (c q) -> p c q", c=NT), r6[:, 3584:4096].rearrange("p (c q) -> p c q", c=NT)]
        score_done, max_ready, exp_done, pd_ready, pT_done, pT_ready, pv_done, oT_evac = (
            sem("score_done"), sem("max_ready"), sem("exp_done"), sem("pd_ready"), sem("pT_done"),
            sem("pT_ready"), sem("pv_done"), sem("oT_evac"))
        rstd2 = sem("rstd2")
        sq_ready, ss_done, norm_done = sem("sq_ready"), sem("ss_done"), sem("norm_done")
        NU = HEADS * NT
        with nc.Block() as block:
            @block.tensor
            def _(pe):
                def scores(n):
                    h, t = n // NT, n % NT
                    if n >= 2:
                        pe.wait_ge(exp_done, n - 1)
                    for m_ in range(2):
                        m = pe.matmul(PS[2 * (n % 2) + m_][:, :], qz[m_][:, h, t * P:(t + 1) * P], kT[:, h, :],
                                      start=True, stop=True)
                    m.then_inc(score_done, 1)

                def turn(n):
                    pe.wait_ge(pd_ready, n + 1)
                    if n >= 2:
                        pe.wait_ge(pT_ready, n - 1)
                    for c in range(NT):
                        m = pe.transpose(PS[4 + n % 2][:, c * P:(c + 1) * P], pd[n % 2][:, c * P:(c + 1) * P], ident)
                    m.then_inc(pT_done, 1)

                def pv(n):
                    h, t = n // NT, n % NT
                    pe.wait_ge(pT_ready, n + 1)
                    if t == 0 and h >= 2:
                        pe.wait_ge(oT_evac, h - 1)
                    for c in range(NT):
                        m = pe.matmul(PS[6 + h % 2][:, t * P:(t + 1) * P], va[:, c, h * P:(h + 1) * P], pT[n % 2][:, c, :],
                                      start=(c == 0), stop=(c == NT - 1))
                    m.then_inc(pv_done, 1)

                for n in range(NU + 2):
                    if n < NU:
                        scores(n)
                    if 1 <= n <= NU:
                        turn(n - 1)
                    if n >= 2:
                        pv(n - 2)
                for h in range(HEADS):
                    pe.wait_ge(sq_ready, h + 1)
                    if h >= 2:
                        pe.wait_ge(rstd2, h - 1)
                    pe.matmul(PS[h % 2][:, :], ones, p0[h % 2], start=True, stop=True).then_inc(ss_done, 1)

            @block.scalar
            def _(act):
                a = A()

                def evac(n):
                    act.wait_ge(pT_done, n + 1)
                    if n >= 2:
                        act.wait_ge(pv_done, n - 1)
                    a(nc.scalar.activation(pT[n % 2].rearrange("p c q -> p (c q)"), PS[4 + n % 2][:, :], ACT.Copy), pT_ready)

                for n in range(NU):
                    act.wait_ge(max_ready, n + 1)
                    s = stat[:, 8 * (n % 2):8 * (n % 2) + 8]
                    for m_, p in ((0, p0), (1, p1)):
                        ins = nc.scalar.activation(p[n % 2], PS[2 * (n % 2) + m_][:, :], ACT.Exp, scale=0.125,
                                                   bias=s[:, 2 + m_:3 + m_], accum_out=s[:, 4 + m_:5 + m_])
                        a(ins, exp_done if m_ else None)
                    if n >= 1:
                        evac(n - 1)
                evac(NU - 1)

                def norm(h):
                    act.wait_ge(ss_done, h + 1)
                    if h >= 2:
                        act.wait_ge(norm_done, h - 1)
                    rsqrt(a, p1[h % 2], PS[h % 2][:, :], 1.0 / P, rstd2, LN_SUB)

                for h in range(HEADS):
                    act.wait_ge(oT_evac, h + 1)
                    if h >= 2:
                        act.wait_ge(ss_done, h - 1)
                    a(nc.scalar.activation(p0[h % 2], oaT[:, h, :], ACT.Square), sq_ready)
                    if h >= 1:
                        norm(h - 1)
                norm(HEADS - 1)

            @block.vector
            def _(dve):
                v = V()

                def maxes(n):
                    s = stat[:, 8 * (n % 2):8 * (n % 2) + 8]
                    dve.wait_ge(score_done, n + 1)
                    for m_ in range(2):
                        v(nc.vector.reduce_max(s[:, m_:m_ + 1], PS[2 * (n % 2) + m_][:, :], AX))
                    v(nc.vector.tensor_scalar(s[:, 2:4], s[:, 0:2], -0.125, None, ALU.mult), max_ready)

                def out(h):
                    dve.wait_ge(pv_done, NT * h + NT)
                    v(nc.vector.tensor_copy(oaT[:, h, :], PS[6 + h % 2][:, :]), oT_evac)

                maxes(0)
                for n in range(NU):
                    if n + 1 < NU:
                        maxes(n + 1)
                    s = stat[:, 8 * (n % 2):8 * (n % 2) + 8]
                    dve.wait_ge(exp_done, n + 1)
                    v(nc.vector.reciprocal(s[:, 4:6], s[:, 4:6]))
                    v(nc.vector.tensor_tensor(s[:, 6:7], s[:, 5:6], lam[:, 0:1], ALU.mult))
                    v(nc.vector.tensor_scalar(p1[n % 2], p1[n % 2], s[:, 6:7], None, ALU.mult))
                    if n >= 2:
                        dve.wait_ge(pT_done, n - 1)
                    v(nc.vector.scalar_tensor_tensor(pd[n % 2], p0[n % 2], s[:, 4:5], p1[n % 2], ALU.mult, ALU.subtract),
                      pd_ready)
                    if n >= 7 and (n - 7) % NT == 0:
                        out((n - 7) // NT)
                out(HEADS - 1)
                for h in range(HEADS):
                    dve.wait_ge(rstd2, h + 1)
                    o = oaT[:, h, :]
                    v(nc.vector.scalar_tensor_tensor(o, o, sublnc, p1[h % 2], ALU.mult, ALU.mult), norm_done)
        if upto == 2:
            return dump(locals())

        gq = R[1][:, :].rearrange("p (h s) -> p h s", h=HEADS)
        gk = R[2][:, :].rearrange("p (h s) -> p h s", h=HEADS)
        gv = R[3][:, :].rearrange("p (t h d) -> p t h d", t=NT, h=HEADS)
        gkt = R[4][:, :].rearrange("p (t h d) -> p t h d", t=NT, h=HEADS)
        zs = R[6][:, :].rearrange("p (h s) -> p h s", h=HEADS)
        wk = SL[3]
        PADW = 520
        padded = [wk[:, i * PADW:(i + 1) * PADW] for i in range(2)]
        conv = [wk[:, 1040 + i * S:1040 + (i + 1) * S] for i in range(3)]
        sq = [wk[:, 2576:3088], wk[:, 3088:3600]]
        wab = wab_[:, :].rearrange("p (k n) -> p k n", k=KD)
        pad_done, p3_done, raw3, conv_done, silu_done, sq3, ss3, rstd3, qk_norm, tr3, tr3_evac, slab3, wab_in, z_done, ab_done, slab3_free = [
            sem(n) for n in ("pad_done", "p3_done", "raw3", "conv_done", "silu_done", "sq3", "ss3", "rstd3", "qk_norm",
                             "tr3", "tr3_evac", "slab3", "wab_in", "z_done", "ab_done", "slab3_free")]
        ab_evac = sem("ab_evac")
        NC3 = 3 * HEADS
        with nc.Block() as block:
            start3 = list(slab_n)

            @block.sync
            def _(sp):
                for i in range(8):
                    g = 6 + i
                    if i >= 3:
                        sp.wait_ge(slab3_free, i - 2)
                    load_slab(sp, i % 3, w_in[:, g * 512:(g + 1) * 512], 512)
                    if i == 0:
                        sp.dma_start(wab, w_in[:, AB:AB + 32].rearrange("(k p) n -> p k n", p=P)).then_inc(wab_in, 16)

            @block.tensor
            def _(pe):
                tr = [0]

                def turn(u):
                    if u < 2 * HEADS:
                        pe.wait_ge(qk_norm, u + 1)
                        src = gk[:, u - HEADS, :]
                    else:
                        pe.wait_ge(silu_done, u + 1)
                        src = conv[u % 3]
                    if tr[0] >= 2:
                        pe.wait_ge(tr3_evac, tr[0] - 1)
                    for t in range(NT):
                        m = pe.transpose(PS[6 + tr[0] % 2][:, t * P:(t + 1) * P], src[:, t * P:(t + 1) * P], ident)
                    m.then_inc(tr3, 1)
                    tr[0] += 1

                for u in range(NC3 + 3):
                    if u < NC3:
                        i, j = u // 4, u % 4
                        pe.wait_ge(slab_in[i % 3], start3[i % 3] + 16 * (i // 3 + 1))
                        if u >= 4:
                            pe.wait_ge(raw3, u - 3)
                        for k in range(KD):
                            m = pe.matmul(PS[u % 4][:, :], slab(i % 3)[:, k, j * P:(j + 1) * P], hT[:, k, :],
                                          start=(k == 0), stop=(k == KD - 1))
                        m.then_inc(p3_done, 1)
                    if 1 <= u <= 2 * HEADS:
                        pe.wait_ge(sq3, u)
                        if u >= 3:
                            pe.wait_ge(rstd3, u - 2)
                        pe.matmul(PS[4 + (u - 1) % 2][:, :], ones, sq[(u - 1) % 2], start=True, stop=True).then_inc(ss3, 1)
                    if u < NC3 and u % 4 == 3:
                        pe.wait_ge(p3_done, u + 1)
                        pe.sem_inc(slab3_free, 1)
                    if HEADS + 2 <= u <= NC3 + 1:
                        turn(u - 2)
                for u in range(HEADS):
                    i, j = 6 + u // 4, u % 4
                    pe.wait_ge(slab_in[i % 3], start3[i % 3] + 16 * (i // 3 + 1))
                    if u >= 4:
                        pe.wait_ge(z_done, u - 3)
                    else:
                        pe.wait_ge(raw3, NC3)
                    for k in range(KD):
                        m = pe.matmul(PS[u % 4][:, :], slab(i % 3)[:, k, j * P:(j + 1) * P], hT[:, k, :],
                                      start=(k == 0), stop=(k == KD - 1))
                    m.then_inc(p3_done, 1)
                pe.wait_ge(wab_in, 16)
                pe.wait_ge(rstd3, 2 * HEADS)
                for t in range(NT):
                    for k in range(KD):
                        m = pe.matmul(PS[4][:, t * 32:(t + 1) * 32], hT[:, k, t * P:(t + 1) * P], wab[:, k, :],
                                      start=(k == 0), stop=(k == KD - 1))
                m.then_inc(ab_done, 1)

            @block.gpsimd
            def _(pool):
                g = G_()
                for i in range(2):
                    g(nc.gpsimd.memset(padded[i], 0.0), pad_done)

            @block.scalar
            def _(act):
                a = A()
                act.wait_ge(pad_done, 2)

                def norm(u):
                    act.wait_ge(ss3, u + 1)
                    rsqrt(a, sq[u % 2], PS[4 + u % 2][:, :], 1.0, rstd3, LN_DK if u < HEADS else 0)

                def evac_turned(n):
                    act.wait_ge(tr3, n + 1)
                    dst = (gkt if n < HEADS else gv)[:, :, n % HEADS, :]
                    a(nc.scalar.activation(dst, PS[6 + n % 2][:, :].rearrange("p (t d) -> p t d", t=NT), ACT.Copy), tr3_evac)

                n = 0
                for u in range(NC3 + 3):
                    if u < NC3:
                        act.wait_ge(p3_done, u + 1)
                        if u >= 2:
                            act.wait_ge(conv_done, u - 1)
                        a(nc.scalar.activation(padded[u % 2][:, 2:2 + S], PS[u % 4][:, :], ACT.Copy), raw3)
                    if 1 <= u <= 2 * HEADS:
                        norm(u - 1)
                    if HEADS + 3 <= u <= NC3 + 2:
                        evac_turned(n)
                        n += 1
                    if u < NC3:
                        act.wait_ge(conv_done, u + 1)
                        a(nc.scalar.activation(conv[u % 3], conv[u % 3], ACT.Silu), silu_done)
                        if u < 2 * HEADS:
                            if u >= 2:
                                act.wait_ge(qk_norm, u - 1)
                            a(nc.scalar.activation(sq[u % 2], conv[u % 3], ACT.Square), sq3)
                for u in range(HEADS):
                    act.wait_ge(p3_done, NC3 + u + 1)
                    a(nc.scalar.activation(zs[:, u, :], PS[u % 4][:, :], ACT.Silu), z_done)
                act.wait_ge(ab_done, 1)
                a(nc.scalar.activation(stat128, PS[4][:, 0:128], ACT.Copy), ab_evac)

            @block.vector
            def _(dve):
                v = V()
                for u in range(NC3 + 1):
                    if u < NC3:
                        dve.wait_ge(raw3, u + 1)
                        if u >= 3:
                            if u - 3 < 2 * HEADS:
                                dve.wait_ge(qk_norm, u - 2)
                            else:
                                dve.wait_ge(tr3, u - 3 - HEADS + 1)
                        c = conv[u % 3]
                        for j in range(CONV_K):
                            src = padded[u % 2][:, j:j + S]
                            w = convw[:, j * NC3 + u:j * NC3 + u + 1]
                            if j == 0:
                                v(nc.vector.tensor_scalar(c, src, w, None, ALU.mult))
                            else:
                                v(nc.vector.scalar_tensor_tensor(c, src, w, c, ALU.mult, ALU.add),
                                  conv_done if j == CONV_K - 1 else None)
                    if 1 <= u <= 2 * HEADS:
                        n = u - 1
                        dve.wait_ge(rstd3, n + 1)
                        dst = gq[:, n, :] if n < HEADS else gk[:, n - HEADS, :]
                        v(nc.vector.tensor_tensor(dst, conv[n % 3], sq[n % 2], ALU.mult), qk_norm)
        if upto == 3:
            return dump(locals())


        def wbuf(d, i):
            n = d * 10 + i
            return SL[n // 8][:, (n % 8) * 512:(n % 8 + 1) * 512].rearrange("p (h n) -> p h n", h=4)

        bufs = [dict(zip(("AT", "A", "X", "XT", "BT", "PM", "QK", "T1", "T2", "QD"), (wbuf(d, i) for i in range(10))))
                for d in range(2)]
        St = SL[2][:, 2048:4096].rearrange("p (a d) -> p a d", a=2 * HEADS)
        OG = SL[3][:, :]
        ogT = OG.rearrange("p (h s) -> p h s", h=HEADS)
        ab3 = stat128.rearrange("p (t n) -> p t n", t=NT)
        v16 = lambda ap: ap.rearrange("p (t n) -> p t n", t=NT)
        names = ("u_ready", "sp_ready", "g_ready", "cum_done", "G_ready", "pre_ready", "st_zero", "gram_done", "diff_ready", "dec_ready",
                 "decm_ready", "A_ready", "at_done", "AT_ready", "X_ready", "XT_ready", "XT0_ready", "BT_ready", "P_done", "P_ready",
                 "XX_done", "ks_done", "bv_ready", "rr_ready", "vn_done", "vn_ready", "vs_ready", "o_done", "s_done",
                 "o_ready", "S_ready", "sq4", "ss4", "rstd4", "og_ready")
        E4 = {n: sem("d_" + n) for n in names}
        PAIRS = [(s, hg) for s in range(NT) for hg in range(2)]

        def all4(ap):
            return ap.unsqueeze(1).to_broadcast([P, 4, P])

        def cols4(ap, c, d, hg):
            n = c * 16 + d * 8 + hg * 4
            return bc(ap[:, n:n + 4], P)

        def chunk(s, d):
            return s if d == 0 else NT - 1 - s

        sq4 = [SL[0][:, 0:512], SL[0][:, 512:1024]]
        rs4 = [SL[0][:, 1024:1536], SL[0][:, 1536:2048]]
        with nc.Block() as block:
            @block.tensor
            def _(pe):
                pe.wait_ge(E4["g_ready"], 1)
                for d in range(2):
                    pe.matmul(v16(PS[0][:, 0:64])[:, :, 8 * d:8 * d + 8], (tri_le, tri_ge)[d],
                              v16(gg)[:, :, 8 * d:8 * d + 8], start=True, stop=True)
                pe.matmul(PS[1][:, 0:64], ones, gg, start=True, stop=True).then_inc(E4["cum_done"], 1)
                pe.wait_ge(E4["pre_ready"], 1)
                pe.wait_ge(E4["st_zero"], 1)
                for n, (s, hg) in enumerate(PAIRS):
                    for d in range(2):
                        q, c, B = 2 * n + d, chunk(s, d), bufs[d]
                        cs = slice(c * P, (c + 1) * P)
                        if n:
                            pe.wait_ge(E4["S_ready"], q - 1)
                        for i in range(4):
                            h = hg * 4 + i
                            col = c * 16 + d * 8 + h
                            pe.matmul(PS[4 * d][:, i * P:(i + 1) * P], gg[:, col:col + 1].to_broadcast([P, P]),
                                      (tri_le, tri_ge)[d], start=True, stop=True)
                        for i in range(4):
                            h = hg * 4 + i
                            pe.matmul(PS[4 * d + 1][:, i * P:(i + 1) * P], gk[:, h, cs], gk[:, h, cs], start=True, stop=True)
                        for i in range(4):
                            h = hg * 4 + i
                            m = pe.matmul(PS[4 * d + 2][:, i * P:(i + 1) * P], gk[:, h, cs], gq[:, h, cs], start=True, stop=True)
                        m.then_inc(E4["gram_done"], 1)
                    for d in range(2):
                        q, B = 2 * n + d, bufs[d]
                        pe.wait_ge(E4["A_ready"], q + 1)
                        for i in range(4):
                            m = pe.transpose(PS[4 * d + 3][:, i * P:(i + 1) * P], B["A"][:, i, :], ident)
                        m.then_inc(E4["at_done"], 1)
                    for l in range(1, NL):
                        lq = (n * (NL - 1) + l - 1) * 2
                        for d in range(2):
                            B = bufs[d]
                            pe.wait_ge(E4["BT_ready"], lq + d + 1)
                            pe.wait_ge(E4["X_ready"], n * 2 * (NL - 1) + 2 * (l - 1) + d + 1)
                            for i in range(4):
                                m = pe.matmul(PS[4 * d][:, i * P:(i + 1) * P], B["BT"][:, i, :], B["X"][:, i, :], start=True, stop=True)
                            m.then_inc(E4["P_done"], 1)
                        for d in range(2):
                            B = bufs[d]
                            pe.wait_ge(E4["P_ready"], lq + d + 1)
                            if l == 1:
                                pe.wait_ge(E4["XT0_ready"], 2 * n + d + 1)
                            else:
                                pe.wait_ge(E4["XT_ready"], n * 2 * (NL - 1) + 2 * (l - 2) + d + 1)
                            for i in range(4):
                                if l < NL - 1:
                                    pe.matmul(PS[4 * d + 1][:, i * P:(i + 1) * P], B["XT"][:, i, :], B["PM"][:, i, :], start=True, stop=True)
                            for i in range(4):
                                m = pe.matmul(PS[4 * d + 2][:, i * P:(i + 1) * P], B["PM"][:, i, :], B["XT"][:, i, :], start=True, stop=True)
                            m.then_inc(E4["XX_done"], 1)
                    for d in range(2):
                        q, c = 2 * n + d, chunk(s, d)
                        for i in range(4):
                            h = hg * 4 + i
                            m = pe.matmul(PS[4 * d + 3][:, i * P:(i + 1) * P], gk[:, h, c * P:(c + 1) * P], St[:, d * 8 + h, :], start=True, stop=True)
                        m.then_inc(E4["ks_done"], 1)
                    for d in range(2):
                        q, B = 2 * n + d, bufs[d]
                        pe.wait_ge(E4["rr_ready"], q + 1)
                        for i in range(4):
                            m = pe.matmul(PS[4 * d][:, i * P:(i + 1) * P], B["XT"][:, i, :], B["T1"][:, i, :], start=True, stop=True)
                        m.then_inc(E4["vn_done"], 1)
                    for d in range(2):
                        q, c, B = 2 * n + d, chunk(s, d), bufs[d]
                        pe.wait_ge(E4["vn_ready"], q + 1)
                        for i in range(4):
                            h = hg * 4 + i
                            pe.matmul(PS[4 * d + 1][:, i * P:(i + 1) * P], B["T2"][:, i, :], B["QK"][:, i, :], start=True, stop=False)
                            m = pe.matmul(PS[4 * d + 1][:, i * P:(i + 1) * P], St[:, d * 8 + h, :], B["QD"][:, i, :], start=False, stop=True)
                        m.then_inc(E4["o_done"], 1)
                        pe.wait_ge(E4["vs_ready"], q + 1)
                        for i in range(4):
                            h = hg * 4 + i
                            m = pe.matmul(PS[4 * d + 2][:, i * P:(i + 1) * P], gkt[:, c, h, :], B["A"][:, i, :], start=True, stop=True)
                        m.then_inc(E4["s_done"], 1)
                for h in range(HEADS):
                    pe.wait_ge(E4["sq4"], h + 1)
                    if h == 0:
                        pe.wait_ge(E4["S_ready"], 2 * len(PAIRS))
                    if h >= 2:
                        pe.wait_ge(E4["rstd4"], h - 1)
                    pe.matmul(PS[h % 2][:, :], ones, sq4[h % 2], start=True, stop=True).then_inc(E4["ss4"], 1)

            @block.scalar
            def _(act):
                a = A()
                act.wait_ge(E4["u_ready"], 1)
                a(nc.scalar.activation(sb_, sb_, ACT.Exp, scale=-1.0))
                a(nc.scalar.activation(sb_, sb_, ACT.Ln, bias=1.0))
                a(nc.scalar.activation(al[:, 0:16], al[:, 0:16], ACT.Exp))
                a(nc.scalar.activation(v16(beta), ab3[:, :, 16:32], ACT.Exp, scale=-1.0), E4["sp_ready"])
                act.wait_ge(E4["G_ready"], 1)
                a(nc.scalar.activation(eG, G, ACT.Exp))
                a(nc.scalar.activation(gl, PS[1][:, 0:64], ACT.Exp))
                a(nc.scalar.activation(decs, decs, ACT.Exp), E4["sp_ready"])
                for n, (s, hg) in enumerate(PAIRS):
                    for d in range(2):
                        q, B = 2 * n + d, bufs[d]
                        act.wait_ge(E4["diff_ready"], q + 1)
                        a(nc.scalar.activation(B["T1"], B["T1"], ACT.Exp, scale=-1.0))
                        a(nc.scalar.activation(B["T2"], B["T2"], ACT.Exp))
                        a(nc.scalar.activation(B["QD"].rearrange("p h n -> p (h n)"), PS[4 * d][:, :], ACT.Exp), E4["dec_ready"])
                    for d in range(2):
                        act.wait_ge(E4["at_done"], 2 * n + d + 1)
                        a(nc.scalar.activation(bufs[d]["AT"].rearrange("p h n -> p (h n)"), PS[4 * d + 3][:, :], ACT.Copy), E4["AT_ready"])
                    for l in range(1, NL):
                        for d in range(2):
                            act.wait_ge(E4["P_done"], (n * (NL - 1) + l - 1) * 2 + d + 1)
                            a(nc.scalar.activation(bufs[d]["PM"].rearrange("p h n -> p (h n)"), PS[4 * d][:, :], ACT.Copy), E4["P_ready"])
                    for d in range(2):
                        act.wait_ge(E4["vn_done"], 2 * n + d + 1)
                        a(nc.scalar.activation(bufs[d]["T2"].rearrange("p h n -> p (h n)"), PS[4 * d][:, :], ACT.Copy), E4["vn_ready"])

                def norm(h):
                    act.wait_ge(E4["ss4"], h + 1)
                    if h >= 2:
                        act.wait_ge(E4["og_ready"], h - 1)
                    rsqrt(a, rs4[h % 2], PS[h % 2][:, :], 1.0 / P, E4["rstd4"])

                act.wait_ge(E4["S_ready"], 2 * len(PAIRS))
                for h in range(HEADS):
                    if h >= 2:
                        act.wait_ge(E4["ss4"], h - 1)
                    a(nc.scalar.activation(sq4[h % 2], ogT[:, h, :], ACT.Square), E4["sq4"])
                    if h >= 1:
                        norm(h - 1)
                norm(HEADS - 1)

            @block.gpsimd
            def _(pool):
                g = G_()
                tt = nc.gpsimd.tensor_tensor
                g(nc.gpsimd.memset(St, 0.0), E4["st_zero"])
                pool.wait_ge(E4["pre_ready"], 1)
                for n, (s, hg) in enumerate(PAIRS):
                    for d in range(2):
                        q, c, B = 2 * n + d, chunk(s, d), bufs[d]
                        pool.wait_ge(E4["dec_ready"], q + 1)
                        g(tt(B["T1"], B["T1"], all4((tri_ge, tri_le)[d]), ALU.mult))
                        g(tt(B["T1"], B["T1"], cols4(beta, c, d, hg), ALU.mult))
                        g(tt(B["T2"], B["T2"], all4((tri_le, tri_ge)[d]), ALU.mult), E4["decm_ready"])
                        g(tt(B["QD"], B["QD"], gq[:, hg * 4:hg * 4 + 4, c * P:(c + 1) * P], ALU.mult))
                    for l in range(1, NL):
                        for d in range(2):
                            B = bufs[d]
                            if l == 1:
                                pool.wait_ge(E4["AT_ready"], 2 * n + d + 1)
                                g(tt(B["XT"], B["AT"], all4((up, low)[d][0]), ALU.mult))
                                g(tt(B["XT"], all4(ident), B["XT"], ALU.subtract), E4["XT0_ready"])
                            else:
                                pool.wait_ge(E4["P_done"], (n * (NL - 1) + l - 2) * 2 + d + 1)
                            g(tt(B["BT"], B["AT"], all4((up, low)[d][l]), ALU.mult), E4["BT_ready"])
                    for d in range(2):
                        q, c, B = 2 * n + d, chunk(s, d), bufs[d]
                        pool.wait_ge(E4["P_done"], (n * (NL - 1) + NL - 2) * 2 + d + 1)
                        g(tt(B["BT"], gv[:, c, hg * 4:hg * 4 + 4, :], cols4(beta, c, d, hg), ALU.mult), E4["bv_ready"])
                    for d in range(2):
                        q, c, B = 2 * n + d, chunk(s, d), bufs[d]
                        pool.wait_ge(E4["vn_ready"], q + 1)
                        g(tt(B["A"], B["T2"], cols4(decs, c, d, hg), ALU.mult), E4["vs_ready"])

            @block.vector
            def _(dve):
                v = V()
                tt = nc.vector.tensor_tensor
                f4 = lambda ap: ap.rearrange("p (h n) -> p h n", h=4)
                dtb = al[:, 16:32].unsqueeze(1).to_broadcast([P, NT, 16])
                v(tt(v16(sa), ab3[:, :, 0:16], dtb, ALU.add))
                v(nc.vector.tensor_scalar(sb_, sa, -1.0, None, ALU.mult))
                v(tt(sb_, sa, sb_, ALU.max), E4["u_ready"])
                dve.wait_ge(E4["sp_ready"], 1)
                v(nc.vector.scalar_tensor_tensor(sa, sa, 0.0, sb_, ALU.max, ALU.add))
                v(nc.vector.tensor_scalar(beta, beta, 1.0, None, ALU.add))
                v(nc.vector.reciprocal(beta, beta))
                v(nc.vector.scalar_tensor_tensor(v16(gg), v16(sa), -1.0, al[:, 0:16].unsqueeze(1).to_broadcast([P, NT, 16]),
                                                 ALU.mult, ALU.mult), E4["g_ready"])
                dve.wait_ge(E4["cum_done"], 1)
                v(nc.vector.tensor_copy(G, PS[0][:, 0:64]))
                v(tt(decs, PS[1][:, 0:64], G, ALU.subtract), E4["G_ready"])
                dve.wait_ge(E4["sp_ready"], 2)
                v(nc.vector.scalar_tensor_tensor(nbeG, eG, -1.0, beta, ALU.mult, ALU.mult), E4["pre_ready"])
                for n, (s, hg) in enumerate(PAIRS):
                    for d in range(2):
                        q, c, B = 2 * n + d, chunk(s, d), bufs[d]
                        dve.wait_ge(E4["gram_done"], q + 1)
                        v(tt(B["T1"], f4(PS[4 * d][:, :]), cols4(G, c, d, hg), ALU.subtract))
                        v(nc.vector.tensor_scalar(B["T2"], B["T1"], 0.0, None, ALU.min))
                        v(nc.vector.tensor_scalar(B["T1"], B["T1"], 0.0, None, ALU.max), E4["diff_ready"])
                    for d in range(2):
                        q, B = 2 * n + d, bufs[d]
                        dve.wait_ge(E4["decm_ready"], q + 1)
                        v(tt(B["A"], f4(PS[4 * d + 1][:, :]), B["T1"], ALU.mult), E4["A_ready"])
                        v(tt(B["QK"], f4(PS[4 * d + 2][:, :]), B["T2"], ALU.mult))
                        v(tt(B["X"], B["A"], all4((low, up)[d][0]), ALU.mult))
                        v(tt(B["X"], all4(ident), B["X"], ALU.subtract), E4["X_ready"])
                    for l in range(1, NL):
                        for d in range(2):
                            B = bufs[d]
                            dve.wait_ge(E4["XX_done"], (n * (NL - 1) + l - 1) * 2 + d + 1)
                            if l < NL - 1:
                                v(tt(B["X"], B["X"], f4(PS[4 * d + 1][:, :]), ALU.subtract), E4["X_ready"])
                            v(tt(B["XT"], B["XT"], f4(PS[4 * d + 2][:, :]), ALU.subtract), E4["XT_ready"])
                    for d in range(2):
                        q, c, B = 2 * n + d, chunk(s, d), bufs[d]
                        dve.wait_ge(E4["ks_done"], q + 1)
                        v(tt(B["T1"], f4(PS[4 * d + 3][:, :]), cols4(nbeG, c, d, hg), ALU.mult))
                        dve.wait_ge(E4["bv_ready"], q + 1)
                        v(tt(B["T1"], B["T1"], B["BT"], ALU.add), E4["rr_ready"])
                    for d in range(2):
                        q, c, B = 2 * n + d, chunk(s, d), bufs[d]
                        o = ogT[:, hg * 4:hg * 4 + 4, c * P:(c + 1) * P]
                        dve.wait_ge(E4["o_done"], q + 1)
                        if s < 2:
                            v(nc.vector.tensor_copy(o, f4(PS[4 * d + 1][:, :])))
                        else:
                            v(tt(o, o, f4(PS[4 * d + 1][:, :]), ALU.add))
                        dve.wait_ge(E4["s_done"], q + 1)
                        for i in range(4):
                            h = d * 8 + hg * 4 + i
                            v(nc.vector.scalar_tensor_tensor(St[:, h, :], St[:, h, :], gl[:, c * 16 + h:c * 16 + h + 1],
                                                             PS[4 * d + 2][:, i * P:(i + 1) * P], ALU.mult, ALU.add),
                              E4["S_ready"] if i == 3 else None)
                for h in range(HEADS):
                    dve.wait_ge(E4["rstd4"], h + 1)
                    v(nc.vector.scalar_tensor_tensor(ogT[:, h, :], ogT[:, h, :], gdnc, rs4[h % 2], ALU.mult, ALU.mult), E4["og_ready"])
                    v(tt(ogT[:, h, :], ogT[:, h, :], zs[:, h, :], ALU.mult))
        if upto == 4:
            return dump(locals())

        spent.extend([proj_done, raw_ready, rot_done, rope_done, slab_used, va_evac, pad_zero, score_done, max_ready,
                      exp_done, pd_ready, pT_done, pT_ready, pv_done, oT_evac, rstd2, sq_ready, ss_done, norm_done,
                      pad_done, p3_done, raw3, conv_done, silu_done, sq3, ss3, rstd3, qk_norm, tr3, tr3_evac, slab3,
                      wab_in, z_done, ab_done, slab3_free, ab_evac, *E4.values()])
        clear_spent()
        mT = R[6][:, :].rearrange("p (k s) -> p k s", k=KD)
        p5, gate5, merge5, m5, out5 = [sem(n) for n in ("p5", "gate5", "merge5", "m5", "out5")]
        wpa, wpg, wo = io["w_proj_attn"][0], io["w_proj_gdn"][0], io["w_out"][0]
        tm = [R[2][:, i * 512:(i + 1) * 512] for i in range(8)]
        w5 = []
        with nc.Block() as block:
            @block.sync
            def _(sp):
                halves = lambda src, n: src[:, n * 512:(n + 1) * 512]
                ga, gb = w_in[:, GATE_A:GATE_A + D], w_in[:, GATE_G:GATE_G + D]
                for slot, src in ((0, halves(wpa, 0)), (1, halves(ga, 0)), (2, halves(wpg, 0)), (4, halves(gb, 0)),
                                  (6, halves(wpa, 1)), (7, halves(ga, 1))):
                    w5.append((slot, load_slab(sp, slot, src, 512)))
                sp.wait_ge(p5, 16)
                for slot, src in ((0, halves(wpg, 1)), (1, halves(gb, 1)), (2, halves(wo, 0)), (4, halves(wo, 1))):
                    w5.append((slot, load_slab(sp, slot, src, 512)))

            @block.tensor
            def _(pe):
                acts = (oaT, hT, ogT, hT)
                for j in range(KD):
                    ws = w5[0:4] if j < 4 else w5[4:8]
                    for i in range(4):
                        slot, (sm, val) = ws[i]
                        if j % 4 == 0:
                            pe.wait_ge(sm, val)
                        if j >= 2 and i == 0:
                            pe.wait_ge(merge5, j - 1)
                        for k in range(KD):
                            m = pe.matmul(PS[4 * (j % 2) + i][:, :], slab(slot)[:, k, (j % 4) * P:(j % 4 + 1) * P],
                                          acts[i][:, k, :], start=(k == 0), stop=(k == KD - 1))
                        m.then_inc(p5, 1)
                pe.wait_ge(merge5, KD)
                for n in range(2):
                    slot, (sm, val) = w5[8 + n]
                    pe.wait_ge(sm, val)
                    for t in range(NT):
                        u = n * NT + t
                        if u >= 4:
                            pe.wait_ge(out5, u - 3)
                        for k in range(KD):
                            m = pe.matmul(PS[u % 4][:, :], mT[:, k, t * P:(t + 1) * P], slab(slot)[:, k, :],
                                          start=(k == 0), stop=(k == KD - 1))
                        m.then_inc(m5, 1)

            @block.scalar
            def _(act):
                a = A()
                for j in range(KD):
                    for i in range(2):
                        act.wait_ge(p5, 4 * j + 2 * i + 2)
                        if j >= 2:
                            act.wait_ge(merge5, j - 1)
                        a(nc.scalar.activation(tm[2 * (j % 2) + i], PS[4 * (j % 2) + 2 * i + 1][:, :], ACT.Sigmoid), gate5)

            @block.vector
            def _(dve):
                v = V()
                tt = nc.vector.tensor_tensor
                for j in range(KD):
                    for i in range(2):
                        s_ = tm[2 * (j % 2) + i]
                        dve.wait_ge(gate5, 2 * j + i + 1)
                        v(tt(s_, s_, PS[4 * (j % 2) + 2 * i][:, :], ALU.mult))
                    v(tt(mT[:, j, :], tm[2 * (j % 2)], tm[2 * (j % 2) + 1], ALU.add), merge5)
                for u in range(2 * NT):
                    n, t = u // NT, u % NT
                    xs = x3[:, t, n * 512:(n + 1) * 512]
                    dve.wait_ge(m5, u + 1)
                    v(tt(xs, xs, PS[u % 4][:, :], ALU.add), out5)
        if upto == 5:
            return dump(locals())

        h2 = R[5][:, :].rearrange("p (t d) -> p t d", t=NT)
        Sel = R[6][:, :].rearrange("p (t n) -> p t n", t=NT)
        SelW = R[4][:, :].rearrange("p (t n) -> p t n", t=NT)
        n2row = R[4][:, 0:D]
        NPAIR = NE // 2
        XE = R12[:, :].rearrange("p (q k n) -> p q k n", q=NPAIR, k=KD)
        ST = HT[:, :].rearrange("p (q t n) -> p q t n", q=NPAIR, t=NT)
        affT, mx8 = SL[3][0:NE, 0:S], SL[3][0:NE, S:S + 8]
        wr = wab_[:, 0:KD * NE].rearrange("p (k e) -> p k e", k=KD)
        lg, msk, posm = sa, sb_, G
        lg3, aff3, msk3, posm3 = (ap.rearrange("p (t e) -> p t e", t=NT) for ap in (lg, aff, msk, posm))
        names = ("n2", "wr", "ss", "rstd", "h2", "t_done", "t_evac", "lg_done", "lgm", "exp", "aff", "affT", "affTc", "mask", "mT",
                 "mc", "pos", "sel", "selw", "xe", "xe_evac", "st", "st_evac")
        E6 = {n: sem("r_" + n) for n in names}
        w_gate, w_up, w_down = io["w_gate"][0], io["w_up"][0], io["w_down"][0]
        RING = [SL[0], SL[1], SL[2], SL[3], R[3], R[4]]
        NR = len(RING)
        PER = 12
        DOWN = (0, 2, 1, 3)
        ring_in = [sem(f"ring_in{i}") for i in range(NR)]

        def expert_slab(eng, r, x):
            x, part = x + r // PER, r % PER
            dst = RING[r % NR]
            if part < 8:
                w = (w_gate, w_up)[part % 4 // 2]
                f0 = part // 4 * 512 + part % 2 * 1024
                src = w[bass.ds(x, 1), :, f0:f0 + 512].rearrange("o (k p) n -> p (o k) n", p=P)
                dst = dst[:, :].rearrange("p (k n) -> p k n", k=KD)
            else:
                f0 = DOWN[part - 8] * 512
                src = w_down[bass.ds(x, 1), f0:f0 + 512, :].rearrange("o (k p) n -> p (o k) n", p=P)
                dst = dst[:, :].rearrange("p (k n) -> p k n", k=4)
            eng.dma_start(dst, src).then_inc(ring_in[r % NR], 16)

        with nc.Block() as block:
            @block.sync
            def _(sp):
                sp.dma_start(wr, io["w_router"][0].rearrange("(k p) e -> p k e", p=P)).then_inc(E6["wr"], 16)
                sp.dma_start(n2row, io["norm2_w"].to_broadcast([P, D])).then_inc(E6["n2"], 16)
                for r in range(3):
                    expert_slab(sp, r, 0)

            @block.scalar
            def _(act):
                a = A()
                for t in range(NT):
                    a(nc.scalar.activation(Sel[:, t, :], x3[:, t, :], ACT.Square, accum_out=stat[:, t:t + 1]))
                rsqrt(a, stat[:, 8:12], stat[:, 0:4], 1.0 / D, E6["rstd"])
                for k in range(KD):
                    act.wait_ge(E6["t_done"], k + 1)
                    a(nc.scalar.activation(hT[:, k, :], PS[k % 4][:, :], ACT.Copy), E6["t_evac"])
                act.wait_ge(E6["lgm"], 1)
                a(nc.scalar.activation(lg, lg, ACT.Exp), E6["exp"])
                act.wait_ge(E6["affT"], 1)
                a(nc.scalar.activation(affT, PS[5][0:NE, :], ACT.Copy), E6["affTc"])
                act.wait_ge(E6["mT"], 1)
                a(nc.scalar.activation(msk, PS[6][:, 0:64], ACT.Copy), E6["mc"])
                for u in range(2 * KD):
                    k, hf = u // 2, u % 2
                    act.wait_ge(E6["xe"], u + 1)
                    a(nc.scalar.activation(XE[:, 4 * hf:4 * hf + 4, k, :], PS[u % 4][:, :].rearrange("p (q n) -> p q n", q=4),
                                           ACT.Copy), E6["xe_evac"])

            @block.tensor
            def _(pe):
                pe.wait_ge(E6["h2"], NT)
                for k in range(KD):
                    if k >= 4:
                        pe.wait_ge(E6["t_evac"], k - 3)
                    for t in range(NT):
                        m = pe.transpose(PS[k % 4][:, t * P:(t + 1) * P], h2[:, t, k * P:(k + 1) * P], ident)
                    m.then_inc(E6["t_done"], 1)
                pe.wait_ge(E6["t_evac"], KD)
                pe.wait_ge(E6["wr"], 16)
                for t in range(NT):
                    for k in range(KD):
                        m = pe.matmul(PS[4][:, t * NE:(t + 1) * NE], hT[:, k, t * P:(t + 1) * P], wr[:, k, :],
                                      start=(k == 0), stop=(k == KD - 1))
                m.then_inc(E6["lg_done"], 1)
                pe.wait_ge(E6["aff"], 1)
                for t in range(NT):
                    m = pe.transpose(PS[5][0:NE, t * P:(t + 1) * P], aff3[:, t, :], ident)
                m.then_inc(E6["affT"], 1)
                pe.wait_ge(E6["mask"], 1)
                for t in range(NT):
                    m = pe.transpose(PS[6][:, t * NE:(t + 1) * NE], affT[:, t * P:(t + 1) * P], ident[0:NE, 0:NE])
                m.then_inc(E6["mT"], 1)
                pe.wait_ge(E6["mc"], 1)
                for t in range(NT):
                    for t_ in range(t + 1):
                        m = pe.matmul(PS[7][:, t * NE:(t + 1) * NE], tri_le if t_ == t else ones, msk3[:, t_, :],
                                      start=(t_ == 0), stop=(t_ == t))
                m.then_inc(E6["pos"], 1)
                pe.wait_ge(E6["sel"], NT)
                for u in range(2 * KD):
                    k, hf = u // 2, u % 2
                    if u >= 4:
                        pe.wait_ge(E6["xe_evac"], u - 3)
                    for t in range(NT):
                        m = pe.matmul(PS[u % 4][:, :], h2[:, t, k * P:(k + 1) * P], Sel[:, t, hf * 512:(hf + 1) * 512],
                                      start=(t == 0), stop=(t == NT - 1))
                    m.then_inc(E6["xe"], 1)
                pe.wait_ge(E6["selw"], NT)
                for q in range(NPAIR):
                    if q >= 4:
                        pe.wait_ge(E6["st_evac"], q - 3)
                    for t in range(NT):
                        m = pe.transpose(PS[4 + q % 4][:, t * P:(t + 1) * P], SelW[:, t, q * P:(q + 1) * P], ident)
                    m.then_inc(E6["st"], 1)

            @block.vector
            def _(dve):
                v = V()
                tt = nc.vector.tensor_tensor
                dve.wait_ge(E6["n2"], 16)
                dve.wait_ge(E6["rstd"], 1)
                for t in range(NT):
                    v(nc.vector.scalar_tensor_tensor(h2[:, t, :], x3[:, t, :], stat[:, 8 + t:9 + t], n2row, ALU.mult, ALU.mult), E6["h2"])
                dve.wait_ge(E6["lg_done"], 1)
                v(nc.vector.reduce_max(stat[:, 0:4], PS[4][:, 0:64].rearrange("p (t e) -> p t e", t=NT), AX))
                v(tt(lg3, PS[4][:, 0:64].rearrange("p (t e) -> p t e", t=NT), bc(stat[:, 0:4], NE), ALU.subtract), E6["lgm"])
                dve.wait_ge(E6["exp"], 1)
                v(nc.vector.reduce_sum(stat[:, 4:8], lg3, AX))
                v(nc.vector.reciprocal(stat[:, 4:8], stat[:, 4:8]))
                v(tt(aff3, lg3, bc(stat[:, 4:8], NE), ALU.mult), E6["aff"])
                dve.wait_ge(E6["affTc"], 1)
                for r in range(CAP // 8):
                    v(nc.vector.max(mx8, affT))
                    v(nc.vector.match_replace(affT, mx8, affT, -1.0))
                v(nc.vector.tensor_scalar(affT, affT, 0.0, None, ALU.is_lt), E6["mask"])
                dve.wait_ge(E6["pos"], 1)
                v(tt(posm, PS[7][:, 0:64], msk, ALU.mult))
                for t in range(NT):
                    v(tt(Sel[:, t, :].rearrange("p (e c) -> p e c", e=NE), iota.unsqueeze(1).to_broadcast([P, NE, CAP]),
                         bc(posm3[:, t, :], CAP), ALU.is_equal), E6["sel"])
                for t in range(NT):
                    v(tt(SelW[:, t, :].rearrange("p (e c) -> p e c", e=NE), Sel[:, t, :].rearrange("p (e c) -> p e c", e=NE),
                         bc(aff3[:, t, :], CAP), ALU.mult), E6["selw"])
                for q in range(NPAIR):
                    dve.wait_ge(E6["st"], q + 1)
                    v(nc.vector.tensor_copy(ST[:, q, :, :], PS[4 + q % 4][:, :].rearrange("p (t n) -> p t n", t=NT)), E6["st_evac"])
        if upto == 6:
            return dump(locals())

        XC = R[5][:, 0:1024].rearrange("p (k n) -> p k n", k=KD)
        STc = R[5][:, 1024:1536].rearrange("p (t n) -> p t n", t=NT)
        SG = [R[5][:, 1536:2048], R[5][:, 2048:2560]]
        H = R[5][:, 2560:3584].rearrange("p (j n) -> p j n", j=2)
        HTE = R[6][:, 0:1024].rearrange("p (c n) -> p c n", c=8)
        YP = R[6][:, 1024:2048]
        names = ("xc", "stc", "g_done", "u_done", "silu", "h", "tp_done", "tp_evac", "dn_done", "y", "o_done", "o_free")
        E7 = {n: sem("e_" + n) for n in names}
        GB, UB, TB, DB, OB = (PS[0], PS[1]), (PS[2], PS[3]), PS[4], PS[5], (PS[6], PS[7])
        with nc.Block() as block:
            @block.sync
            def _(sp):
                def reload(r, i):
                    sp.wait_ge(ring_in[r % NR], 16)
                    x, part = 2 * i + (r - NR) // PER, (r - NR) % PER
                    if part < 8:
                        sp.wait_ge(E7[("g_done", "u_done")[part % 4 // 2]], 2 * x + part // 4 + 1)
                    else:
                        sp.wait_ge(E7["dn_done"], 4 * x + part - 8 + 1)
                    expert_slab(sp, r, 2 * i)

                for r in range(3, NR):
                    expert_slab(sp, r, 0)
                with sp.Fori(0, NPAIR - 1) as i:
                    for r in range(NR, NR + 2 * PER):
                        reload(r, i)
                for r in range(NR, 2 * PER):
                    reload(r, NPAIR - 1)

            @block.gpsimd
            def _(pool):
                def copies(q):
                    nc.gpsimd.tensor_copy(XC, XE[:, bass.ds(q, 1), :, :].rearrange("p o k n -> p (o k) n")).then_inc(E7["xc"], 1)

                def copy_st(q):
                    nc.gpsimd.tensor_copy(STc, ST[:, bass.ds(q, 1), :, :].rearrange("p o t n -> p (o t) n")).then_inc(E7["stc"], 1)

                copies(0)
                copy_st(0)
                with pool.Fori(0, NPAIR - 1) as i:
                    pool.wait_ge(E7["u_done"], 4 * i + 4)
                    copies(i + 1)
                    pool.wait_ge(E7["o_done"], 8 * i + 8)
                    copy_st(i + 1)

            @block.tensor
            def _(pe):
                with pe.Fori(0, NPAIR) as i:
                    pe.wait_ge(E7["xc"], i + 1)
                    for e in range(2):
                        x = 2 * i + e
                        toks = slice(e * CAP, (e + 1) * CAP)

                        def arrive(part):
                            r = e * PER + part
                            pe.wait_ge(ring_in[r % NR], 64 * i + 16 * (r // NR + 1))
                            return RING[r % NR][:, :]

                        def wide(bank, part, done):
                            lo, hi = (arrive(part + n).rearrange("p (k n) -> p k n", k=KD) for n in range(2))
                            for k in range(KD):
                                pe.matmul(bank[0:CAP, :], XC[:, k, toks], lo[:, k, :], start=(k == 0), stop=(k == KD - 1))
                                m = pe.matmul(bank[CAP:P, :], XC[:, k, toks], hi[:, k, :], start=(k == 0), stop=(k == KD - 1))
                            m.then_inc(done, 1)

                        def turn(j):
                            pe.wait_ge(E7["h"], 2 * x + j + 1)
                            for c in range(4):
                                m = pe.transpose(TB[:, c * P:(c + 1) * P], H[:, j, c * P:(c + 1) * P], ident)
                            m.then_inc(E7["tp_done"], 1)

                        def down(n):
                            w = arrive(8 + n).rearrange("p (k n) -> p k n", k=4)
                            if n % 2 == 0:
                                pe.wait_ge(E7["tp_evac"], 2 * x + n // 2 + 1)
                            if n == 0 and e == 1:
                                pe.wait_ge(E7["y"], 2 * i + 1)
                            half, c0 = DOWN[n] // 2, DOWN[n] % 2 * 4
                            for k in range(4):
                                hk = HTE[:, c0 + k, half * CAP:(half + 1) * CAP]
                                first, last = n == 0 and k == 0, n == 3 and k == 3
                                pe.matmul(DB[0:CAP, :], hk, w[:, k, 0:512], start=first, stop=last)
                                m = pe.matmul(DB[CAP:P, :], hk, w[:, k, 512:1024], start=first, stop=last)
                            m.then_inc(E7["dn_done"], 1)

                        wide(GB[0], 0, E7["g_done"])
                        wide(UB[0], 2, E7["u_done"])
                        wide(GB[1], 4, E7["g_done"])
                        turn(0)
                        wide(UB[1], 6, E7["u_done"])
                        down(0)
                        down(1)
                        turn(1)
                        down(2)
                        down(3)
                    pe.wait_ge(E7["y"], 2 * i + 2)
                    pe.wait_ge(E7["stc"], i + 1)
                    for n in range(2 * NT):
                        t, half = n // 2, n % 2
                        pe.wait_ge(E7["o_free"], 8 * i + n + 1)
                        pe.matmul(OB[half][:, :], STc[:, t, :], YP[:, half * 512:(half + 1) * 512], start=True, stop=True)\
                          .then_inc(E7["o_done"], 1)

            @block.scalar
            def _(act):
                with act.Fori(0, NPAIR) as i:
                    for e in range(2):
                        x = 2 * i + e

                        def silu(j):
                            act.wait_ge(E7["g_done"], 2 * x + j + 1)
                            nc.scalar.activation(SG[j], GB[j][:, :], ACT.Silu).then_inc(E7["silu"], 1)

                        def evac(j):
                            act.wait_ge(E7["tp_done"], 2 * x + j + 1)
                            nc.scalar.activation(HTE[:, 4 * j:4 * j + 4, :], TB[:, :].rearrange("p (c n) -> p c n", c=4), ACT.Copy)\
                              .then_inc(E7["tp_evac"], 1)

                        silu(0)
                        silu(1)
                        evac(0)
                        evac(1)

            @block.vector
            def _(dve):
                dve.sem_inc(E7["o_free"], 2)
                with dve.Fori(0, NPAIR) as i:
                    for e in range(2):
                        x = 2 * i + e
                        for j in range(2):
                            dve.wait_ge(E7["u_done"], 2 * x + j + 1)
                            dve.wait_ge(E7["silu"], 2 * x + j + 1)
                            nc.vector.tensor_tensor(H[:, j, :], SG[j], UB[j][:, :], ALU.mult).then_inc(E7["h"], 1)
                        dve.wait_ge(E7["dn_done"], 4 * x + 4)
                        rows = slice(e * CAP, (e + 1) * CAP)
                        nc.vector.tensor_copy(YP[rows, 0:512], DB[0:CAP, :])
                        nc.vector.tensor_copy(YP[rows, 512:1024], DB[CAP:P, :]).then_inc(E7["y"], 1)
                    for n in range(2 * NT):
                        t, half = n // 2, n % 2
                        xs = x3[:, t, half * 512:(half + 1) * 512]
                        dve.wait_ge(E7["o_done"], 8 * i + n + 1)
                        nc.vector.tensor_tensor(xs, xs, OB[half][:, :], ALU.add).then_inc(E7["o_free"], 1)
        if upto == 7:
            return dump(locals())

        spent.extend([p5, gate5, merge5, m5, out5, *E6.values(), *E7.values()])
        clear_spent()
        w2 = io["w_in_2"][0]
        nfrow = R[1][:, 0:D]
        junk = R[5][:, :].rearrange("p (t d) -> p t d", t=NT)
        E8 = {n: sem("f_" + n) for n in ("nf", "rstd", "x", "t_done", "t_evac", "misc")}
        PROJ2 = [("a_q", A_Q), ("a_iq", A_IQ), ("misc", None), ("b_i", B_I), ("a_gate", A_GATE), ("b_q", B_Q),
                 ("b_gate", B_GATE), ("b_f", B_F)]
        MISC = P + 64 + 64 + 8
        w_uk, w_uv = (SL[3][:, i * 512:(i + 1) * 512].rearrange("p (h r) -> p h r", h=4) for i in range(2))
        onehot = SL[3][0:32, 1024:1024 + REL]
        rb = SL[3][0:32, 1664:1668]
        kvrow = stat128
        start8 = list(slab_n)

        def load2(eng, i):
            name, c0 = PROJ2[i]
            if name == "misc":
                dst = SL[i % 3][:, 0:KD * MISC].rearrange("p (k n) -> p k n", k=KD)
                for to, c, n in ((0, A_CKV, P), (P, A_IK, 64), (P + 64, A_IK, 64), (2 * P, A_IW, 8)):
                    eng.dma_start(dst[:, :, to:to + n], w2[:, c:c + n].rearrange("(k p) n -> p k n", p=P)).then_inc(slab_in[i % 3], 16)
                slab_n[i % 3] += 64
            else:
                load_slab(eng, i % 3, w2[:, c0:c0 + 512], 512)
            after2[i] = slab_n[i % 3]

        after2 = {}
        with nc.Block() as block:
            @block.sync
            def _(sp):
                sp.dma_start(nfrow, io["norm_f_w"].unsqueeze(0).to_broadcast([P, D])).then_inc(E8["nf"], 16)
                for i in range(3):
                    load2(sp, i)
                sp.dma_start(kvrow, io["kv_norm_g_2"].to_broadcast([P, P])).then_inc(E8["misc"], 16)
                sp.dma_start(w_uk, io["w_uk_2"][0].rearrange("h d r -> d h r")).then_inc(E8["misc"], 16)
                sp.dma_start(w_uv, io["w_uv_2"][0].rearrange("h r v -> r h v")).then_inc(E8["misc"], 16)
                sp.dma_start(onehot, io["table"][0:32, T_BUCKET:T_BUCKET + REL]).then_inc(E8["misc"], 16)
                sp.dma_start(rb, io["rel_bias_2"]).then_inc(E8["misc"], 16)

            @block.scalar
            def _(act):
                a = A()
                for t in range(NT):
                    a(nc.scalar.activation(junk[:, t, :], x3[:, t, :], ACT.Square, accum_out=stat[:, t:t + 1]))
                rsqrt(a, stat[:, 8:12], stat[:, 0:4], 1.0 / D, E8["rstd"])
                for k in range(KD):
                    act.wait_ge(E8["t_done"], k + 1)
                    a(nc.scalar.activation(hT[:, k, :], PS[k % 4][:, :], ACT.Copy), E8["t_evac"])

            @block.tensor
            def _(pe):
                pe.wait_ge(E8["x"], NT)
                for k in range(KD):
                    if k >= 4:
                        pe.wait_ge(E8["t_evac"], k - 3)
                    for t in range(NT):
                        m = pe.transpose(PS[k % 4][:, t * P:(t + 1) * P], x3[:, t, k * P:(k + 1) * P], ident)
                    m.then_inc(E8["t_done"], 1)

            @block.vector
            def _(dve):
                v = V()
                dve.wait_ge(E8["nf"], 16)
                dve.wait_ge(E8["rstd"], 1)
                for t in range(NT):
                    xs = x3[:, t, :]
                    v(nc.vector.scalar_tensor_tensor(xs, xs, stat[:, 8 + t:9 + t], nfrow, ALU.mult, ALU.mult), E8["x"])
        if upto == 8:
            return dump(locals())

        def r4(ap):
            return ap.rearrange("p (h s) -> p h s", h=4)

        aqT, qlT = r4(R[1][:, 0:2048]), r4(R[1][:, 2048:4096])
        iqT, ikz = r4(R[2][:, 0:2048]), (R[2][:, 2048:2560], R[2][:, 2560:3072])
        cT, ctok = R[2][:, 3072:3584], R[2][:, 3584:4096].rearrange("p (t r) -> p t r", t=NT)
        agT, bgT = r4(R[3][:, 0:2048]), r4(R[3][:, 2048:4096])
        bqT, kkT = r4(R[4][:, 0:2048]), r4(R[4][:, 2048:4096])
        bT, vtok = r4(R[5][:, 0:2048]), r4(R[5][:, 2048:4096])
        iw = gl[:, 0:32]
        lb, olb, lbt = stat[:, 12:16], stat[:, 16:20], stat[:, 20:32]
        sig = [R[6][:, i * 512:(i + 1) * 512] for i in range(2)]
        csq = R[6][:, 1024:1536]
        E9 = {n: sem("g_" + n) for n in ("p", "evac", "ikpad", "lbd", "lbe", "lb", "c_rstd", "c", "ct", "ct_evac", "ql", "ql_evac", "f", "slab")}
        UNITS = []
        for i, (name, _) in enumerate(PROJ2):
            UNITS += [(i, name, j) for j in range(3 if name == "misc" else 4)]
        ctok_ps = 0
        with nc.Block() as block:
            @block.sync
            def _(sp):
                for i in range(3, len(PROJ2)):
                    used = max(n for n, u in enumerate(UNITS) if u[0] == i - 3) + 1
                    sp.wait_ge(E9["p"], used)
                    load2(sp, i)

            @block.gpsimd
            def _(pool):
                g = G_()
                g(nc.gpsimd.memset(ikz[0][64:128, :], 0.0), E9["ikpad"])
                g(nc.gpsimd.memset(ikz[1][0:64, :], 0.0), E9["ikpad"])

            @block.tensor
            def _(pe):
                pe.wait_ge(E8["misc"], 80)

                def c_turn():
                    pe.wait_ge(E9["c"], 4)
                    for t in range(NT):
                        m = pe.transpose(PS[4][:, t * P:(t + 1) * P], ctok[:, t, :], ident)
                    m.then_inc(E9["ct"], 1)

                def q_lat(h):
                    if h >= 2:
                        pe.wait_ge(E9["ql_evac"], h - 1)
                    pe.matmul(PS[5 + h % 2][:, :], w_uk[:, h, :], aqT[:, h, :], start=True, stop=True).then_inc(E9["ql"], 1)

                for n, (i, name, j) in enumerate(UNITS):
                    pe.wait_ge(slab_in[i % 3], after2[i])
                    if n >= 4:
                        pe.wait_ge(E9["evac"], n - 3)
                    bank = PS[n % 4]
                    if name == "misc":
                        w = SL[i % 3][:, 0:KD * MISC].rearrange("p (k n) -> p k n", k=KD)
                        if j == 0 or j == 1:
                            c0, cn = (0, P) if j == 0 else (2 * P, 8)
                            for t in range(NT):
                                for k in range(KD):
                                    m = pe.matmul(bank[:, t * cn:(t + 1) * cn], hT[:, k, t * P:(t + 1) * P], w[:, k, c0:c0 + cn],
                                                  start=(k == 0), stop=(k == KD - 1))
                        else:
                            for k in range(KD):
                                m = pe.matmul(bank[:, :], w[:, k, P:2 * P], hT[:, k, :], start=(k == 0), stop=(k == KD - 1))
                    elif name == "b_i":
                        for k in range(KD):
                            m = pe.matmul(bank[:, :], hT[:, k, j * P:(j + 1) * P], slab(i % 3)[:, k, :],
                                          start=(k == 0), stop=(k == KD - 1))
                    else:
                        for k in range(KD):
                            m = pe.matmul(bank[:, :], slab(i % 3)[:, k, j * P:(j + 1) * P], hT[:, k, :],
                                          start=(k == 0), stop=(k == KD - 1))
                    m.then_inc(E9["p"], 1)
                    if name == "a_gate" and j == 0:
                        c_turn()
                    if name == "a_gate":
                        q_lat(j)

            @block.scalar
            def _(act):
                a = A()
                act.wait_ge(E9["lbd"], 1)
                a(nc.scalar.activation(lbt[:, 0:8], lbt[:, 0:8], ACT.Exp), E9["lbe"])
                act.wait_ge(E9["ikpad"], 2)
                cp = nc.scalar.activation
                for n, (i, name, j) in enumerate(UNITS):
                    bank = PS[n % 4]
                    act.wait_ge(E9["p"], n + 1)
                    if name == "a_q":
                        a(cp(aqT[:, j, :], bank[:, :], ACT.Copy), E9["evac"])
                    elif name == "a_iq":
                        a(cp(iqT[:, j, :], bank[:, :], ACT.Copy), E9["evac"])
                    elif name == "misc" and j == 0:
                        a(cp(ctok.rearrange("p t r -> p (t r)"), bank[:, :], ACT.Copy), E9["evac"])
                        for t in range(NT):
                            a(cp(csq[:, t * P:(t + 1) * P], ctok[:, t, :], ACT.Square, accum_out=stat[:, t:t + 1]))
                        rsqrt(a, stat[:, 4:8], stat[:, 0:4], 1.0 / P, E9["c_rstd"])
                    elif name == "misc" and j == 1:
                        a(cp(iw, bank[:, 0:32], ACT.Copy, scale=8 ** -0.5), E9["evac"])
                    elif name == "misc":
                        a(cp(ikz[0][0:64, :], bank[0:64, :], ACT.Copy))
                        a(cp(ikz[1][64:128, :], bank[64:128, :], ACT.Copy), E9["evac"])
                    elif name == "b_i":
                        a(cp(vtok[:, j, :], bank[:, :], ACT.Copy), E9["evac"])
                    elif name == "b_f":
                        if j >= 2:
                            act.wait_ge(E9["f"], j - 1)
                        a(cp(sig[j % 2], bank[:, :], ACT.Sigmoid), E9["evac"])
                    else:
                        dst = {"a_gate": agT, "b_q": bqT, "b_gate": bgT}[name]
                        a(cp(dst[:, j, :], bank[:, :], ACT.Silu), E9["evac"])
                    if name == "a_gate" and j == 0:
                        act.wait_ge(E9["ct"], 1)
                        a(cp(cT, PS[4][:, :], ACT.Copy), E9["ct_evac"])
                    if name == "a_gate":
                        act.wait_ge(E9["ql"], j + 1)
                        a(cp(qlT[:, j, :], PS[5 + j % 2][:, :], ACT.Copy), E9["ql_evac"])
                act.wait_ge(E9["f"], 4)
                a(cp(bT, bT, ACT.Ln))

            @block.vector
            def _(dve):
                v = V()
                tt, ts = nc.vector.tensor_tensor, nc.vector.tensor_scalar
                v(tt(lbt[:, 8:12], lbc[:, 0:4], lbc[:, 4:8], ALU.max))
                v(tt(lbt[:, 0:4], lbc[:, 0:4], lbt[:, 8:12], ALU.subtract))
                v(tt(lbt[:, 4:8], lbc[:, 4:8], lbt[:, 8:12], ALU.subtract), E9["lbd"])
                dve.wait_ge(E9["lbe"], 1)
                v(tt(lbt[:, 8:12], lbt[:, 0:4], lbt[:, 4:8], ALU.add))
                v(nc.vector.reciprocal(lbt[:, 8:12], lbt[:, 8:12]))
                v(tt(lb, lbt[:, 0:4], lbt[:, 8:12], ALU.mult))
                v(ts(olb, lb, -1.0, 1.0, ALU.mult, ALU.add))
                dve.wait_ge(E8["misc"], 80)
                dve.wait_ge(E9["c_rstd"], 1)
                for t in range(NT):
                    v(nc.vector.scalar_tensor_tensor(ctok[:, t, :], ctok[:, t, :], stat[:, 4 + t:5 + t], kvrow, ALU.mult, ALU.mult), E9["c"])
                at_f = min(n for n, u in enumerate(UNITS) if u[1] == "b_f")
                for j in range(4):
                    dve.wait_ge(E9["evac"], at_f + j + 1)
                    v(ts(bT[:, j, :], sig[j % 2], olb[:, j:j + 1], lb[:, j:j + 1], ALU.mult, ALU.add))
                    v(ts(kkT[:, j, :], bT[:, j, :], -1.0, 1.0, ALU.mult, ALU.add), E9["f"])
        if upto == 9:
            return dump(locals())

        bias_m = r4(SL[0][:, 0:2048])
        keep = r4(SL[1][:, 0:2048])
        frow = SL[2][:, 0:4 * REL].rearrange("p (h u) -> p h u", h=4)
        score = [SL[0][:, 2048 + i * 512:2560 + i * 512] for i in range(3)]
        rel = [SL[1][:, 2048 + i * 512:2560 + i * 512] for i in range(4)]
        mx = stat[:, 0:8]
        scratch = io["scratch"]
        E10 = {n: sem("i_" + n) for n in ("dot", "relu", "used", "f", "fr", "out", "in")}
        ITEMS = [(t, h) for t in range(1, NT) for h in range(8)]
        with nc.Block() as block:
            @block.tensor
            def _(pe):
                for h in range(4):
                    if h:
                        pe.wait_ge(E10["fr"], h)
                    pe.matmul(PS[4][:, :], rb[:, h:h + 1].to_broadcast([32, P]), onehot[:, 0:512], start=True, stop=True)
                    pe.matmul(PS[5][:, 0:REL - 512], rb[:, h:h + 1].to_broadcast([32, P]), onehot[:, 512:REL],
                              start=True, stop=True).then_inc(E10["f"], 1)
                for n, (t, h) in enumerate(ITEMS):
                    W = (t + 1) * P
                    if n >= 4:
                        pe.wait_ge(E10["relu"], n - 3)
                    pe.matmul(PS[n % 4][:, 0:W], iqT[:, h // 2, t * P:(t + 1) * P], ikz[h % 2][:, 0:W],
                              start=True, stop=True).then_inc(E10["dot"], 1)

            @block.scalar
            def _(act):
                a = A()
                for h in range(4):
                    act.wait_ge(E10["f"], h + 1)
                    a(nc.scalar.activation(frow[:, h, 0:512], PS[4][:, :], ACT.Copy))
                    a(nc.scalar.activation(frow[:, h, 512:REL], PS[5][:, 0:REL - 512], ACT.Copy), E10["fr"])
                for n, (t, h) in enumerate(ITEMS):
                    W = (t + 1) * P
                    act.wait_ge(E10["dot"], n + 1)
                    if n >= 4:
                        act.wait_ge(E10["used"], n - 3)
                    a(nc.scalar.activation(rel[n % 4][:, 0:W], PS[n % 4][:, 0:W], ACT.Relu, scale=0.125), E10["relu"])

            @block.sync
            def _(sp):
                for h in range(4):
                    sp.wait_ge(E10["fr"], h + 1)
                    sp.dma_start(scratch[h].rearrange("(p u) -> p u", p=P), frow[:, h, :]).then_inc(E10["out"], 16)
                sp.wait_ge(E10["out"], 64)
                for h in range(4):
                    skew = scratch[h, P - 1:P - 1 + P * (REL - 1)].rearrange("(p u) -> p u", p=P)[:, 0:512]
                    sp.dma_start(bias_m[:, h, :], skew).then_inc(E10["in"], 16)
                sp.wait_ge(E10["in"], 64)

            @block.vector
            def _(dve):
                v = V()
                ts = nc.vector.tensor_scalar
                for n, (t, h) in enumerate(ITEMS):
                    W = (t + 1) * P
                    sc, r = score[t - 1][:, 0:W], rel[n % 4][:, 0:W]
                    w = iw[:, t * 8 + h:t * 8 + h + 1]
                    dve.wait_ge(E10["relu"], n + 1)
                    if h == 0:
                        v(ts(sc, r, w, None, ALU.mult), E10["used"])
                    else:
                        v(nc.vector.scalar_tensor_tensor(sc, r, w, sc, ALU.mult, ALU.add), E10["used"])
                for t in range(NT):
                    W = (t + 1) * P
                    k_ = keep[:, t, 0:W]
                    if t == 0:
                        v(nc.vector.memset(k_, 0.0))
                        v(nc.vector.memset(keep[0:64, t, 64:P], -BIG))
                        continue
                    sc = score[t - 1]
                    v(nc.vector.memset(sc[0:64, W - 64:W], -BIG))
                    for r in range(TOPK // 8):
                        v(nc.vector.max(mx, sc[:, 0:W]))
                        v(nc.vector.match_replace(sc[:, 0:W], mx, sc[:, 0:W], -STRUCK))
                    v(ts(k_, sc[:, 0:W], -0.5 * (BIG + STRUCK), -BIG, ALU.is_gt, ALU.mult))
        if upto == 10:
            return dump(locals())

        oT = R[6][:, :].rearrange("p (k s) -> p k s", k=KD)
        lgt = [SL[2][:, i * 512:(i + 1) * 512] for i in range(2)]
        pTc = [SL[2][:, 1024 + i * 512:1536 + i * 512].rearrange("p (c q) -> p c q", c=NT) for i in range(2)]
        olT = [SL[2][:, 2048 + i * 512:2560 + i * 512] for i in range(2)]
        E11 = {n: sem("j_" + n) for n in ("s", "lm", "exp", "p", "t", "te", "o", "oe", "v", "g")}
        NU2 = 4 * NT
        with nc.Block() as block:
            @block.tensor
            def _(pe):
                def turn(n):
                    t = n % NT
                    pe.wait_ge(E11["p"], n + 1)
                    if n >= 2:
                        pe.wait_ge(E11["te"], n - 1)
                    for c in range(t + 1):
                        m = pe.transpose(PS[2 + n % 2][:, c * P:(c + 1) * P], lgt[n % 2][:, c * P:(c + 1) * P], ident)
                    m.then_inc(E11["t"], 1)

                def pv(n):
                    h, t = n // NT, n % NT
                    pe.wait_ge(E11["te"], n + 1)
                    if t == 0 and h >= 2:
                        pe.wait_ge(E11["oe"], h - 1)
                    for c in range(t + 1):
                        m = pe.matmul(PS[4 + h % 2][:, t * P:(t + 1) * P], ctok[:, c, :], pTc[n % 2][:, c, :],
                                      start=(c == 0), stop=(c == t))
                    m.then_inc(E11["o"], 1)

                def up_v(h):
                    pe.wait_ge(E11["oe"], h + 1)
                    if h >= 2:
                        pe.wait_ge(E11["g"], h - 1)
                    pe.matmul(PS[6 + h % 2][:, :], w_uv[:, h, :], olT[h % 2], start=True, stop=True).then_inc(E11["v"], 1)

                for n in range(NU2 + 3):
                    if n < NU2:
                        h, t = n // NT, n % NT
                        if n >= 2:
                            pe.wait_ge(E11["lm"], n - 1)
                        pe.matmul(PS[n % 2][:, 0:(t + 1) * P], qlT[:, h, t * P:(t + 1) * P], cT[:, 0:(t + 1) * P],
                                  start=True, stop=True).then_inc(E11["s"], 1)
                    if 1 <= n <= NU2:
                        turn(n - 1)
                    if 2 <= n <= NU2 + 1:
                        pv(n - 2)
                    if n >= 6 and (n - 6) % NT == 0:
                        up_v((n - 6) // NT)

            @block.scalar
            def _(act):
                a = A()

                def evac(n):
                    t = n % NT
                    act.wait_ge(E11["t"], n + 1)
                    if n >= 2:
                        act.wait_ge(E11["o"], n - 1)
                    a(nc.scalar.activation(pTc[n % 2][:, 0:t + 1, :],
                                           PS[2 + n % 2][:, 0:(t + 1) * P].rearrange("p (c q) -> p c q", c=t + 1), ACT.Copy), E11["te"])
                    if t == NT - 1:
                        h = n // NT
                        act.wait_ge(E11["o"], n + 1)
                        if h >= 2:
                            act.wait_ge(E11["v"], h - 1)
                        a(nc.scalar.activation(olT[h % 2], PS[4 + h % 2][:, :], ACT.Copy), E11["oe"])

                for n in range(NU2):
                    W = (n % NT + 1) * P
                    s = stat[:, 8 * (n % 2):8 * (n % 2) + 8]
                    act.wait_ge(E11["lm"], n + 1)
                    a(nc.scalar.activation(lgt[n % 2][:, 0:W], lgt[n % 2][:, 0:W], ACT.Exp, bias=s[:, 1:2], accum_out=s[:, 2:3]), E11["exp"])
                    if n >= 1:
                        evac(n - 1)
                evac(NU2 - 1)

            @block.vector
            def _(dve):
                v = V()
                tt, ts = nc.vector.tensor_tensor, nc.vector.tensor_scalar

                def logits(n):
                    h, t = n // NT, n % NT
                    W = (t + 1) * P
                    s = stat[:, 8 * (n % 2):8 * (n % 2) + 8]
                    l = lgt[n % 2][:, 0:W]
                    dve.wait_ge(E11["s"], n + 1)
                    if n >= 2:
                        dve.wait_ge(E11["t"], n - 1)
                    v(nc.vector.scalar_tensor_tensor(l, PS[n % 2][:, 0:W], P ** -0.5, bias_m[:, h, 512 - W:512], ALU.mult, ALU.add))
                    v(tt(l, l, keep[:, t, 0:W], ALU.add))
                    v(nc.vector.reduce_max(s[:, 0:1], l, AX))
                    v(ts(s[:, 1:2], s[:, 0:1], -1.0, None, ALU.mult), E11["lm"])

                def out(h):
                    dve.wait_ge(E11["v"], h + 1)
                    v(tt(oT[:, h, :], PS[6 + h % 2][:, :], agT[:, h, :], ALU.mult), E11["g"])

                logits(0)
                for n in range(NU2):
                    if n + 1 < NU2:
                        logits(n + 1)
                    W = (n % NT + 1) * P
                    s = stat[:, 8 * (n % 2):8 * (n % 2) + 8]
                    l = lgt[n % 2][:, 0:W]
                    dve.wait_ge(E11["exp"], n + 1)
                    v(nc.vector.reciprocal(s[:, 3:4], s[:, 2:3]))
                    v(ts(l, l, s[:, 3:4], None, ALU.mult), E11["p"])
                    if n >= 7 and (n - 7) % NT == 0:
                        out((n - 7) // NT)
                out(2)
                out(3)
        if upto == 11:
            return dump(locals())

        FB = [SL[0][:, 0:2048], SL[0][:, 2048:4096]]
        QF = [SL[1][:, 0:2048], SL[1][:, 2048:4096]]
        KF = [SL[2][:, 0:2048], SL[2][:, 2048:4096]]
        sco = SL[3][:, 0:2048].rearrange("p (a t) -> p a t", a=16)
        QE = SL[3][:, 2048:4096].rearrange("p (a t) -> p a t", a=16)
        bq, kk, bb = R[4][:, 0:2048], R[4][:, 2048:4096], R[5][:, 0:2048]
        resets = HT[:, 0:2048]
        KDt = HT[:, 2048:4096].rearrange("p (a d) -> p a d", a=16)
        Sb = R[1][:, 0:512].rearrange("p (h d) -> p h d", h=4)
        eL = decs[:, 0:16]
        sq12 = [R[1][:, 1024:1536], R[1][:, 1536:2048]]
        rs12 = [R[1][:, 2048:2560], R[1][:, 2560:3072]]
        c16 = lambda ap: ap.rearrange("p (a t) -> p a t", a=16)
        E12 = {n: sem("k_" + n) for n in ("reset", "b", "diff", "F", "Q", "K", "s", "sc", "e", "qe", "kd", "t", "te", "o", "oe", "u", "S", "sq", "ss", "rs", "n", "el")}
        LV = [None] + LEVELS
        wo2 = io["w_o_2"][0]
        with nc.Block() as block:
            @block.gpsimd
            def _(pool):
                g = G_()
                g(nc.gpsimd.memset(resets, 1.0))
                g(nc.gpsimd.memset(c16(resets)[:, :, 0:1], 0.0), E12["reset"])
                for i in range(1, NL + 1):
                    pool.wait_ge(E12["F"], i)
                    if i >= 2:
                        pool.wait_ge(E12["s"], 4 * (i - 1))
                    g(nc.gpsimd.tensor_tensor(KF[i % 2], kk, FB[i % 2], ALU.mult), E12["K"])
                pool.wait_ge(E12["e"], 1)
                g(nc.gpsimd.tensor_tensor(QE.rearrange("p a t -> p (a t)"), bq, FB[0], ALU.mult), E12["qe"])
                pool.wait_ge(E12["e"], 2)
                pool.wait_ge(E12["s"], 4 * NL + 4)
                g(nc.gpsimd.tensor_tensor(KF[0], kk, FB[1], ALU.mult), E12["kd"])

            @block.scalar
            def _(act):
                a = A()
                for i in range(1, NL + 1):
                    act.wait_ge(E12["diff"], i)
                    a(nc.scalar.activation(FB[i % 2], FB[i % 2], ACT.Abs))
                    a(nc.scalar.activation(FB[i % 2], FB[i % 2], ACT.Exp, scale=-1.0), E12["F"])
                act.wait_ge(E12["Q"], NL - 1)
                act.wait_ge(E12["K"], NL - 1)
                a(nc.scalar.activation(FB[0], bb, ACT.Exp), E12["e"])
                a(nc.scalar.activation(eL, c16(bb)[:, :, P - 1], ACT.Exp), E12["el"])
                act.wait_ge(E12["diff"], NL + 1)
                a(nc.scalar.activation(FB[1], FB[1], ACT.Exp, scale=-1.0), E12["e"])
                for u in range(4):
                    act.wait_ge(E12["t"], u + 1)
                    a(nc.scalar.activation(KDt[:, 4 * u:4 * u + 4, :], PS[4 + u % 2][:, :].rearrange("p (a d) -> p a d", a=4), ACT.Copy), E12["te"])

                def norm(h):
                    act.wait_ge(E12["ss"], h + 1)
                    if h >= 2:
                        act.wait_ge(E12["n"], h - 1)
                    rsqrt(a, rs12[h % 2], PS[h % 2][:, :], 1.0 / P, E12["rs"])

                act.wait_ge(E12["oe"], NT)
                for h in range(4):
                    if h >= 2:
                        act.wait_ge(E12["ss"], h - 1)
                    a(nc.scalar.activation(sq12[h % 2], oT[:, 4 + h, :], ACT.Square), E12["sq"])
                    if h >= 1:
                        norm(h - 1)
                norm(3)

            @block.tensor
            def _(pe):
                for i in range(NL + 1):
                    if i:
                        pe.wait_ge(E12["Q"], i)
                        pe.wait_ge(E12["K"], i)
                    k_, q_ = (c16(kk), c16(bq)) if i == 0 else (c16(KF[i % 2]), c16(QF[i % 2]))
                    for u in range(4):
                        if i:
                            pe.wait_ge(E12["sc"], 4 * (i - 1) + u + 1)
                        for j in range(4):
                            m = pe.matmul(PS[u][:, j * P:(j + 1) * P], k_[:, 4 * u + j, :], q_[:, 4 * u + j, :], start=True, stop=True)
                        m.then_inc(E12["s"], 1)
                pe.wait_ge(E12["kd"], 1)
                for u in range(4):
                    if u >= 2:
                        pe.wait_ge(E12["te"], u - 1)
                    for j in range(4):
                        m = pe.transpose(PS[4 + u % 2][:, j * P:(j + 1) * P], c16(KF[0])[:, 4 * u + j, :], ident)
                    m.then_inc(E12["t"], 1)
                pe.wait_ge(E12["te"], 4)
                pe.wait_ge(E12["qe"], 1)
                pe.wait_ge(E12["sc"], 4 * NL + 4)
                for c in range(NT):
                    if c:
                        pe.wait_ge(E12["S"], c)
                    for h in range(4):
                        a_ = 4 * h + c
                        o = PS[c % 2][:, h * P:(h + 1) * P]
                        pe.matmul(o, vtok[:, c, h * P:(h + 1) * P], sco[:, a_, :], start=True, stop=(c == 0))
                        if c:
                            m = pe.matmul(o, Sb[:, h, :], QE[:, a_, :], start=False, stop=True)
                    if c:
                        m.then_inc(E12["o"], 1)
                    for h in range(4):
                        m = pe.matmul(PS[2 + c % 2][:, h * P:(h + 1) * P], KDt[:, 4 * h + c, :], vtok[:, c, h * P:(h + 1) * P], start=True, stop=True)
                    m.then_inc(E12["u"], 1)
                pe.wait_ge(E12["oe"], NT)
                for h in range(4):
                    pe.wait_ge(E12["sq"], h + 1)
                    if h >= 2:
                        pe.wait_ge(E12["rs"], h - 1)
                    pe.matmul(PS[h % 2][:, :], ones, sq12[h % 2], start=True, stop=True).then_inc(E12["ss"], 1)

            @block.vector
            def _(dve):
                v = V()
                tt = nc.vector.tensor_tensor
                dve.wait_ge(E12["reset"], 1)
                v(nc.vector.tensor_tensor_scan(FB[0], resets, bb, 0.0, ALU.mult, ALU.add))
                v(nc.vector.tensor_copy(bb, FB[0]), E12["b"])

                def diff(i):
                    s = LEVELS[i - 1]
                    blocks = lambda ap: ap.rearrange("p (n w) -> p n w", w=2 * s)
                    mid = blocks(bb)[:, :, s - 1:s].to_broadcast([P, 2048 // (2 * s), 2 * s])
                    v(tt(blocks(FB[i % 2]), blocks(bb), mid, ALU.subtract), E12["diff"])

                def add(i):
                    mask = ident if i == 0 else up[i - 1]
                    for u in range(4):
                        dve.wait_ge(E12["s"], 4 * i + u + 1)
                        ps, dst = PS[u][:, :].rearrange("p (a t) -> p a t", a=4), sco[:, 4 * u:4 * u + 4, :]
                        if i == 0:
                            v(tt(dst, ps, all4(mask), ALU.mult), E12["sc"])
                        else:
                            tmp = R[1][:, 512:1024].rearrange("p (a t) -> p a t", a=4)
                            v(tt(tmp, ps, all4(mask), ALU.mult))
                            v(tt(dst, dst, tmp, ALU.add), E12["sc"])

                diff(1)
                add(0)
                for i in range(1, NL + 1):
                    dve.wait_ge(E12["F"], i)
                    v(tt(QF[i % 2], bq, FB[i % 2], ALU.mult), E12["Q"])
                    if i < NL:
                        if i >= 2:
                            dve.wait_ge(E12["K"], i - 1)
                        diff(i + 1)
                    add(i)
                dve.wait_ge(E12["K"], NL)
                last = c16(bb)[:, :, P - 1:P].to_broadcast([P, 16, P])
                v(tt(c16(FB[1]), c16(bb), last, ALU.subtract), E12["diff"])
                dve.wait_ge(E12["el"], 1)
                for c in range(NT):
                    if c:
                        dve.wait_ge(E12["o"], c)
                    dve.wait_ge(E12["u"], c + 1)
                    v(nc.vector.tensor_copy(oT[:, 4:8, c * P:(c + 1) * P], PS[c % 2][:, :].rearrange("p (h t) -> p h t", h=4)), E12["oe"])
                    for h in range(4):
                        ps = PS[2 + c % 2][:, h * P:(h + 1) * P]
                        sem_ = E12["S"] if h == 3 else None
                        if c == 0:
                            v(nc.vector.tensor_copy(Sb[:, h, :], ps), sem_)
                        else:
                            v(nc.vector.scalar_tensor_tensor(Sb[:, h, :], Sb[:, h, :], eL[:, 4 * h + c:4 * h + c + 1], ps, ALU.mult, ALU.add), sem_)
                for h in range(4):
                    dve.wait_ge(E12["rs"], h + 1)
                    o = oT[:, 4 + h, :]
                    v(nc.vector.scalar_tensor_tensor(o, o, hgc[:, h:h + 1], rs12[h % 2], ALU.mult, ALU.mult), E12["n"])
                    v(tt(o, o, bgT[:, h, :], ALU.mult))
        if upto == 12:
            return dump(locals())

        lgrow, lbrow = R[2][:, 0:D], R[2][:, D:2 * D]
        sqr = R[3][:, 0:D]
        E13 = {n: sem("l_" + n) for n in ("rows", "w", "y", "x", "sum", "nm", "var", "out", "st")}
        with nc.Block() as block:
            @block.sync
            def _(sp):
                for n in range(2):
                    sp.dma_start(slab(n), wo2[:, n * 512:(n + 1) * 512].rearrange("(k p) n -> p k n", p=P)).then_inc(E13["w"], 16)
                sp.dma_start(lgrow, io["ln_g_2"].to_broadcast([P, D])).then_inc(E13["rows"], 16)
                sp.dma_start(lbrow, io["ln_b_2"].to_broadcast([P, D])).then_inc(E13["rows"], 16)
                for t in range(NT):
                    sp.wait_ge(E13["out"], t + 1)
                    sp.dma_start(io["out"][0, t * P:(t + 1) * P, :], x3[:, t, :]).then_inc(E13["st"], 16)
                sp.wait_ge(E13["st"], 16 * NT)

            @block.tensor
            def _(pe):
                pe.wait_ge(E13["w"], 32)
                for t in range(NT):
                    for n in range(2):
                        for k in range(KD):
                            m = pe.matmul(PS[2 * t + n][:, :], oT[:, k, t * P:(t + 1) * P], slab(n)[:, k, :],
                                          start=(k == 0), stop=(k == KD - 1))
                        m.then_inc(E13["y"], 1)

            @block.scalar
            def _(act):
                a = A()
                for t in range(NT):
                    s = stat[:, 8 * t:8 * t + 8]
                    act.wait_ge(E13["x"], t + 1)
                    a(nc.scalar.activation(sqr, x3[:, t, :], ACT.Copy, accum_out=s[:, 0:1]), E13["sum"])
                    act.wait_ge(E13["nm"], t + 1)
                    a(nc.scalar.activation(sqr, x3[:, t, :], ACT.Square, bias=s[:, 1:2], accum_out=s[:, 2:3]))
                    rsqrt(a, s[:, 3:4], s[:, 2:3], 1.0 / D, E13["var"], eps=LN_EPS)

            @block.vector
            def _(dve):
                v = V()
                dve.wait_ge(E13["rows"], 32)

                def finish(t):
                    s = stat[:, 8 * t:8 * t + 8]
                    dve.wait_ge(E13["var"], t + 1)
                    v(nc.vector.tensor_scalar(x3[:, t, :], x3[:, t, :], s[:, 1:2], s[:, 3:4], ALU.add, ALU.mult))
                    v(nc.vector.tensor_tensor(x3[:, t, :], x3[:, t, :], lgrow, ALU.mult))
                    v(nc.vector.tensor_tensor(x3[:, t, :], x3[:, t, :], lbrow, ALU.add), E13["out"])

                for t in range(NT):
                    for n in range(2):
                        xs = x3[:, t, n * 512:(n + 1) * 512]
                        dve.wait_ge(E13["y"], 2 * t + n + 1)
                        v(nc.vector.scalar_tensor_tensor(xs, xs, ALPHA, PS[2 * t + n][:, :], ALU.mult, ALU.add), E13["x"] if n else None)
                    dve.wait_ge(E13["sum"], t + 1)
                    v(nc.vector.tensor_scalar(stat[:, 8 * t + 1:8 * t + 2], stat[:, 8 * t:8 * t + 1], -1.0 / D, None, ALU.mult), E13["nm"])
                    if t:
                        finish(t - 1)
                finish(NT - 1)


def kernel(**inputs):
    import concourse.bacc as bacc
    from concourse.bass_utils import run_bass_kernel_spmd

    nc = bacc.Bacc("TRN2", target_bir_lowering=False, num_devices=1)
    arrays = {name: np.ascontiguousarray(a) for name, a in inputs.items()}
    arrays["table"] = shape_table()
    io = {name: nc.dram_tensor(name, a.shape, mybir.dt.from_np(a.dtype), kind="ExternalInput").ap()
          for name, a in arrays.items()}
    io["scratch"] = nc.dram_tensor("scratch", [4, P * REL], F32, kind="Internal").ap()
    io["out"] = nc.dram_tensor("y", [1, S, D], F32, kind="ExternalOutput").ap()
    build(nc, io)
    result = run_bass_kernel_spmd(nc, [arrays], core_ids=[0])
    return result.results[0]["y"]
```

```python
import math
from contextlib import ExitStack

import numpy as np
import concourse.bass as bass
from concourse import mybir

F32 = mybir.dt.float32
ALU = mybir.AluOpType
ACT = mybir.ActivationFunctionType
AX = mybir.AxisListType.X

P = 128
S = 512
NT = S // P
D = 1024
KD = D // P
HEADS = 8
EPS = 1e-6
LAMBDA_INIT = 0.8 - 0.6 * math.exp(0.0)
CONV_K = 5
NE = 16
FF = 2048
CAP = 2 * S // NE
SLAB = 4096
QA, KA, VA, QKVG, ZG, AB = 0, 1024, 2048, 3072, 6144, 7168
GATE_A, GATE_G = 7200, 8224
A_Q, A_CKV, A_IQ, A_IK, A_IW, A_GATE, B_Q, B_F, B_I, B_GATE = 0, 512, 640, 1152, 1216, 1224, 1736, 2248, 2760, 3272
LEVELS = [1, 2, 4, 8, 16, 32, 64]
NL = len(LEVELS)
TOPK = 128
BIG = 3.0e38
STRUCK = 3.2e38
ALPHA = 2.0 ** 0.25
REL = 640
T_ID, T_ONE, T_LE, T_GE, T_LOW = 0, 128, 256, 384, 512
T_UP = T_LOW + NL * P
T_IOTA = T_UP + NL * P
T_KEEP = T_IOTA + CAP
T_ROT = T_KEEP
T_COS = T_ROT + P
T_SIN = T_COS + S
T_BUCKET = T_SIN + S
T_ALL = T_BUCKET + REL


def shape_table():
    i, j = np.arange(P)[:, None], np.arange(P)[None, :]
    t = np.zeros((P, T_ALL), np.float32)
    t[:, T_ID:T_ID + P] = i == j
    t[:, T_ONE:T_ONE + P] = 1.0
    t[:, T_LE:T_LE + P] = i <= j
    t[:, T_GE:T_GE + P] = i >= j
    for n, s in enumerate(LEVELS):
        low = (i // (2 * s) == j // (2 * s)) & (i % (2 * s) >= s) & (j % (2 * s) < s)
        t[:, T_LOW + n * P:T_LOW + (n + 1) * P] = low
        t[:, T_UP + n * P:T_UP + (n + 1) * P] = low.T
    t[:, T_IOTA:T_IOTA + CAP] = np.arange(1, CAP + 1)
    rot = np.zeros((P, P), np.float32)
    for b in (0, 64):
        for m in range(32):
            rot[b + m + 32, b + m] = -1.0
            rot[b + m, b + m + 32] = 1.0
    t[:, T_ROT:T_ROT + P] = rot
    inv = np.float32(10000.0) ** (-np.arange(0, 64, 2, dtype=np.float32) / np.float32(64))
    ang = np.arange(S, dtype=np.float32)[None, :] * inv[np.arange(P) % 32][:, None]
    t[:, T_COS:T_COS + S] = np.cos(ang)
    t[:, T_SIN:T_SIN + S] = np.sin(ang)
    rel = np.arange(REL) - 511
    n = np.abs(rel)
    nf = np.maximum(n, 1).astype(np.float32)
    large = 8 + (np.log(nf / np.float32(8)) / np.float32(math.log(256 / 8)) * np.float32(8)).astype(np.int32)
    bucket = np.where(rel > 0, 16, 0) + np.where(n < 8, n, np.minimum(large, 15))
    for u in range(REL):
        t[bucket[u], T_BUCKET + u] = 1.0
    return t


LN_SUB, LN_DK, LN_EPS = 1, 2, 3
BIASES = (EPS, math.log(1.0 - LAMBDA_INIT), -0.5 * math.log(P), 1e-5)


class Chain:

    def __init__(self, eng, own, counts):
        self.eng, self.own, self.counts = eng, own, counts

    def __call__(self, ins, sem=None, last=True):
        sem = self.own if sem is None else sem
        ins.then_inc(sem, 1)
        key = id(sem)
        self.counts[key] = self.counts.get(key, 0) + 1
        if last:
            self.eng.wait_ge(sem, self.counts[key])


def build(nc, io):
    ctx = ExitStack()
    counts = {}
    with ctx:
        def sb(name, cols):
            return ctx.enter_context(nc.sbuf_tensor(name, [P, cols], F32))

        spent, cleared = [], []

        def sem(name):
            return cleared.pop(0) if cleared else ctx.enter_context(nc.semaphore(name))

        def clear_spent():
            with nc.Block() as block:
                @block.gpsimd
                def _(pool):
                    for s_ in spent:
                        pool.sem_clear(s_)
            for s_ in spent:
                counts.pop(id(s_), None)
            cleared.extend(spent)
            spent.clear()

        tab = sb("tab", T_KEEP)
        ident, ones = tab[:, T_ID:T_ID + P], tab[:, T_ONE:T_ONE + P]
        tri_le, tri_ge = tab[:, T_LE:T_LE + P], tab[:, T_GE:T_GE + P]
        low = [tab[:, T_LOW + n * P:T_LOW + (n + 1) * P] for n in range(NL)]
        up = [tab[:, T_UP + n * P:T_UP + (n + 1) * P] for n in range(NL)]
        iota = tab[:, T_IOTA:T_IOTA + CAP]
        X = sb("X", NT * D)
        HT = sb("HT", KD * S)
        SL = [sb(f"SL{i}", SLAB) for i in range(4)]
        R12 = sb("R12", 2 * SLAB)
        R = [None, R12[:, 0:SLAB], R12[:, SLAB:2 * SLAB]] + [sb(f"R{i}", SLAB) for i in range(3, 7)]
        wab_ = sb("wab", KD * 32)
        small = sb("small", 1100)
        x3 = X[:, :].rearrange("p (t d) -> p t d", t=NT)
        hT = HT[:, :].rearrange("p (k s) -> p k s", k=KD)
        at = [0]

        def take(n):
            at[0] += n
            assert at[0] <= 1100
            return small[:, at[0] - n:at[0]]

        convw = take(120)
        vcols = take(30)
        norm1c, sublnc, gdnc = vcols[:, 0:8], vcols[:, 16:17], vcols[:, 17:18]
        lbc, hgc = vcols[:, 18:26], vcols[:, 26:30]
        lam = take(4)
        stat = take(32)
        al = take(32)
        gg = take(64)
        beta = take(64)
        eG = take(64)
        G = take(64)
        nbeG = take(64)
        decs = take(64)
        gl = take(64)
        sa = take(64)
        sb_ = take(64)
        bias = take(len(BIASES))
        stat128 = take(128)
        aff = beta
        PS = [ctx.enter_context(nc.psum_tensor(f"PS{i}", [P, 512], F32)) for i in range(8)]

        dve_link, act_link, pool_link = sem("dve_link"), sem("act_link"), sem("pool_link")

        def V():
            return Chain(nc.vector, dve_link, counts)

        def A():
            return Chain(nc.scalar, act_link, counts)

        def G_():
            return Chain(nc.gpsimd, pool_link, counts)

        def bc(ap, n):
            return ap.unsqueeze(2).to_broadcast([P, ap.shape[1], n])

        def rsqrt(a, out, sums, scale, done, factor=0, eps=0):
            a(nc.scalar.activation(out, sums, ACT.Ln, scale=scale, bias=bias[:, eps:eps + 1]))
            a(nc.scalar.activation(out, out, ACT.Exp, scale=-0.5, bias=bias[:, factor:factor + 1] if factor else 0.0), done)

        slab_in = [sem(f"slab_in{i}") for i in range(8)]
        slab_n = [0] * 8
        SLB = SL + R[1:5]

        def load_slab(eng, slot, src, cols):
            k = src.shape[0] // P
            dst = SLB[slot][:, 0:k * cols].rearrange("p (k n) -> p k n", k=k)
            eng.dma_start(dst, src.rearrange("(k p) n -> p k n", p=P)).then_inc(slab_in[slot], 16)
            slab_n[slot] += 16
            return slab_in[slot], slab_n[slot]

        def slab(slot, k=KD, cols=512):
            return SLB[slot][:, 0:k * cols].rearrange("p (k n) -> p k n", k=k)

        tab_in, rot_in, rows_in, x_in, bc_in = sem("tab_in"), sem("rot_in"), sem("rows_in"), sem("x_in"), sem("bc_in")
        tile_in = [sem(f"tile_in{t}") for t in range(NT)]
        vec_t, h_ready, hT_done, hT_evac = sem("vec_t"), sem("h_ready"), sem("hT_done"), sem("hT_evac")
        bias_ready, rstd_ready = sem("bias_ready"), sem("rstd_ready")
        h_scaled, lam_dot = sem("h_scaled"), sem("lam_dot")
        rows = R[6]
        lamrow = R[6][:, 256:512].rearrange("p (a d) -> p a d", a=4)
        hn = R[1][:, :].rearrange("p (t d) -> p t d", t=NT)
        w_in = io["w_in"][0]
        with nc.Block() as block:
            @block.sync
            def _(sp):
                for t in range(NT):
                    sp.dma_start(x3[:, t, :], io["x"][0, t * P:(t + 1) * P, :]).then_inc(tile_in[t], 16)
                sp.dma_start(tab[:, :], io["table"][:, 0:T_KEEP]).then_inc(tab_in, 16)
                for g in range(4):
                    load_slab(sp, g, w_in[:, g * 512:(g + 1) * 512], 512)
                    if g == 0:
                        sp.dma_start(R[5][:, 0:P + 2 * S], io["table"][:, T_ROT:T_BUCKET]).then_inc(rot_in, 16)

            @block.scalar
            def _(act):
                a = A()
                conv_rows = io["conv_w"][0].rearrange("t (c p) -> (t c) p", p=P)
                act.dma_start(rows[0:120, 0:P], conv_rows).then_inc(rows_in, 16)
                at_row = 0
                for name, n in (("norm1_w", 8), ("norm2_w", 8), ("subln_w", 1), ("gdn_norm_w", 1),
                                ("lb_logits_2", 8), ("hgrn_norm_g_2", 4)):
                    src = io[name]
                    src = src.rearrange("l (k p) -> (l k) p", p=P)
                    act.dma_start(rows[at_row:at_row + n, P:2 * P], src).then_inc(rows_in, 16)
                    at_row += n
                for i, name in enumerate(("lambda_q1", "lambda_k1", "lambda_q2", "lambda_k2")):
                    act.dma_start(lamrow[:, i, :], io[name].to_broadcast([P, 64])).then_inc(bc_in, 16)
                for i, name in enumerate(("a_log_fwd", "a_log_bwd", "dt_bias_fwd", "dt_bias_bwd")):
                    act.dma_start(al[:, 8 * i:8 * i + 8], io[name].to_broadcast([P, 8])).then_inc(bc_in, 16)
                for t in range(NT):
                    act.wait_ge(tile_in[t], 16)
                    a(nc.scalar.activation(hn[:, t, :], x3[:, t, :], ACT.Square, accum_out=stat[:, t:t + 1]),
                      h_ready)
                act.wait_ge(bias_ready, len(BIASES))
                rsqrt(a, stat[:, 8:12], stat[:, 0:4], 1.0 / D, rstd_ready)
                act.wait_ge(lam_dot, 2)
                a(nc.scalar.activation(lam[:, 2:4], lam[:, 0:2], ACT.Exp))
                act.wait_ge(vec_t, 1)
                a(nc.scalar.activation(convw, PS[6][:, 0:120], ACT.Copy))
                a(nc.scalar.activation(vcols, PS[7][:, 0:30], ACT.Copy))
                for k in range(KD):
                    act.wait_ge(hT_done, k + 1)
                    a(nc.scalar.activation(hT[:, k, :], PS[k % 4][:, :], ACT.Copy, scale=norm1c[:, k:k + 1]),
                      hT_evac)

            @block.gpsimd
            def _(pool):
                g = G_()
                for i, c in enumerate(BIASES):
                    g(nc.gpsimd.memset(bias[:, i:i + 1], c), bias_ready)

            @block.vector
            def _(dve):
                v = V()
                dve.wait_ge(rstd_ready, 1)
                for t in range(NT):
                    v(nc.vector.tensor_scalar(hn[:, t, :], x3[:, t, :], stat[:, 8 + t:9 + t], None, ALU.mult),
                      h_scaled)
                dve.wait_ge(bc_in, 16 * 8)
                for i in range(2):
                    v(nc.vector.tensor_tensor(lamrow[:, 2 * i, :], lamrow[:, 2 * i, :], lamrow[:, 2 * i + 1, :], ALU.mult))
                    v(nc.vector.reduce_sum(lam[:, i:i + 1], lamrow[:, 2 * i, :], AX), lam_dot)

            @block.tensor
            def _(pe):
                pe.wait_ge(tab_in, 16)
                pe.wait_ge(rows_in, 16 * 7)
                pe.transpose(PS[6][:, 0:120], rows[0:120, 0:P], ident[0:120, 0:120])
                pe.transpose(PS[7][:, 0:30], rows[0:30, P:2 * P], ident[0:30, 0:30]).then_inc(vec_t, 1)
                pe.wait_ge(h_scaled, NT)
                for k in range(KD):
                    if k >= 4:
                        pe.wait_ge(hT_evac, k - 3)
                    for t in range(NT):
                        m = pe.transpose(PS[k % 4][:, t * P:(t + 1) * P], hn[:, t, k * P:(k + 1) * P], ident)
                    m.then_inc(hT_done, 1)

        qz = [R[1][:, :].rearrange("p (h s) -> p h s", h=HEADS), R[2][:, :].rearrange("p (h s) -> p h s", h=HEADS)]
        kT = R[3][:, :].rearrange("p (h s) -> p h s", h=HEADS)
        va = R[4][:, :].rearrange("p (t d) -> p t d", t=NT)
        rot_m, cosT, sinT = R[5][:, 0:P], R[5][:, P:P + S], R[5][:, P + S:P + 2 * S]
        raw = [R[5][:, 1152 + i * S:1152 + (i + 1) * S] for i in range(2)]
        t1, t2 = R[5][:, 2176:2688], R[5][:, 2688:3200]
        proj_done, raw_ready, rot_done, rope_done, slab_used, va_evac = (
            sem("proj_done"), sem("raw_ready"), sem("rot_done"), sem("rope_done"), sem("slab_used"), sem("va_evac"))
        pad_zero = sem("pad_zero")
        NQK = 2 * HEADS
        with nc.Block() as block:
            @block.sync
            def _(sp):
                for g in range(4, 6):
                    sp.wait_ge(slab_used, g - 3)
                    load_slab(sp, g % 4, w_in[:, g * 512:(g + 1) * 512], 512)

            @block.tensor
            def _(pe):
                def rotate(u):
                    if u == 0:
                        pe.wait_ge(rot_in, 16)
                    pe.wait_ge(raw_ready, u + 1)
                    if u >= 2:
                        pe.wait_ge(rope_done, u - 1)
                    pe.matmul(PS[4 + u % 2][:, :], rot_m, raw[u % 2], start=True, stop=True).then_inc(rot_done, 1)

                for u in range(NQK):
                    g, j = u // 4, u % 4
                    pe.wait_ge(slab_in[g % 4], 16 * (g // 4 + 1))
                    if u >= 4:
                        pe.wait_ge(raw_ready, u - 3)
                    for k in range(KD):
                        m = pe.matmul(PS[u % 4][:, :], slab(g % 4)[:, k, j * P:(j + 1) * P], hT[:, k, :],
                                      start=(k == 0), stop=(k == KD - 1))
                    m.then_inc(proj_done, 1)
                    if u >= 1:
                        rotate(u - 1)
                    if j == 3:
                        pe.wait_ge(rot_done, u)
                        pe.sem_inc(slab_used, 1)
                rotate(NQK - 1)
                for n in range(2):
                    pe.wait_ge(slab_in[n], 32)
                    for t in range(NT):
                        u = NT * n + t
                        b = u % 4
                        if u >= 4:
                            pe.wait_ge(va_evac, u - 3)
                        else:
                            pe.wait_ge(raw_ready, NQK)
                        for k in range(KD):
                            m = pe.matmul(PS[b][:, :], hT[:, k, t * P:(t + 1) * P], slab(n)[:, k, :],
                                          start=(k == 0), stop=(k == KD - 1))
                        m.then_inc(proj_done, 1)

            @block.scalar
            def _(act):
                a = A()
                for u in range(NQK):
                    act.wait_ge(proj_done, u + 1)
                    if u >= 2:
                        act.wait_ge(rope_done, u - 1)
                    a(nc.scalar.activation(raw[u % 2], PS[u % 4][:, :], ACT.Copy), raw_ready)
                for u in range(8):
                    n, t = u // NT, u % NT
                    act.wait_ge(proj_done, NQK + u + 1)
                    a(nc.scalar.activation(va[:, t, n * 512:(n + 1) * 512], PS[u % 4][:, :], ACT.Copy), va_evac)

            @block.gpsimd
            def _(pool):
                g = G_()
                g(nc.gpsimd.memset(R[1][64:128, :], 0.0), pad_zero)
                g(nc.gpsimd.memset(R[2][0:64, :], 0.0), pad_zero)

            @block.vector
            def _(dve):
                v = V()
                v(nc.vector.tensor_tensor(lam[:, 0:1], lam[:, 2:3], lam[:, 3:4], ALU.subtract))
                v(nc.vector.tensor_scalar(lam[:, 0:1], lam[:, 0:1], LAMBDA_INIT, None, ALU.add))
                dve.wait_ge(rot_in, 16)
                for u in range(NQK):
                    dve.wait_ge(raw_ready, u + 1)
                    v(nc.vector.tensor_tensor(t1, raw[u % 2], cosT, ALU.mult))
                    dve.wait_ge(rot_done, u + 1)
                    v(nc.vector.tensor_tensor(t2, PS[4 + u % 2][:, :], sinT, ALU.mult))
                    if u < HEADS:
                        v(nc.vector.tensor_tensor(qz[0][0:64, u, :], t1[0:64, :], t2[0:64, :], ALU.add))
                        v(nc.vector.tensor_tensor(qz[1][64:128, u, :], t1[64:128, :], t2[64:128, :], ALU.add),
                          rope_done)
                    else:
                        v(nc.vector.tensor_tensor(kT[:, u - HEADS, :], t1, t2, ALU.add), rope_done)
        oaT = R[5][:, :].rearrange("p (h s) -> p h s", h=HEADS)
        r6 = R[6]
        NB = 3
        p0 = [r6[:, i * 512:(i + 1) * 512] for i in range(NB)]
        p1 = [r6[:, (NB + i) * 512:(NB + i + 1) * 512] for i in range(NB)]
        pT = [r6[:, 3072:3584].rearrange("p (c q) -> p c q", c=NT), r6[:, 3584:4096].rearrange("p (c q) -> p c q", c=NT)]
        score_done, max_ready, exp_done, pd_ready, pT_done, pT_ready, pv_done, oT_evac = (
            sem("score_done"), sem("max_ready"), sem("exp_done"), sem("pd_ready"), sem("pT_done"),
            sem("pT_ready"), sem("pv_done"), sem("oT_evac"))
        rstd2 = sem("rstd2")
        sq_ready, ss_done, norm_done = sem("sq_ready"), sem("ss_done"), sem("norm_done")
        NU = HEADS * NT
        with nc.Block() as block:
            @block.tensor
            def _(pe):
                def scores(n):
                    h, t = n // NT, n % NT
                    if n >= 2:
                        pe.wait_ge(exp_done, n - 1)
                    for m_ in range(2):
                        m = pe.matmul(PS[2 * (n % 2) + m_][:, :], qz[m_][:, h, t * P:(t + 1) * P], kT[:, h, :],
                                      start=True, stop=True)
                    m.then_inc(score_done, 1)

                def turn(n):
                    pe.wait_ge(pd_ready, n + 1)
                    if n >= 2:
                        pe.wait_ge(pT_ready, n - 1)
                    for c in range(NT):
                        m = pe.transpose(PS[4 + n % 2][:, c * P:(c + 1) * P], p0[n % NB][:, c * P:(c + 1) * P], ident)
                    m.then_inc(pT_done, 1)

                def pv(n):
                    h, t = n // NT, n % NT
                    pe.wait_ge(pT_ready, n + 1)
                    if t == 0 and h >= 2:
                        pe.wait_ge(oT_evac, h - 1)
                    for c in range(NT):
                        m = pe.matmul(PS[6 + h % 2][:, t * P:(t + 1) * P], va[:, c, h * P:(h + 1) * P], pT[n % 2][:, c, :],
                                      start=(c == 0), stop=(c == NT - 1))
                    m.then_inc(pv_done, 1)

                for n in range(NU + 3):
                    if n < NU:
                        scores(n)
                    if 2 <= n <= NU + 1:
                        turn(n - 2)
                    if n >= 3:
                        pv(n - 3)
                for h in range(HEADS):
                    pe.wait_ge(sq_ready, h + 1)
                    if h >= 2:
                        pe.wait_ge(rstd2, h - 1)
                    pe.matmul(PS[h % 2][:, :], ones, p0[h % 2], start=True, stop=True).then_inc(ss_done, 1)

            @block.scalar
            def _(act):
                a = A()

                def evac(n):
                    act.wait_ge(pT_done, n + 1)
                    if n >= 2:
                        act.wait_ge(pv_done, n - 1)
                    a(nc.scalar.activation(pT[n % 2].rearrange("p c q -> p (c q)"), PS[4 + n % 2][:, :], ACT.Copy), pT_ready)

                for n in range(NU):
                    act.wait_ge(max_ready, n + 1)
                    if n >= NB:
                        act.wait_ge(pT_done, n - NB + 1)
                    s = stat[:, 8 * (n % NB):8 * (n % NB) + 8]
                    for m_, p in ((0, p0), (1, p1)):
                        ins = nc.scalar.activation(p[n % NB], PS[2 * (n % 2) + m_][:, :], ACT.Exp, scale=0.125,
                                                   bias=s[:, 2 + m_:3 + m_], accum_out=s[:, 4 + m_:5 + m_])
                        a(ins, exp_done if m_ else None)
                    if n >= 2:
                        evac(n - 2)
                evac(NU - 2)
                evac(NU - 1)

                def norm(h):
                    act.wait_ge(ss_done, h + 1)
                    if h >= 2:
                        act.wait_ge(norm_done, h - 1)
                    rsqrt(a, p1[h % 2], PS[h % 2][:, :], 1.0 / P, rstd2, LN_SUB)

                for h in range(HEADS):
                    act.wait_ge(oT_evac, h + 1)
                    if h >= 2:
                        act.wait_ge(ss_done, h - 1)
                    a(nc.scalar.activation(p0[h % 2], oaT[:, h, :], ACT.Square), sq_ready)
                    if h >= 1:
                        norm(h - 1)
                norm(HEADS - 1)

            @block.vector
            def _(dve):
                v = V()

                def maxes(n):
                    s = stat[:, 8 * (n % NB):8 * (n % NB) + 8]
                    dve.wait_ge(score_done, n + 1)
                    for m_ in range(2):
                        v(nc.vector.reduce_max(s[:, m_:m_ + 1], PS[2 * (n % 2) + m_][:, :], AX))
                    v(nc.vector.tensor_scalar(s[:, 2:4], s[:, 0:2], -0.125, None, ALU.mult), max_ready)

                def out(h):
                    dve.wait_ge(pv_done, NT * h + NT)
                    v(nc.vector.tensor_copy(oaT[:, h, :], PS[6 + h % 2][:, :]), oT_evac)

                maxes(0)
                for n in range(NU):
                    if n + 1 < NU:
                        maxes(n + 1)
                    s = stat[:, 8 * (n % NB):8 * (n % NB) + 8]
                    dve.wait_ge(exp_done, n + 1)
                    v(nc.vector.reciprocal(s[:, 4:6], s[:, 4:6]))
                    v(nc.vector.tensor_tensor(s[:, 6:7], s[:, 5:6], lam[:, 0:1], ALU.mult))
                    v(nc.vector.tensor_scalar(p1[n % NB], p1[n % NB], s[:, 6:7], None, ALU.mult))
                    v(nc.vector.scalar_tensor_tensor(p0[n % NB], p0[n % NB], s[:, 4:5], p1[n % NB], ALU.mult, ALU.subtract),
                      pd_ready)
                    if n >= 7 and (n - 7) % NT == 0:
                        out((n - 7) // NT)
                out(HEADS - 1)
                for h in range(HEADS):
                    dve.wait_ge(rstd2, h + 1)
                    o = oaT[:, h, :]
                    v(nc.vector.scalar_tensor_tensor(o, o, sublnc, p1[h % 2], ALU.mult, ALU.mult), norm_done)
        gq = R[1][:, :].rearrange("p (h s) -> p h s", h=HEADS)
        gk = R[2][:, :].rearrange("p (h s) -> p h s", h=HEADS)
        gv = R[3][:, :].rearrange("p (t h d) -> p t h d", t=NT, h=HEADS)
        gkt = R[4][:, :].rearrange("p (t h d) -> p t h d", t=NT, h=HEADS)
        zs = R[6][:, :].rearrange("p (h s) -> p h s", h=HEADS)
        wk = SL[3]
        PADW = 520
        padded = [wk[:, i * PADW:(i + 1) * PADW] for i in range(2)]
        conv = [wk[:, 1040 + i * S:1040 + (i + 1) * S] for i in range(3)]
        sq = [wk[:, 2576:3088], wk[:, 3088:3600]]
        wab = wab_[:, :].rearrange("p (k n) -> p k n", k=KD)
        pad_done, p3_done, raw3, conv_done, silu_done, sq3, ss3, rstd3, qk_norm, tr3, tr3_evac, slab3, wab_in, z_done, ab_done, slab3_free = [
            sem(n) for n in ("pad_done", "p3_done", "raw3", "conv_done", "silu_done", "sq3", "ss3", "rstd3", "qk_norm",
                             "tr3", "tr3_evac", "slab3", "wab_in", "z_done", "ab_done", "slab3_free")]
        ab_evac = sem("ab_evac")
        NC3 = 3 * HEADS
        with nc.Block() as block:
            start3 = list(slab_n)

            @block.sync
            def _(sp):
                for i in range(8):
                    g = 6 + i
                    if i >= 3:
                        sp.wait_ge(slab3_free, i - 2)
                    load_slab(sp, i % 3, w_in[:, g * 512:(g + 1) * 512], 512)
                    if i == 0:
                        sp.dma_start(wab, w_in[:, AB:AB + 32].rearrange("(k p) n -> p k n", p=P)).then_inc(wab_in, 16)

            @block.tensor
            def _(pe):
                tr = [0]

                def turn(u):
                    if u < 2 * HEADS:
                        pe.wait_ge(qk_norm, u + 1)
                        src = gk[:, u - HEADS, :]
                    else:
                        pe.wait_ge(silu_done, u + 1)
                        src = conv[u % 3]
                    if tr[0] >= 2:
                        pe.wait_ge(tr3_evac, tr[0] - 1)
                    for t in range(NT):
                        m = pe.transpose(PS[6 + tr[0] % 2][:, t * P:(t + 1) * P], src[:, t * P:(t + 1) * P], ident)
                    m.then_inc(tr3, 1)
                    tr[0] += 1

                for u in range(NC3 + 3):
                    if u < NC3:
                        i, j = u // 4, u % 4
                        pe.wait_ge(slab_in[i % 3], start3[i % 3] + 16 * (i // 3 + 1))
                        if u >= 4:
                            pe.wait_ge(raw3, u - 3)
                        for k in range(KD):
                            m = pe.matmul(PS[u % 4][:, :], slab(i % 3)[:, k, j * P:(j + 1) * P], hT[:, k, :],
                                          start=(k == 0), stop=(k == KD - 1))
                        m.then_inc(p3_done, 1)
                    if 1 <= u <= 2 * HEADS:
                        pe.wait_ge(sq3, u)
                        if u >= 3:
                            pe.wait_ge(rstd3, u - 2)
                        pe.matmul(PS[4 + (u - 1) % 2][:, :], ones, sq[(u - 1) % 2], start=True, stop=True).then_inc(ss3, 1)
                    if u < NC3 and u % 4 == 3:
                        pe.wait_ge(p3_done, u + 1)
                        pe.sem_inc(slab3_free, 1)
                    if HEADS + 2 <= u <= NC3 + 1:
                        turn(u - 2)
                for u in range(HEADS):
                    i, j = 6 + u // 4, u % 4
                    pe.wait_ge(slab_in[i % 3], start3[i % 3] + 16 * (i // 3 + 1))
                    if u >= 4:
                        pe.wait_ge(z_done, u - 3)
                    else:
                        pe.wait_ge(raw3, NC3)
                    for k in range(KD):
                        m = pe.matmul(PS[u % 4][:, :], slab(i % 3)[:, k, j * P:(j + 1) * P], hT[:, k, :],
                                      start=(k == 0), stop=(k == KD - 1))
                    m.then_inc(p3_done, 1)
                pe.wait_ge(wab_in, 16)
                pe.wait_ge(rstd3, 2 * HEADS)
                for t in range(NT):
                    for k in range(KD):
                        m = pe.matmul(PS[4][:, t * 32:(t + 1) * 32], hT[:, k, t * P:(t + 1) * P], wab[:, k, :],
                                      start=(k == 0), stop=(k == KD - 1))
                m.then_inc(ab_done, 1)

            @block.gpsimd
            def _(pool):
                g = G_()
                for i in range(2):
                    g(nc.gpsimd.memset(padded[i], 0.0), pad_done)

            @block.scalar
            def _(act):
                a = A()
                act.wait_ge(pad_done, 2)

                def norm(u):
                    act.wait_ge(ss3, u + 1)
                    rsqrt(a, sq[u % 2], PS[4 + u % 2][:, :], 1.0, rstd3, LN_DK if u < HEADS else 0)

                def evac_turned(n):
                    act.wait_ge(tr3, n + 1)
                    dst = (gkt if n < HEADS else gv)[:, :, n % HEADS, :]
                    a(nc.scalar.activation(dst, PS[6 + n % 2][:, :].rearrange("p (t d) -> p t d", t=NT), ACT.Copy), tr3_evac)

                n = 0
                for u in range(NC3 + 3):
                    if u < NC3:
                        act.wait_ge(p3_done, u + 1)
                        if u >= 2:
                            act.wait_ge(conv_done, u - 1)
                        a(nc.scalar.activation(padded[u % 2][:, 2:2 + S], PS[u % 4][:, :], ACT.Copy), raw3)
                    if 1 <= u <= 2 * HEADS:
                        norm(u - 1)
                    if HEADS + 3 <= u <= NC3 + 2:
                        evac_turned(n)
                        n += 1
                    if u < NC3:
                        act.wait_ge(conv_done, u + 1)
                        a(nc.scalar.activation(conv[u % 3], conv[u % 3], ACT.Silu), silu_done)
                        if u < 2 * HEADS:
                            if u >= 2:
                                act.wait_ge(qk_norm, u - 1)
                            a(nc.scalar.activation(sq[u % 2], conv[u % 3], ACT.Square), sq3)
                for u in range(HEADS):
                    act.wait_ge(p3_done, NC3 + u + 1)
                    a(nc.scalar.activation(zs[:, u, :], PS[u % 4][:, :], ACT.Silu), z_done)
                act.wait_ge(ab_done, 1)
                a(nc.scalar.activation(stat128, PS[4][:, 0:128], ACT.Copy), ab_evac)

            @block.vector
            def _(dve):
                v = V()
                for u in range(NC3 + 1):
                    if u < NC3:
                        dve.wait_ge(raw3, u + 1)
                        if u >= 3:
                            if u - 3 < 2 * HEADS:
                                dve.wait_ge(qk_norm, u - 2)
                            else:
                                dve.wait_ge(tr3, u - 3 - HEADS + 1)
                        c = conv[u % 3]
                        for j in range(CONV_K):
                            src = padded[u % 2][:, j:j + S]
                            w = convw[:, j * NC3 + u:j * NC3 + u + 1]
                            if j == 0:
                                v(nc.vector.tensor_scalar(c, src, w, None, ALU.mult))
                            else:
                                v(nc.vector.scalar_tensor_tensor(c, src, w, c, ALU.mult, ALU.add),
                                  conv_done if j == CONV_K - 1 else None)
                    if 1 <= u <= 2 * HEADS:
                        n = u - 1
                        dve.wait_ge(rstd3, n + 1)
                        dst = gq[:, n, :] if n < HEADS else gk[:, n - HEADS, :]
                        v(nc.vector.tensor_tensor(dst, conv[n % 3], sq[n % 2], ALU.mult), qk_norm)

        places = [reg[:, i * 512:(i + 1) * 512].rearrange("p (h n) -> p h n", h=4)
                  for reg in (SL[0], SL[1], SL[2], X) for i in range(8)]
        names = ("AT", "A", "X", "BT", "PM", "RR", "BV", "XT0", "XT1", "QK0", "QK1", "QD0", "QD1")
        bufs = [dict(zip(names, places[d * len(names):])) for d in range(2)]
        St = X[:, 2048:4096].rearrange("p (a d) -> p a d", a=2 * HEADS)
        OG = SL[3][:, :]
        ogT = OG.rearrange("p (h s) -> p h s", h=HEADS)
        ab3 = stat128.rearrange("p (t n) -> p t n", t=NT)
        v16 = lambda ap: ap.rearrange("p (t n) -> p t n", t=NT)
        names = ("u_ready", "sp_ready", "g_ready", "cum_done", "G_ready", "pre_ready", "st_zero", "gram_done", "diff_ready", "dec_ready",
                 "decm_ready", "A_ready", "at_done", "AT_ready", "X_ready", "XT_ready", "XT0_ready", "BT_ready", "P_done", "P_ready",
                 "XX_done", "ks_done", "bv_ready", "rr_ready", "vn_done", "vn_ready", "vs_ready", "o_done", "s_done",
                 "o_ready", "S_ready", "sq4", "ss4", "rstd4", "og_ready")
        E4 = {n: sem("d_" + n) for n in names}
        PAIRS = [(s, hg) for s in range(NT) for hg in range(2)]

        def all4(ap):
            return ap.unsqueeze(1).to_broadcast([P, 4, P])

        def cols4(ap, c, d, hg):
            n = c * 16 + d * 8 + hg * 4
            return bc(ap[:, n:n + 4], P)

        def chunk(s, d):
            return s if d == 0 else NT - 1 - s

        def each(n):
            s, hg = PAIRS[n]
            for d in range(2):
                B = bufs[d]
                yield 2 * n + d, d, chunk(s, d), [hg * 4 + i for i in range(4)], B, {k: B[k + str(n % 2)] for k in ("XT", "QK", "QD")}

        def flat(ap):
            return ap.rearrange("p h n -> p (h n)")

        def bank(d, i):
            return PS[4 * d + i]

        def part(ps, i):
            return ps[:, i * P:(i + 1) * P]

        sq4 = [SL[0][:, 0:512], SL[0][:, 512:1024]]
        rs4 = [SL[0][:, 1024:1536], SL[0][:, 1536:2048]]
        with nc.Block() as block:
            @block.tensor
            def _(pe):
                pe.wait_ge(E4["g_ready"], 1)
                for d in range(2):
                    pe.matmul(v16(PS[0][:, 0:64])[:, :, 8 * d:8 * d + 8], (tri_le, tri_ge)[d],
                              v16(gg)[:, :, 8 * d:8 * d + 8], start=True, stop=True)
                pe.matmul(PS[1][:, 0:64], ones, gg, start=True, stop=True).then_inc(E4["cum_done"], 1)
                pe.wait_ge(E4["pre_ready"], 1)
                pe.wait_ge(E4["st_zero"], 1)

                def gram(n):
                    for q, d, c, heads, B, W in each(n):
                        cs = slice(c * P, (c + 1) * P)
                        if n:
                            pe.wait_ge(E4["XT_ready"], (n - 1) * 2 * (NL - 1) + 2 * (NL - 2) + d + 1)
                        for i, h in enumerate(heads):
                            col = c * 16 + d * 8 + h
                            pe.matmul(part(bank(d, 0), i), gg[:, col:col + 1].to_broadcast([P, P]),
                                      (tri_le, tri_ge)[d], start=True, stop=True)
                        for i, h in enumerate(heads):
                            pe.matmul(part(bank(d, 1), i), gk[:, h, cs], gk[:, h, cs], start=True, stop=True)
                        for i, h in enumerate(heads):
                            m = pe.matmul(part(bank(d, 2), i), gk[:, h, cs], gq[:, h, cs], start=True, stop=True)
                        m.then_inc(E4["gram_done"], 1)

                def turn_A(n):
                    for q, d, c, heads, B, W in each(n):
                        pe.wait_ge(E4["A_ready"], q + 1)
                        for i in range(4):
                            m = pe.transpose(part(bank(d, 1), i), B["A"][:, i, :], ident)
                        m.then_inc(E4["at_done"], 1)

                def level_P(n, l):
                    for q, d, c, heads, B, W in each(n):
                        pe.wait_ge(E4["BT_ready"], (n * (NL - 1) + l - 1) * 2 + d + 1)
                        pe.wait_ge(E4["X_ready"], n * 2 * (NL - 1) + 2 * (l - 1) + d + 1)
                        for i in range(4):
                            m = pe.matmul(part(bank(d, 0), i), B["BT"][:, i, :], B["X"][:, i, :], start=True, stop=True)
                        m.then_inc(E4["P_done"], 1)

                def level_X(n, l):
                    for q, d, c, heads, B, W in each(n):
                        pe.wait_ge(E4["P_ready"], (n * (NL - 1) + l - 1) * 2 + d + 1)
                        if l == 1:
                            pe.wait_ge(E4["XT0_ready"], q + 1)
                        else:
                            pe.wait_ge(E4["XT_ready"], n * 2 * (NL - 1) + 2 * (l - 2) + d + 1)
                        for i in range(4):
                            if l < NL - 1:
                                pe.matmul(part(bank(d, 1), i), W["XT"][:, i, :], B["PM"][:, i, :], start=True, stop=True)
                        for i in range(4):
                            m = pe.matmul(part(bank(d, 2), i), B["PM"][:, i, :], W["XT"][:, i, :], start=True, stop=True)
                        m.then_inc(E4["XX_done"], 1)

                def scan_ks(n):
                    for q, d, c, heads, B, W in each(n):
                        if n >= 1:
                            pe.wait_ge(E4["S_ready"], q - 1)
                        for i, h in enumerate(heads):
                            m = pe.matmul(part(bank(d, 3), i), gk[:, h, c * P:(c + 1) * P], St[:, d * 8 + h, :], start=True, stop=True)
                        m.then_inc(E4["ks_done"], 1)

                def scan_v(n):
                    for q, d, c, heads, B, W in each(n):
                        pe.wait_ge(E4["rr_ready"], q + 1)
                        for i in range(4):
                            m = pe.matmul(part(bank(d, 3), i), W["XT"][:, i, :], B["RR"][:, i, :], start=True, stop=True)
                        m.then_inc(E4["vn_done"], 1)

                def scan_o(n):
                    for q, d, c, heads, B, W in each(n):
                        pe.wait_ge(E4["vn_ready"], q + 1)
                        for i, h in enumerate(heads):
                            pe.matmul(part(bank(d, 3), i), B["RR"][:, i, :], W["QK"][:, i, :], start=True, stop=False)
                            m = pe.matmul(part(bank(d, 3), i), St[:, d * 8 + h, :], W["QD"][:, i, :], start=False, stop=True)
                        m.then_inc(E4["o_done"], 1)

                def scan_s(n):
                    for q, d, c, heads, B, W in each(n):
                        pe.wait_ge(E4["o_ready"], q + 1)
                        pe.wait_ge(E4["vs_ready"], q + 1)
                        for i, h in enumerate(heads):
                            m = pe.matmul(part(bank(d, 3), i), gkt[:, c, h, :], B["BV"][:, i, :], start=True, stop=True)
                        m.then_inc(E4["s_done"], 1)

                for n in range(len(PAIRS) + 1):
                    inv, scan = n < len(PAIRS), n >= 1
                    if inv:
                        gram(n)
                    if scan:
                        scan_ks(n - 1)
                    if inv:
                        turn_A(n)
                    if scan:
                        scan_v(n - 1)
                    if inv:
                        level_P(n, 1)
                    if scan:
                        scan_o(n - 1)
                    if inv:
                        level_X(n, 1)
                        level_P(n, 2)
                    if scan:
                        scan_s(n - 1)
                    if inv:
                        level_X(n, 2)
                        for l in range(3, NL):
                            level_P(n, l)
                            level_X(n, l)
                for h in range(HEADS):
                    pe.wait_ge(E4["sq4"], h + 1)
                    if h == 0:
                        pe.wait_ge(E4["S_ready"], 2 * len(PAIRS))
                    if h >= 2:
                        pe.wait_ge(E4["rstd4"], h - 1)
                    pe.matmul(PS[h % 2][:, :], ones, sq4[h % 2], start=True, stop=True).then_inc(E4["ss4"], 1)

            @block.scalar
            def _(act):
                a = A()
                act.wait_ge(E4["u_ready"], 1)
                a(nc.scalar.activation(sb_, sb_, ACT.Exp, scale=-1.0))
                a(nc.scalar.activation(sb_, sb_, ACT.Ln, bias=1.0))
                a(nc.scalar.activation(al[:, 0:16], al[:, 0:16], ACT.Exp))
                a(nc.scalar.activation(v16(beta), ab3[:, :, 16:32], ACT.Exp, scale=-1.0), E4["sp_ready"])
                act.wait_ge(E4["G_ready"], 1)
                a(nc.scalar.activation(eG, G, ACT.Exp))
                a(nc.scalar.activation(gl, PS[1][:, 0:64], ACT.Exp))
                a(nc.scalar.activation(decs, decs, ACT.Exp), E4["sp_ready"])
                def copy_out(wait, n, dst, src, done):
                    act.wait_ge(wait, n)
                    a(nc.scalar.activation(flat(dst), src[:, :], ACT.Copy), done)

                def evac_P(n, l):
                    for q, d, c, heads, B, W in each(n):
                        copy_out(E4["P_done"], (n * (NL - 1) + l - 1) * 2 + d + 1, B["PM"], bank(d, 0), E4["P_ready"])

                for n in range(len(PAIRS) + 1):
                    if n < len(PAIRS):
                        for q, d, c, heads, B, W in each(n):
                            act.wait_ge(E4["diff_ready"], q + 1)
                            a(nc.scalar.activation(B["A"], B["A"], ACT.Exp, scale=-1.0))
                            a(nc.scalar.activation(W["QK"], W["QK"], ACT.Exp))
                            a(nc.scalar.activation(flat(W["QD"]), bank(d, 0)[:, :], ACT.Exp), E4["dec_ready"])
                        for q, d, c, heads, B, W in each(n):
                            copy_out(E4["at_done"], q + 1, B["AT"], bank(d, 1), E4["AT_ready"])
                    if n:
                        for q, d, c, heads, B, W in each(n - 1):
                            copy_out(E4["vn_done"], q + 1, B["RR"], bank(d, 3), E4["vn_ready"])
                    if n < len(PAIRS):
                        for l in range(1, NL):
                            evac_P(n, l)

                def norm(h):
                    act.wait_ge(E4["ss4"], h + 1)
                    if h >= 2:
                        act.wait_ge(E4["og_ready"], h - 1)
                    rsqrt(a, rs4[h % 2], PS[h % 2][:, :], 1.0 / P, E4["rstd4"])

                act.wait_ge(E4["S_ready"], 2 * len(PAIRS))
                for h in range(HEADS):
                    if h >= 2:
                        act.wait_ge(E4["ss4"], h - 1)
                    a(nc.scalar.activation(sq4[h % 2], ogT[:, h, :], ACT.Square), E4["sq4"])
                    if h >= 1:
                        norm(h - 1)
                norm(HEADS - 1)

            @block.gpsimd
            def _(pool):
                g = G_()
                tt = nc.gpsimd.tensor_tensor
                g(nc.gpsimd.memset(St, 0.0), E4["st_zero"])
                pool.wait_ge(E4["pre_ready"], 1)
                for n in range(len(PAIRS) + 1):
                    if n:
                        for q, d, c, heads, B, W in each(n - 1):
                            if n >= 2:
                                pool.wait_ge(E4["s_done"], q - 1)
                            g(tt(B["BV"], gv[:, c, heads[0]:heads[0] + 4, :], cols4(beta, c, d, heads[0] // 4), ALU.mult), E4["bv_ready"])
                    if n < len(PAIRS):
                        for q, d, c, heads, B, W in each(n):
                            pool.wait_ge(E4["dec_ready"], q + 1)
                            g(tt(B["A"], B["A"], all4((tri_ge, tri_le)[d]), ALU.mult))
                            g(tt(B["A"], B["A"], cols4(beta, c, d, heads[0] // 4), ALU.mult))
                            g(tt(W["QK"], W["QK"], all4((tri_le, tri_ge)[d]), ALU.mult), E4["decm_ready"])
                            g(tt(W["QD"], W["QD"], gq[:, heads[0]:heads[0] + 4, c * P:(c + 1) * P], ALU.mult))
                        for q, d, c, heads, B, W in each(n):
                            pool.wait_ge(E4["AT_ready"], q + 1)
                            g(tt(B["BT"], B["AT"], all4((up, low)[d][1]), ALU.mult), E4["BT_ready"])
                            g(tt(W["XT"], B["AT"], all4((up, low)[d][0]), ALU.mult))
                            g(tt(W["XT"], all4(ident), W["XT"], ALU.subtract), E4["XT0_ready"])
                    if n:
                        for q, d, c, heads, B, W in each(n - 1):
                            pool.wait_ge(E4["vn_ready"], q + 1)
                            g(tt(B["BV"], B["RR"], cols4(decs, c, d, heads[0] // 4), ALU.mult), E4["vs_ready"])
                    if n < len(PAIRS):
                        for l in range(2, NL):
                            for q, d, c, heads, B, W in each(n):
                                pool.wait_ge(E4["P_done"], (n * (NL - 1) + l - 2) * 2 + d + 1)
                                g(tt(B["BT"], B["AT"], all4((up, low)[d][l]), ALU.mult), E4["BT_ready"])

            @block.vector
            def _(dve):
                v = V()
                tt = nc.vector.tensor_tensor
                f4 = lambda ap: ap.rearrange("p (h n) -> p h n", h=4)
                dtb = al[:, 16:32].unsqueeze(1).to_broadcast([P, NT, 16])
                v(tt(v16(sa), ab3[:, :, 0:16], dtb, ALU.add))
                v(nc.vector.tensor_scalar(sb_, sa, -1.0, None, ALU.mult))
                v(tt(sb_, sa, sb_, ALU.max), E4["u_ready"])
                dve.wait_ge(E4["sp_ready"], 1)
                v(nc.vector.scalar_tensor_tensor(sa, sa, 0.0, sb_, ALU.max, ALU.add))
                v(nc.vector.tensor_scalar(beta, beta, 1.0, None, ALU.add))
                v(nc.vector.reciprocal(beta, beta))
                v(nc.vector.scalar_tensor_tensor(v16(gg), v16(sa), -1.0, al[:, 0:16].unsqueeze(1).to_broadcast([P, NT, 16]),
                                                 ALU.mult, ALU.mult), E4["g_ready"])
                dve.wait_ge(E4["cum_done"], 1)
                v(nc.vector.tensor_copy(G, PS[0][:, 0:64]))
                v(tt(decs, PS[1][:, 0:64], G, ALU.subtract), E4["G_ready"])
                dve.wait_ge(E4["sp_ready"], 2)
                v(nc.vector.scalar_tensor_tensor(nbeG, eG, -1.0, beta, ALU.mult, ALU.mult), E4["pre_ready"])
                def level(n, l):
                    for q, d, c, heads, B, W in each(n):
                        dve.wait_ge(E4["XX_done"], (n * (NL - 1) + l - 1) * 2 + d + 1)
                        if l < NL - 1:
                            v(tt(B["X"], B["X"], f4(bank(d, 1)[:, :]), ALU.subtract), E4["X_ready"])
                        v(tt(W["XT"], W["XT"], f4(bank(d, 2)[:, :]), ALU.subtract), E4["XT_ready"])

                for n in range(len(PAIRS) + 1):
                    inv, scan = n < len(PAIRS), n >= 1
                    if inv:
                        for q, d, c, heads, B, W in each(n):
                            dve.wait_ge(E4["gram_done"], q + 1)
                            v(tt(B["A"], f4(bank(d, 0)[:, :]), cols4(G, c, d, heads[0] // 4), ALU.subtract))
                            v(nc.vector.tensor_scalar(W["QK"], B["A"], 0.0, None, ALU.min))
                            v(nc.vector.tensor_scalar(B["A"], B["A"], 0.0, None, ALU.max), E4["diff_ready"])
                    if scan:
                        for q, d, c, heads, B, W in each(n - 1):
                            dve.wait_ge(E4["ks_done"], q + 1)
                            v(tt(B["RR"], f4(bank(d, 3)[:, :]), cols4(nbeG, c, d, heads[0] // 4), ALU.mult))
                            dve.wait_ge(E4["bv_ready"], q + 1)
                            v(tt(B["RR"], B["RR"], B["BV"], ALU.add), E4["rr_ready"])
                    if inv:
                        for q, d, c, heads, B, W in each(n):
                            dve.wait_ge(E4["decm_ready"], q + 1)
                            v(tt(B["A"], f4(bank(d, 1)[:, :]), B["A"], ALU.mult), E4["A_ready"])
                            v(tt(W["QK"], f4(bank(d, 2)[:, :]), W["QK"], ALU.mult))
                            v(tt(B["X"], B["A"], all4((low, up)[d][0]), ALU.mult))
                            v(tt(B["X"], all4(ident), B["X"], ALU.subtract), E4["X_ready"])
                    if scan:
                        for q, d, c, heads, B, W in each(n - 1):
                            o = ogT[:, heads[0]:heads[0] + 4, c * P:(c + 1) * P]
                            dve.wait_ge(E4["o_done"], q + 1)
                            if PAIRS[n - 1][0] < NT // 2:
                                v(nc.vector.tensor_copy(o, f4(bank(d, 3)[:, :])), E4["o_ready"])
                            else:
                                v(tt(o, o, f4(bank(d, 3)[:, :]), ALU.add), E4["o_ready"])
                    if inv:
                        level(n, 1)
                    if scan:
                        for q, d, c, heads, B, W in each(n - 1):
                            dve.wait_ge(E4["s_done"], q + 1)
                            for i, h in enumerate(heads):
                                col = c * 16 + d * 8 + h
                                v(nc.vector.scalar_tensor_tensor(St[:, d * 8 + h, :], St[:, d * 8 + h, :], gl[:, col:col + 1],
                                                                 part(bank(d, 3), i), ALU.mult, ALU.add),
                                  E4["S_ready"] if i == 3 else None)
                    if inv:
                        for l in range(2, NL):
                            level(n, l)
                for h in range(HEADS):
                    dve.wait_ge(E4["rstd4"], h + 1)
                    v(nc.vector.scalar_tensor_tensor(ogT[:, h, :], ogT[:, h, :], gdnc, rs4[h % 2], ALU.mult, ALU.mult), E4["og_ready"])
                    v(tt(ogT[:, h, :], ogT[:, h, :], zs[:, h, :], ALU.mult))
        spent.extend([proj_done, raw_ready, rot_done, rope_done, slab_used, va_evac, pad_zero, score_done, max_ready,
                      exp_done, pd_ready, pT_done, pT_ready, pv_done, oT_evac, rstd2, sq_ready, ss_done, norm_done,
                      pad_done, p3_done, raw3, conv_done, silu_done, sq3, ss3, rstd3, qk_norm, tr3, tr3_evac, slab3,
                      wab_in, z_done, ab_done, slab3_free, ab_evac, *E4.values()])
        clear_spent()
        mT = R[6][:, :].rearrange("p (k s) -> p k s", k=KD)
        p5, gate5, merge5, m5, out5 = [sem(n) for n in ("p5", "gate5", "merge5", "m5", "out5")]
        wpa, wpg, wo = io["w_proj_attn"][0], io["w_proj_gdn"][0], io["w_out"][0]
        tm = [R[2][:, i * 512:(i + 1) * 512] for i in range(8)]
        w5 = []
        with nc.Block() as block:
            @block.sync
            def _(sp):
                halves = lambda src, n: src[:, n * 512:(n + 1) * 512]
                ga, gb = w_in[:, GATE_A:GATE_A + D], w_in[:, GATE_G:GATE_G + D]
                for slot, src in ((0, halves(wpa, 0)), (1, halves(ga, 0)), (2, halves(wpg, 0)), (4, halves(gb, 0)),
                                  (6, halves(wpa, 1)), (7, halves(ga, 1))):
                    w5.append((slot, load_slab(sp, slot, src, 512)))
                sp.dma_start(x3, io["x"][0].rearrange("(t p) d -> p t d", p=P)).then_inc(x_in, 16)
                sp.wait_ge(p5, 16)
                for slot, src in ((0, halves(wpg, 1)), (1, halves(gb, 1)), (2, halves(wo, 0)), (4, halves(wo, 1))):
                    w5.append((slot, load_slab(sp, slot, src, 512)))

            @block.tensor
            def _(pe):
                acts = (oaT, hT, ogT, hT)
                for j in range(KD):
                    ws = w5[0:4] if j < 4 else w5[4:8]
                    for i in range(4):
                        slot, (sm, val) = ws[i]
                        if j % 4 == 0:
                            pe.wait_ge(sm, val)
                        if j >= 2 and i == 0:
                            pe.wait_ge(merge5, j - 1)
                        for k in range(KD):
                            m = pe.matmul(PS[4 * (j % 2) + i][:, :], slab(slot)[:, k, (j % 4) * P:(j % 4 + 1) * P],
                                          acts[i][:, k, :], start=(k == 0), stop=(k == KD - 1))
                        m.then_inc(p5, 1)
                pe.wait_ge(merge5, KD)
                for n in range(2):
                    slot, (sm, val) = w5[8 + n]
                    pe.wait_ge(sm, val)
                    for t in range(NT):
                        u = n * NT + t
                        if u >= 4:
                            pe.wait_ge(out5, u - 3)
                        for k in range(KD):
                            m = pe.matmul(PS[u % 4][:, :], mT[:, k, t * P:(t + 1) * P], slab(slot)[:, k, :],
                                          start=(k == 0), stop=(k == KD - 1))
                        m.then_inc(m5, 1)

            @block.scalar
            def _(act):
                a = A()
                for j in range(KD):
                    for i in range(2):
                        act.wait_ge(p5, 4 * j + 2 * i + 2)
                        if j >= 2:
                            act.wait_ge(merge5, j - 1)
                        a(nc.scalar.activation(tm[2 * (j % 2) + i], PS[4 * (j % 2) + 2 * i + 1][:, :], ACT.Sigmoid), gate5)

            @block.vector
            def _(dve):
                v = V()
                tt = nc.vector.tensor_tensor
                for j in range(KD):
                    for i in range(2):
                        s_ = tm[2 * (j % 2) + i]
                        dve.wait_ge(gate5, 2 * j + i + 1)
                        v(tt(s_, s_, PS[4 * (j % 2) + 2 * i][:, :], ALU.mult))
                    v(tt(mT[:, j, :], tm[2 * (j % 2)], tm[2 * (j % 2) + 1], ALU.add), merge5)
                dve.wait_ge(x_in, 16)
                for u in range(2 * NT):
                    n, t = u // NT, u % NT
                    xs = x3[:, t, n * 512:(n + 1) * 512]
                    dve.wait_ge(m5, u + 1)
                    v(tt(xs, xs, PS[u % 4][:, :], ALU.add), out5)
        h2 = R[5][:, :].rearrange("p (t d) -> p t d", t=NT)
        Sel = R[6][:, :].rearrange("p (t n) -> p t n", t=NT)
        SelW = R[4][:, :].rearrange("p (t n) -> p t n", t=NT)
        n2row = R[4][:, 0:D]
        NPAIR = NE // 2
        XE = R12[:, :].rearrange("p (q k n) -> p q k n", q=NPAIR, k=KD)
        ST = HT[:, :].rearrange("p (q t n) -> p q t n", q=NPAIR, t=NT)
        affT, mx8 = SL[3][0:NE, 0:S], SL[3][0:NE, S:S + 8]
        wr = wab_[:, 0:KD * NE].rearrange("p (k e) -> p k e", k=KD)
        lg, msk, posm = sa, sb_, G
        lg3, aff3, msk3, posm3 = (ap.rearrange("p (t e) -> p t e", t=NT) for ap in (lg, aff, msk, posm))
        names = ("n2", "wr", "ss", "rstd", "h2", "t_done", "t_evac", "lg_done", "lgm", "exp", "aff", "affT", "affTc", "mask", "mT",
                 "mc", "pos", "sel", "selw", "xe", "xe_evac", "st", "st_evac")
        E6 = {n: sem("r_" + n) for n in names}
        w_gate, w_up, w_down = io["w_gate"][0], io["w_up"][0], io["w_down"][0]
        RING = [SL[0], SL[1], SL[2], SL[3], R[3], R[4]]
        NR = len(RING)
        PER = 12
        DOWN = (0, 2, 1, 3)
        ring_in = [sem(f"ring_in{i}") for i in range(NR)]

        def expert_slab(eng, r, x):
            x, part = x + r // PER, r % PER
            dst = RING[r % NR]
            if part < 8:
                w = (w_gate, w_up)[part % 4 // 2]
                f0 = part // 4 * 512 + part % 2 * 1024
                src = w[bass.ds(x, 1), :, f0:f0 + 512].rearrange("o (k p) n -> p (o k) n", p=P)
                dst = dst[:, :].rearrange("p (k n) -> p k n", k=KD)
            else:
                f0 = DOWN[part - 8] * 512
                src = w_down[bass.ds(x, 1), f0:f0 + 512, :].rearrange("o (k p) n -> p (o k) n", p=P)
                dst = dst[:, :].rearrange("p (k n) -> p k n", k=4)
            eng.dma_start(dst, src).then_inc(ring_in[r % NR], 16)

        with nc.Block() as block:
            @block.sync
            def _(sp):
                sp.dma_start(wr, io["w_router"][0].rearrange("(k p) e -> p k e", p=P)).then_inc(E6["wr"], 16)
                sp.dma_start(n2row, io["norm2_w"].to_broadcast([P, D])).then_inc(E6["n2"], 16)
                for r in range(3):
                    expert_slab(sp, r, 0)

            @block.scalar
            def _(act):
                a = A()
                for t in range(NT):
                    a(nc.scalar.activation(Sel[:, t, :], x3[:, t, :], ACT.Square, accum_out=stat[:, t:t + 1]))
                rsqrt(a, stat[:, 8:12], stat[:, 0:4], 1.0 / D, E6["rstd"])
                for k in range(KD):
                    act.wait_ge(E6["t_done"], k + 1)
                    a(nc.scalar.activation(hT[:, k, :], PS[k % 4][:, :], ACT.Copy), E6["t_evac"])
                act.wait_ge(E6["lgm"], 1)
                a(nc.scalar.activation(lg, lg, ACT.Exp), E6["exp"])
                act.wait_ge(E6["affT"], 1)
                a(nc.scalar.activation(affT, PS[5][0:NE, :], ACT.Copy), E6["affTc"])
                act.wait_ge(E6["mT"], 1)
                a(nc.scalar.activation(msk, PS[6][:, 0:64], ACT.Copy), E6["mc"])
                for u in range(2 * KD):
                    k, hf = u // 2, u % 2
                    act.wait_ge(E6["xe"], u + 1)
                    a(nc.scalar.activation(XE[:, 4 * hf:4 * hf + 4, k, :], PS[u % 4][:, :].rearrange("p (q n) -> p q n", q=4),
                                           ACT.Copy), E6["xe_evac"])

            @block.tensor
            def _(pe):
                pe.wait_ge(E6["h2"], NT)
                for k in range(KD):
                    if k >= 4:
                        pe.wait_ge(E6["t_evac"], k - 3)
                    for t in range(NT):
                        m = pe.transpose(PS[k % 4][:, t * P:(t + 1) * P], h2[:, t, k * P:(k + 1) * P], ident)
                    m.then_inc(E6["t_done"], 1)
                pe.wait_ge(E6["t_evac"], KD)
                pe.wait_ge(E6["wr"], 16)
                for t in range(NT):
                    for k in range(KD):
                        m = pe.matmul(PS[4][:, t * NE:(t + 1) * NE], hT[:, k, t * P:(t + 1) * P], wr[:, k, :],
                                      start=(k == 0), stop=(k == KD - 1))
                m.then_inc(E6["lg_done"], 1)
                pe.wait_ge(E6["aff"], 1)
                for t in range(NT):
                    m = pe.transpose(PS[5][0:NE, t * P:(t + 1) * P], aff3[:, t, :], ident)
                m.then_inc(E6["affT"], 1)
                pe.wait_ge(E6["mask"], 1)
                for t in range(NT):
                    m = pe.transpose(PS[6][:, t * NE:(t + 1) * NE], affT[:, t * P:(t + 1) * P], ident[0:NE, 0:NE])
                m.then_inc(E6["mT"], 1)
                pe.wait_ge(E6["mc"], 1)
                for t in range(NT):
                    for t_ in range(t + 1):
                        m = pe.matmul(PS[7][:, t * NE:(t + 1) * NE], tri_le if t_ == t else ones, msk3[:, t_, :],
                                      start=(t_ == 0), stop=(t_ == t))
                m.then_inc(E6["pos"], 1)
                pe.wait_ge(E6["sel"], NT)
                for u in range(2 * KD):
                    k, hf = u // 2, u % 2
                    if u >= 4:
                        pe.wait_ge(E6["xe_evac"], u - 3)
                    for t in range(NT):
                        m = pe.matmul(PS[u % 4][:, :], h2[:, t, k * P:(k + 1) * P], Sel[:, t, hf * 512:(hf + 1) * 512],
                                      start=(t == 0), stop=(t == NT - 1))
                    m.then_inc(E6["xe"], 1)
                pe.wait_ge(E6["selw"], NT)
                for q in range(NPAIR):
                    if q >= 4:
                        pe.wait_ge(E6["st_evac"], q - 3)
                    for t in range(NT):
                        m = pe.transpose(PS[4 + q % 4][:, t * P:(t + 1) * P], SelW[:, t, q * P:(q + 1) * P], ident)
                    m.then_inc(E6["st"], 1)

            @block.vector
            def _(dve):
                v = V()
                tt = nc.vector.tensor_tensor
                dve.wait_ge(E6["n2"], 16)
                dve.wait_ge(E6["rstd"], 1)
                for t in range(NT):
                    v(nc.vector.scalar_tensor_tensor(h2[:, t, :], x3[:, t, :], stat[:, 8 + t:9 + t], n2row, ALU.mult, ALU.mult), E6["h2"])
                dve.wait_ge(E6["lg_done"], 1)
                v(nc.vector.reduce_max(stat[:, 0:4], PS[4][:, 0:64].rearrange("p (t e) -> p t e", t=NT), AX))
                v(tt(lg3, PS[4][:, 0:64].rearrange("p (t e) -> p t e", t=NT), bc(stat[:, 0:4], NE), ALU.subtract), E6["lgm"])
                dve.wait_ge(E6["exp"], 1)
                v(nc.vector.reduce_sum(stat[:, 4:8], lg3, AX))
                v(nc.vector.reciprocal(stat[:, 4:8], stat[:, 4:8]))
                v(tt(aff3, lg3, bc(stat[:, 4:8], NE), ALU.mult), E6["aff"])
                dve.wait_ge(E6["affTc"], 1)
                for r in range(CAP // 8):
                    v(nc.vector.max(mx8, affT))
                    v(nc.vector.match_replace(affT, mx8, affT, -1.0))
                v(nc.vector.tensor_scalar(affT, affT, 0.0, None, ALU.is_lt), E6["mask"])
                dve.wait_ge(E6["pos"], 1)
                v(tt(posm, PS[7][:, 0:64], msk, ALU.mult))
                for t in range(NT):
                    v(tt(Sel[:, t, :].rearrange("p (e c) -> p e c", e=NE), iota.unsqueeze(1).to_broadcast([P, NE, CAP]),
                         bc(posm3[:, t, :], CAP), ALU.is_equal), E6["sel"])
                for t in range(NT):
                    v(tt(SelW[:, t, :].rearrange("p (e c) -> p e c", e=NE), Sel[:, t, :].rearrange("p (e c) -> p e c", e=NE),
                         bc(aff3[:, t, :], CAP), ALU.mult), E6["selw"])
                for q in range(NPAIR):
                    dve.wait_ge(E6["st"], q + 1)
                    v(nc.vector.tensor_copy(ST[:, q, :, :], PS[4 + q % 4][:, :].rearrange("p (t n) -> p t n", t=NT)), E6["st_evac"])
        XC = R[5][:, 0:1024].rearrange("p (k n) -> p k n", k=KD)
        STc = R[5][:, 1024:1536].rearrange("p (t n) -> p t n", t=NT)
        SG = [R[5][:, 1536:2048], R[5][:, 2048:2560]]
        H = R[5][:, 2560:3584].rearrange("p (j n) -> p j n", j=2)
        HTE = R[6][:, 0:1024].rearrange("p (c n) -> p c n", c=8)
        YP = R[6][:, 1024:2048]
        names = ("xc", "stc", "g_done", "u_done", "silu", "h", "tp_done", "tp_evac", "dn_done", "y", "o_done", "o_free")
        E7 = {n: sem("e_" + n) for n in names}
        GB, UB, TB, DB, OB = (PS[0], PS[1]), (PS[2], PS[3]), PS[4], PS[5], (PS[6], PS[7])
        with nc.Block() as block:
            @block.sync
            def _(sp):
                def reload(r, i):
                    sp.wait_ge(ring_in[r % NR], 16)
                    x, part = 2 * i + (r - NR) // PER, (r - NR) % PER
                    if part < 8:
                        sp.wait_ge(E7[("g_done", "u_done")[part % 4 // 2]], 2 * x + part // 4 + 1)
                    else:
                        sp.wait_ge(E7["dn_done"], 4 * x + part - 8 + 1)
                    expert_slab(sp, r, 2 * i)

                for r in range(3, NR):
                    expert_slab(sp, r, 0)
                with sp.Fori(0, NPAIR - 1) as i:
                    for r in range(NR, NR + 2 * PER):
                        reload(r, i)
                for r in range(NR, 2 * PER):
                    reload(r, NPAIR - 1)

            @block.gpsimd
            def _(pool):
                def copies(q):
                    nc.gpsimd.tensor_copy(XC, XE[:, bass.ds(q, 1), :, :].rearrange("p o k n -> p (o k) n")).then_inc(E7["xc"], 1)

                def copy_st(q):
                    nc.gpsimd.tensor_copy(STc, ST[:, bass.ds(q, 1), :, :].rearrange("p o t n -> p (o t) n")).then_inc(E7["stc"], 1)

                copies(0)
                copy_st(0)
                with pool.Fori(0, NPAIR - 1) as i:
                    pool.wait_ge(E7["u_done"], 4 * i + 4)
                    copies(i + 1)
                    pool.wait_ge(E7["o_done"], 8 * i + 8)
                    copy_st(i + 1)

            @block.tensor
            def _(pe):
                with pe.Fori(0, NPAIR) as i:
                    pe.wait_ge(E7["xc"], i + 1)
                    for e in range(2):
                        x = 2 * i + e
                        toks = slice(e * CAP, (e + 1) * CAP)

                        def arrive(part):
                            r = e * PER + part
                            pe.wait_ge(ring_in[r % NR], 64 * i + 16 * (r // NR + 1))
                            return RING[r % NR][:, :]

                        def wide(bank, part, done):
                            lo, hi = (arrive(part + n).rearrange("p (k n) -> p k n", k=KD) for n in range(2))
                            for k in range(KD):
                                pe.matmul(bank[0:CAP, :], XC[:, k, toks], lo[:, k, :], start=(k == 0), stop=(k == KD - 1))
                                m = pe.matmul(bank[CAP:P, :], XC[:, k, toks], hi[:, k, :], start=(k == 0), stop=(k == KD - 1))
                            m.then_inc(done, 1)

                        def turn(j):
                            pe.wait_ge(E7["h"], 2 * x + j + 1)
                            for c in range(4):
                                m = pe.transpose(TB[:, c * P:(c + 1) * P], H[:, j, c * P:(c + 1) * P], ident)
                            m.then_inc(E7["tp_done"], 1)

                        def down(n):
                            w = arrive(8 + n).rearrange("p (k n) -> p k n", k=4)
                            if n % 2 == 0:
                                pe.wait_ge(E7["tp_evac"], 2 * x + n // 2 + 1)
                            if n == 0 and e == 1:
                                pe.wait_ge(E7["y"], 2 * i + 1)
                            half, c0 = DOWN[n] // 2, DOWN[n] % 2 * 4
                            for k in range(4):
                                hk = HTE[:, c0 + k, half * CAP:(half + 1) * CAP]
                                first, last = n == 0 and k == 0, n == 3 and k == 3
                                pe.matmul(DB[0:CAP, :], hk, w[:, k, 0:512], start=first, stop=last)
                                m = pe.matmul(DB[CAP:P, :], hk, w[:, k, 512:1024], start=first, stop=last)
                            m.then_inc(E7["dn_done"], 1)

                        wide(GB[0], 0, E7["g_done"])
                        wide(UB[0], 2, E7["u_done"])
                        wide(GB[1], 4, E7["g_done"])
                        turn(0)
                        wide(UB[1], 6, E7["u_done"])
                        down(0)
                        down(1)
                        turn(1)
                        down(2)
                        down(3)
                    pe.wait_ge(E7["y"], 2 * i + 2)
                    pe.wait_ge(E7["stc"], i + 1)
                    for n in range(2 * NT):
                        t, half = n // 2, n % 2
                        pe.wait_ge(E7["o_free"], 8 * i + n + 1)
                        pe.matmul(OB[half][:, :], STc[:, t, :], YP[:, half * 512:(half + 1) * 512], start=True, stop=True)\
                          .then_inc(E7["o_done"], 1)

            @block.scalar
            def _(act):
                with act.Fori(0, NPAIR) as i:
                    for e in range(2):
                        x = 2 * i + e

                        def silu(j):
                            act.wait_ge(E7["g_done"], 2 * x + j + 1)
                            nc.scalar.activation(SG[j], GB[j][:, :], ACT.Silu).then_inc(E7["silu"], 1)

                        def evac(j):
                            act.wait_ge(E7["tp_done"], 2 * x + j + 1)
                            nc.scalar.activation(HTE[:, 4 * j:4 * j + 4, :], TB[:, :].rearrange("p (c n) -> p c n", c=4), ACT.Copy)\
                              .then_inc(E7["tp_evac"], 1)

                        silu(0)
                        silu(1)
                        evac(0)
                        evac(1)

            @block.vector
            def _(dve):
                dve.sem_inc(E7["o_free"], 2)
                with dve.Fori(0, NPAIR) as i:
                    for e in range(2):
                        x = 2 * i + e
                        for j in range(2):
                            dve.wait_ge(E7["u_done"], 2 * x + j + 1)
                            dve.wait_ge(E7["silu"], 2 * x + j + 1)
                            nc.vector.tensor_tensor(H[:, j, :], SG[j], UB[j][:, :], ALU.mult).then_inc(E7["h"], 1)
                        dve.wait_ge(E7["dn_done"], 4 * x + 4)
                        rows = slice(e * CAP, (e + 1) * CAP)
                        nc.vector.tensor_copy(YP[rows, 0:512], DB[0:CAP, :])
                        nc.vector.tensor_copy(YP[rows, 512:1024], DB[CAP:P, :]).then_inc(E7["y"], 1)
                    for n in range(2 * NT):
                        t, half = n // 2, n % 2
                        xs = x3[:, t, half * 512:(half + 1) * 512]
                        dve.wait_ge(E7["o_done"], 8 * i + n + 1)
                        nc.vector.tensor_tensor(xs, xs, OB[half][:, :], ALU.add).then_inc(E7["o_free"], 1)
        spent.extend([p5, gate5, merge5, m5, out5, *E6.values(), *E7.values()])
        clear_spent()
        w2 = io["w_in_2"][0]
        nfrow = R[1][:, 0:D]
        junk = R[5][:, :].rearrange("p (t d) -> p t d", t=NT)
        E8 = {n: sem("f_" + n) for n in ("nf", "rstd", "x", "t_done", "t_evac", "misc")}
        PROJ2 = [("a_iq", A_IQ), ("misc", None), ("a_q", A_Q), ("a_gate", A_GATE), ("b_i", B_I), ("b_q", B_Q),
                 ("b_gate", B_GATE), ("b_f", B_F)]
        MISC = P + 64 + 64 + 8
        w_uk, w_uv = (SL[3][:, i * 512:(i + 1) * 512].rearrange("p (h r) -> p h r", h=4) for i in range(2))
        onehot = SL[3][0:32, 1024:1024 + REL]
        rb = SL[3][0:32, 1664:1668]
        kvrow = stat128

        def load2(eng, i):
            name, c0 = PROJ2[i]
            if name == "misc":
                dst = SL[i % 3][:, 0:KD * MISC].rearrange("p (k n) -> p k n", k=KD)
                for to, c, n in ((0, A_CKV, P), (P, A_IK, 64), (P + 64, A_IK, 64), (2 * P, A_IW, 8)):
                    eng.dma_start(dst[:, :, to:to + n], w2[:, c:c + n].rearrange("(k p) n -> p k n", p=P)).then_inc(slab_in[i % 3], 16)
                slab_n[i % 3] += 64
            else:
                load_slab(eng, i % 3, w2[:, c0:c0 + 512], 512)
            after2[i] = slab_n[i % 3]

        after2 = {}
        with nc.Block() as block:
            @block.sync
            def _(sp):
                sp.dma_start(nfrow, io["norm_f_w"].unsqueeze(0).to_broadcast([P, D])).then_inc(E8["nf"], 16)
                for i in range(3):
                    load2(sp, i)
                sp.dma_start(kvrow, io["kv_norm_g_2"].to_broadcast([P, P])).then_inc(E8["misc"], 16)
                sp.dma_start(w_uk, io["w_uk_2"][0].rearrange("h d r -> d h r")).then_inc(E8["misc"], 16)
                sp.dma_start(w_uv, io["w_uv_2"][0].rearrange("h r v -> r h v")).then_inc(E8["misc"], 16)
                sp.dma_start(onehot, io["table"][0:32, T_BUCKET:T_BUCKET + REL]).then_inc(E8["misc"], 16)
                sp.dma_start(rb, io["rel_bias_2"]).then_inc(E8["misc"], 16)

            @block.scalar
            def _(act):
                a = A()
                for t in range(NT):
                    a(nc.scalar.activation(junk[:, t, :], x3[:, t, :], ACT.Square, accum_out=stat[:, t:t + 1]))
                rsqrt(a, stat[:, 8:12], stat[:, 0:4], 1.0 / D, E8["rstd"])
                for k in range(KD):
                    act.wait_ge(E8["t_done"], k + 1)
                    a(nc.scalar.activation(hT[:, k, :], PS[k % 4][:, :], ACT.Copy), E8["t_evac"])

            @block.tensor
            def _(pe):
                pe.wait_ge(E8["x"], NT)
                for k in range(KD):
                    if k >= 4:
                        pe.wait_ge(E8["t_evac"], k - 3)
                    for t in range(NT):
                        m = pe.transpose(PS[k % 4][:, t * P:(t + 1) * P], x3[:, t, k * P:(k + 1) * P], ident)
                    m.then_inc(E8["t_done"], 1)

            @block.vector
            def _(dve):
                v = V()
                dve.wait_ge(E8["nf"], 16)
                dve.wait_ge(E8["rstd"], 1)
                for t in range(NT):
                    xs = x3[:, t, :]
                    v(nc.vector.scalar_tensor_tensor(xs, xs, stat[:, 8 + t:9 + t], nfrow, ALU.mult, ALU.mult), E8["x"])
        def r4(ap):
            return ap.rearrange("p (h s) -> p h s", h=4)

        aqT, qlT = r4(R[1][:, 0:2048]), r4(R[1][:, 2048:4096])
        iqT, ikz = r4(R[2][:, 0:2048]), (R[2][:, 2048:2560], R[2][:, 2560:3072])
        cT, ctok = R[2][:, 3072:3584], R[2][:, 3584:4096].rearrange("p (t r) -> p t r", t=NT)
        agT, bgT = r4(R[3][:, 0:2048]), r4(R[3][:, 2048:4096])
        bqT, kkT = r4(R[4][:, 0:2048]), r4(R[4][:, 2048:4096])
        bT, vtok = r4(R[5][:, 0:2048]), r4(R[5][:, 2048:4096])
        iw = gl[:, 0:32]
        lb, olb, lbt = stat[:, 12:16], stat[:, 16:20], stat[:, 20:32]
        sig = [R[6][:, i * 512:(i + 1) * 512] for i in range(2)]
        csq = R[6][:, 1024:1536]
        E9 = {n: sem("g_" + n) for n in ("p", "evac", "ikpad", "lbd", "lbe", "lb", "c_rstd", "c", "ct", "ct_evac", "ql", "ql_evac", "f")}
        UNITS = []
        for i, (name, _) in enumerate(PROJ2):
            UNITS += [(i, name, j) for j in range(3 if name == "misc" else 4)]
        UNIT = {(name, j): n for n, (_, name, j) in enumerate(UNITS)}
        bias_m = r4(SL[0][:, 0:2048])
        keep = r4(SL[3][:, 2048:4096])
        frow = SL[2][:, 0:4 * REL].rearrange("p (h u) -> p h u", h=4)
        score = [R[6][:, 1536 + i * 512:2048 + i * 512] for i in range(3)]
        rel = [R[6][:, 3072 + i * 512:3584 + i * 512] for i in range(2)]
        mx = gl[:, 32:40]
        scratch = io["scratch"]
        E10 = {n: sem("i_" + n) for n in ("dot", "relu", "used", "f", "fr", "out", "in")}
        ITEMS = [(t, h) for t in range(1, NT) for h in range(8)]
        first_item = {}
        for n in range(0, len(ITEMS), 2):
            t, h = ITEMS[n]
            first_item[UNIT["a_q", 0] + 5 * (t - 1) + h // 2] = n
        with nc.Block() as block:
            @block.sync
            def _(sp):
                for i in range(3, len(PROJ2)):
                    used = max(n for n, u in enumerate(UNITS) if u[0] == i - 3) + 1
                    sp.wait_ge(E9["p"], used)
                    load2(sp, i)
                for h in range(4):
                    sp.wait_ge(E10["fr"], h + 1)
                    sp.dma_start(scratch[h].rearrange("(p u) -> p u", p=P), frow[:, h, :]).then_inc(E10["out"], 16)
                sp.wait_ge(E10["out"], 64)
                sp.wait_ge(E9["p"], UNIT["b_gate", 3] + 1)
                for h in range(4):
                    skew = scratch[h, P - 1:P - 1 + P * (REL - 1)].rearrange("(p u) -> p u", p=P)[:, 0:512]
                    sp.dma_start(bias_m[:, h, :], skew).then_inc(E10["in"], 16)
                sp.wait_ge(E10["in"], 64)

            @block.gpsimd
            def _(pool):
                g = G_()
                g(nc.gpsimd.memset(ikz[0][64:128, :], 0.0), E9["ikpad"])
                g(nc.gpsimd.memset(ikz[1][0:64, :], 0.0), E9["ikpad"])

            @block.tensor
            def _(pe):
                pe.wait_ge(E8["misc"], 80)

                def index_dot(n):
                    t, h = ITEMS[n]
                    W = (t + 1) * P
                    if n == 8:
                        pe.wait_ge(E9["ct_evac"], 1)
                    if n == 0:
                        pe.wait_ge(E9["evac"], UNIT["misc", 2] + 1)
                    if n >= 2:
                        pe.wait_ge(E10["relu"], n - 1)
                    pe.matmul(PS[4 + 3 * (n % 2)][:, 0:W], iqT[:, h // 2, t * P:(t + 1) * P], ikz[h % 2][:, 0:W],
                              start=True, stop=True).then_inc(E10["dot"], 1)

                def bias_row(h):
                    pe.wait_ge(E10["relu"], len(ITEMS))
                    pe.wait_ge(E9["ql_evac"], 4)
                    if h:
                        pe.wait_ge(E10["fr"], h)
                    pe.matmul(PS[4][:, :], rb[:, h:h + 1].to_broadcast([32, P]), onehot[:, 0:512], start=True, stop=True)
                    pe.matmul(PS[5][:, 0:REL - 512], rb[:, h:h + 1].to_broadcast([32, P]), onehot[:, 512:REL],
                              start=True, stop=True).then_inc(E10["f"], 1)

                def c_turn():
                    pe.wait_ge(E9["c"], 4)
                    pe.wait_ge(E10["relu"], 8)
                    for t in range(NT):
                        m = pe.transpose(PS[4][:, t * P:(t + 1) * P], ctok[:, t, :], ident)
                    m.then_inc(E9["ct"], 1)

                def q_lat(h):
                    if h >= 2:
                        pe.wait_ge(E9["ql_evac"], h - 1)
                    pe.matmul(PS[5 + h % 2][:, :], w_uk[:, h, :], aqT[:, h, :], start=True, stop=True).then_inc(E9["ql"], 1)

                for n, (i, name, j) in enumerate(UNITS):
                    pe.wait_ge(slab_in[i % 3], after2[i])
                    if n >= 4:
                        pe.wait_ge(E9["evac"], n - 3)
                    bank = PS[n % 4]
                    if name == "misc":
                        w = SL[i % 3][:, 0:KD * MISC].rearrange("p (k n) -> p k n", k=KD)
                        if j == 0 or j == 1:
                            c0, cn = (0, P) if j == 0 else (2 * P, 8)
                            for t in range(NT):
                                for k in range(KD):
                                    m = pe.matmul(bank[:, t * cn:(t + 1) * cn], hT[:, k, t * P:(t + 1) * P], w[:, k, c0:c0 + cn],
                                                  start=(k == 0), stop=(k == KD - 1))
                        else:
                            for k in range(KD):
                                m = pe.matmul(bank[:, :], w[:, k, P:2 * P], hT[:, k, :], start=(k == 0), stop=(k == KD - 1))
                    elif name == "b_i":
                        for k in range(KD):
                            m = pe.matmul(bank[:, :], hT[:, k, j * P:(j + 1) * P], slab(i % 3)[:, k, :],
                                          start=(k == 0), stop=(k == KD - 1))
                    else:
                        for k in range(KD):
                            m = pe.matmul(bank[:, :], slab(i % 3)[:, k, j * P:(j + 1) * P], hT[:, k, :],
                                          start=(k == 0), stop=(k == KD - 1))
                    m.then_inc(E9["p"], 1)
                    if name == "a_gate" and j == 0:
                        c_turn()
                    if name == "a_gate":
                        q_lat(j)
                    if n in first_item:
                        index_dot(first_item[n])
                        index_dot(first_item[n] + 1)
                    if name == "b_gate":
                        bias_row(j)

            @block.scalar
            def _(act):
                a = A()
                act.wait_ge(E9["lbd"], 1)
                a(nc.scalar.activation(lbt[:, 0:8], lbt[:, 0:8], ACT.Exp), E9["lbe"])
                act.wait_ge(E9["ikpad"], 2)
                cp = nc.scalar.activation
                for n, (i, name, j) in enumerate(UNITS):
                    bank = PS[n % 4]
                    act.wait_ge(E9["p"], n + 1)
                    if name == "a_q":
                        a(cp(aqT[:, j, :], bank[:, :], ACT.Copy), E9["evac"])
                    elif name == "a_iq":
                        a(cp(iqT[:, j, :], bank[:, :], ACT.Copy), E9["evac"])
                    elif name == "misc" and j == 0:
                        a(cp(ctok.rearrange("p t r -> p (t r)"), bank[:, :], ACT.Copy), E9["evac"])
                        for t in range(NT):
                            a(cp(csq[:, t * P:(t + 1) * P], ctok[:, t, :], ACT.Square, accum_out=stat[:, t:t + 1]))
                        rsqrt(a, stat[:, 4:8], stat[:, 0:4], 1.0 / P, E9["c_rstd"])
                    elif name == "misc" and j == 1:
                        a(cp(iw, bank[:, 0:32], ACT.Copy, scale=8 ** -0.5), E9["evac"])
                    elif name == "misc":
                        a(cp(ikz[0][0:64, :], bank[0:64, :], ACT.Copy))
                        a(cp(ikz[1][64:128, :], bank[64:128, :], ACT.Copy), E9["evac"])
                    elif name == "b_i":
                        a(cp(vtok[:, j, :], bank[:, :], ACT.Copy), E9["evac"])
                    elif name == "b_f":
                        if j >= 2:
                            act.wait_ge(E9["f"], j - 1)
                        a(cp(sig[j % 2], bank[:, :], ACT.Sigmoid), E9["evac"])
                    else:
                        dst = {"a_gate": agT, "b_q": bqT, "b_gate": bgT}[name]
                        a(cp(dst[:, j, :], bank[:, :], ACT.Silu), E9["evac"])
                    if name == "a_gate" and j == 0:
                        act.wait_ge(E9["ct"], 1)
                        a(cp(cT, PS[4][:, :], ACT.Copy), E9["ct_evac"])
                    if name == "a_gate":
                        act.wait_ge(E9["ql"], j + 1)
                        a(cp(qlT[:, j, :], PS[5 + j % 2][:, :], ACT.Copy), E9["ql_evac"])
                    if n in first_item:
                        for m in (first_item[n], first_item[n] + 1):
                            W = (ITEMS[m][0] + 1) * P
                            act.wait_ge(E10["dot"], m + 1)
                            if m >= 2:
                                act.wait_ge(E10["used"], m - 1)
                            a(cp(rel[m % 2][:, 0:W], PS[4 + 3 * (m % 2)][:, 0:W], ACT.Relu, scale=0.125), E10["relu"])
                    if name == "b_gate":
                        act.wait_ge(E10["f"], j + 1)
                        a(cp(frow[:, j, 0:512], PS[4][:, :], ACT.Copy))
                        a(cp(frow[:, j, 512:REL], PS[5][:, 0:REL - 512], ACT.Copy), E10["fr"])
                act.wait_ge(E9["f"], 4)
                a(cp(bT, bT, ACT.Ln))

            @block.vector
            def _(dve):
                v = V()
                tt, ts = nc.vector.tensor_tensor, nc.vector.tensor_scalar
                v(tt(lbt[:, 8:12], lbc[:, 0:4], lbc[:, 4:8], ALU.max))
                v(tt(lbt[:, 0:4], lbc[:, 0:4], lbt[:, 8:12], ALU.subtract))
                v(tt(lbt[:, 4:8], lbc[:, 4:8], lbt[:, 8:12], ALU.subtract), E9["lbd"])
                dve.wait_ge(E9["lbe"], 1)
                v(tt(lbt[:, 8:12], lbt[:, 0:4], lbt[:, 4:8], ALU.add))
                v(nc.vector.reciprocal(lbt[:, 8:12], lbt[:, 8:12]))
                v(tt(lb, lbt[:, 0:4], lbt[:, 8:12], ALU.mult))
                v(ts(olb, lb, -1.0, 1.0, ALU.mult, ALU.add))
                dve.wait_ge(E8["misc"], 80)
                dve.wait_ge(E9["c_rstd"], 1)
                for t in range(NT):
                    v(nc.vector.scalar_tensor_tensor(ctok[:, t, :], ctok[:, t, :], stat[:, 4 + t:5 + t], kvrow, ALU.mult, ALU.mult), E9["c"])
                for t in range(NT):
                    W = (t + 1) * P
                    k_ = keep[:, t, 0:W]
                    if t == 0:
                        v(nc.vector.memset(k_, 0.0))
                        v(nc.vector.memset(keep[0:64, t, 64:P], -BIG))
                        continue
                    sc = score[t - 1][:, 0:W]
                    for h in range(8):
                        n = 8 * (t - 1) + h
                        w = iw[:, t * 8 + h:t * 8 + h + 1]
                        dve.wait_ge(E10["relu"], n + 1)
                        if h == 0:
                            v(ts(sc, rel[n % 2][:, 0:W], w, None, ALU.mult), E10["used"])
                        else:
                            v(nc.vector.scalar_tensor_tensor(sc, rel[n % 2][:, 0:W], w, sc, ALU.mult, ALU.add), E10["used"])
                    v(nc.vector.memset(sc[0:64, W - 64:W], -BIG))
                    for r in range(TOPK // 8):
                        v(nc.vector.max(mx, sc))
                        v(nc.vector.match_replace(sc, mx, sc, -STRUCK))
                    v(ts(k_, sc, -0.5 * (BIG + STRUCK), -BIG, ALU.is_gt, ALU.mult))
                at_f = min(n for n, u in enumerate(UNITS) if u[1] == "b_f")
                for j in range(4):
                    dve.wait_ge(E9["evac"], at_f + j + 1)
                    v(ts(bT[:, j, :], sig[j % 2], olb[:, j:j + 1], lb[:, j:j + 1], ALU.mult, ALU.add))
                    v(ts(kkT[:, j, :], bT[:, j, :], -1.0, 1.0, ALU.mult, ALU.add), E9["f"])
        oT = R[6][:, :].rearrange("p (k s) -> p k s", k=KD)
        lgt = [SL[2][:, i * 512:(i + 1) * 512] for i in range(NB)]
        pTc = [SL[2][:, 1536 + i * 512:2048 + i * 512].rearrange("p (c q) -> p c q", c=NT) for i in range(2)]
        olT = [SL[2][:, 2560 + i * 512:3072 + i * 512] for i in range(2)]
        E11 = {n: sem("j_" + n) for n in ("s", "lm", "exp", "p", "t", "te", "o", "oe", "v", "g")}
        NU2 = 4 * NT
        with nc.Block() as block:
            @block.tensor
            def _(pe):
                def turn(n):
                    t = n % NT
                    pe.wait_ge(E11["p"], n + 1)
                    if n >= 2:
                        pe.wait_ge(E11["te"], n - 1)
                    for c in range(t + 1):
                        m = pe.transpose(PS[2 + n % 2][:, c * P:(c + 1) * P], lgt[n % NB][:, c * P:(c + 1) * P], ident)
                    m.then_inc(E11["t"], 1)

                def pv(n):
                    h, t = n // NT, n % NT
                    pe.wait_ge(E11["te"], n + 1)
                    if t == 0 and h >= 2:
                        pe.wait_ge(E11["oe"], h - 1)
                    for c in range(t + 1):
                        m = pe.matmul(PS[4 + h % 2][:, t * P:(t + 1) * P], ctok[:, c, :], pTc[n % 2][:, c, :],
                                      start=(c == 0), stop=(c == t))
                    m.then_inc(E11["o"], 1)

                def up_v(h):
                    pe.wait_ge(E11["oe"], h + 1)
                    if h >= 2:
                        pe.wait_ge(E11["g"], h - 1)
                    pe.matmul(PS[6 + h % 2][:, :], w_uv[:, h, :], olT[h % 2], start=True, stop=True).then_inc(E11["v"], 1)

                for n in range(NU2 + 4):
                    if n < NU2:
                        h, t = n // NT, n % NT
                        if n >= 2:
                            pe.wait_ge(E11["lm"], n - 1)
                        pe.matmul(PS[n % 2][:, 0:(t + 1) * P], qlT[:, h, t * P:(t + 1) * P], cT[:, 0:(t + 1) * P],
                                  start=True, stop=True).then_inc(E11["s"], 1)
                    if 2 <= n <= NU2 + 1:
                        turn(n - 2)
                    if 3 <= n <= NU2 + 2:
                        pv(n - 3)
                    if n >= 7 and (n - 7) % NT == 0:
                        up_v((n - 7) // NT)

            @block.scalar
            def _(act):
                a = A()

                def evac(n):
                    t = n % NT
                    act.wait_ge(E11["t"], n + 1)
                    if n >= 2:
                        act.wait_ge(E11["o"], n - 1)
                    a(nc.scalar.activation(pTc[n % 2][:, 0:t + 1, :],
                                           PS[2 + n % 2][:, 0:(t + 1) * P].rearrange("p (c q) -> p c q", c=t + 1), ACT.Copy), E11["te"])
                    if t == NT - 1:
                        h = n // NT
                        act.wait_ge(E11["o"], n + 1)
                        if h >= 2:
                            act.wait_ge(E11["v"], h - 1)
                        a(nc.scalar.activation(olT[h % 2], PS[4 + h % 2][:, :], ACT.Copy), E11["oe"])

                for n in range(NU2):
                    W = (n % NT + 1) * P
                    s = stat[:, 8 * (n % NB):8 * (n % NB) + 8]
                    act.wait_ge(E11["lm"], n + 1)
                    a(nc.scalar.activation(lgt[n % NB][:, 0:W], lgt[n % NB][:, 0:W], ACT.Exp, bias=s[:, 1:2], accum_out=s[:, 2:3]), E11["exp"])
                    if n >= 2:
                        evac(n - 2)
                evac(NU2 - 2)
                evac(NU2 - 1)

            @block.vector
            def _(dve):
                v = V()
                tt, ts = nc.vector.tensor_tensor, nc.vector.tensor_scalar

                def logits(n):
                    h, t = n // NT, n % NT
                    W = (t + 1) * P
                    s = stat[:, 8 * (n % NB):8 * (n % NB) + 8]
                    l = lgt[n % NB][:, 0:W]
                    dve.wait_ge(E11["s"], n + 1)
                    if n >= NB:
                        dve.wait_ge(E11["t"], n - NB + 1)
                    v(nc.vector.scalar_tensor_tensor(l, PS[n % 2][:, 0:W], P ** -0.5, bias_m[:, h, 512 - W:512], ALU.mult, ALU.add))
                    v(tt(l, l, keep[:, t, 0:W], ALU.add))
                    v(nc.vector.reduce_max(s[:, 0:1], l, AX))
                    v(ts(s[:, 1:2], s[:, 0:1], -1.0, None, ALU.mult), E11["lm"])

                def out(h):
                    dve.wait_ge(E11["v"], h + 1)
                    v(tt(oT[:, h, :], PS[6 + h % 2][:, :], agT[:, h, :], ALU.mult), E11["g"])

                logits(0)
                for n in range(NU2):
                    if n + 1 < NU2:
                        logits(n + 1)
                    W = (n % NT + 1) * P
                    s = stat[:, 8 * (n % NB):8 * (n % NB) + 8]
                    l = lgt[n % NB][:, 0:W]
                    dve.wait_ge(E11["exp"], n + 1)
                    v(nc.vector.reciprocal(s[:, 3:4], s[:, 2:3]))
                    v(ts(l, l, s[:, 3:4], None, ALU.mult), E11["p"])
                    if n >= 9 and (n - 9) % NT == 0:
                        out((n - 9) // NT)
                out(2)
                out(3)
        FB = [SL[0][:, 0:2048], SL[0][:, 2048:4096]]
        QF = [SL[1][:, 0:2048], SL[1][:, 2048:4096]]
        KF = [SL[2][:, 0:2048], SL[2][:, 2048:4096]]
        sco = SL[3][:, 0:2048].rearrange("p (a t) -> p a t", a=16)
        QE = SL[3][:, 2048:4096].rearrange("p (a t) -> p a t", a=16)
        bq, kk, bb = R[4][:, 0:2048], R[4][:, 2048:4096], R[5][:, 0:2048]
        resets = HT[:, 0:2048]
        KDt = HT[:, 2048:4096].rearrange("p (a d) -> p a d", a=16)
        Sb = R[1][:, 0:512].rearrange("p (h d) -> p h d", h=4)
        eL = decs[:, 0:16]
        sq12 = [R[1][:, 1024:1536], R[1][:, 1536:2048]]
        rs12 = [R[1][:, 2048:2560], R[1][:, 2560:3072]]
        c16 = lambda ap: ap.rearrange("p (a t) -> p a t", a=16)
        E12 = {n: sem("k_" + n) for n in ("reset", "b", "diff", "F", "Q", "K", "s", "sc", "e", "qe", "kd", "t", "te", "o", "oe", "u", "S", "sq", "ss", "rs", "n", "el")}
        LV = [None] + LEVELS
        wo2 = io["w_o_2"][0]
        wo_half = [reg[:, :].rearrange("p (k n) -> p k n", k=KD) for reg in (R[2], SL[1])]
        wo_in = sem("wo_in")
        with nc.Block() as block:
            @block.sync
            def _(sp):
                for n in range(2):
                    if n:
                        sp.wait_ge(E12["s"], 4 * NL + 4)
                    sp.dma_start(wo_half[n], wo2[:, n * 512:(n + 1) * 512].rearrange("(k p) n -> p k n", p=P)).then_inc(wo_in, 16)

            @block.gpsimd
            def _(pool):
                g = G_()
                g(nc.gpsimd.memset(resets, 1.0))
                g(nc.gpsimd.memset(c16(resets)[:, :, 0:1], 0.0), E12["reset"])
                for i in range(1, NL + 1):
                    pool.wait_ge(E12["F"], i)
                    if i >= 2:
                        pool.wait_ge(E12["s"], 4 * (i - 1))
                    g(nc.gpsimd.tensor_tensor(KF[i % 2], kk, FB[i % 2], ALU.mult), E12["K"])
                pool.wait_ge(E12["e"], 1)
                g(nc.gpsimd.tensor_tensor(QE.rearrange("p a t -> p (a t)"), bq, FB[0], ALU.mult), E12["qe"])
                pool.wait_ge(E12["e"], 2)
                pool.wait_ge(E12["s"], 4 * NL + 4)
                g(nc.gpsimd.tensor_tensor(KF[0], kk, FB[1], ALU.mult), E12["kd"])

            @block.scalar
            def _(act):
                a = A()
                for i in range(1, NL + 1):
                    act.wait_ge(E12["diff"], i)
                    a(nc.scalar.activation(FB[i % 2], FB[i % 2], ACT.Abs))
                    a(nc.scalar.activation(FB[i % 2], FB[i % 2], ACT.Exp, scale=-1.0), E12["F"])
                act.wait_ge(E12["Q"], NL - 1)
                act.wait_ge(E12["K"], NL - 1)
                a(nc.scalar.activation(FB[0], bb, ACT.Exp), E12["e"])
                a(nc.scalar.activation(eL, c16(bb)[:, :, P - 1], ACT.Exp), E12["el"])
                act.wait_ge(E12["diff"], NL + 1)
                a(nc.scalar.activation(FB[1], FB[1], ACT.Exp, scale=-1.0), E12["e"])
                for u in range(4):
                    act.wait_ge(E12["t"], u + 1)
                    a(nc.scalar.activation(KDt[:, 4 * u:4 * u + 4, :], PS[4 + u % 2][:, :].rearrange("p (a d) -> p a d", a=4), ACT.Copy), E12["te"])

                def norm(h):
                    act.wait_ge(E12["ss"], h + 1)
                    if h >= 2:
                        act.wait_ge(E12["n"], h - 1)
                    rsqrt(a, rs12[h % 2], PS[h % 2][:, :], 1.0 / P, E12["rs"])

                act.wait_ge(E12["oe"], NT)
                for h in range(4):
                    if h >= 2:
                        act.wait_ge(E12["ss"], h - 1)
                    a(nc.scalar.activation(sq12[h % 2], oT[:, 4 + h, :], ACT.Square), E12["sq"])
                    if h >= 1:
                        norm(h - 1)
                norm(3)

            @block.tensor
            def _(pe):
                for i in range(NL + 1):
                    if i:
                        pe.wait_ge(E12["Q"], i)
                        pe.wait_ge(E12["K"], i)
                    k_, q_ = (c16(kk), c16(bq)) if i == 0 else (c16(KF[i % 2]), c16(QF[i % 2]))
                    for u in range(4):
                        if i:
                            pe.wait_ge(E12["sc"], 4 * (i - 1) + u + 1)
                        for j in range(4):
                            m = pe.matmul(PS[u][:, j * P:(j + 1) * P], k_[:, 4 * u + j, :], q_[:, 4 * u + j, :], start=True, stop=True)
                        m.then_inc(E12["s"], 1)
                pe.wait_ge(E12["kd"], 1)
                for u in range(4):
                    if u >= 2:
                        pe.wait_ge(E12["te"], u - 1)
                    for j in range(4):
                        m = pe.transpose(PS[4 + u % 2][:, j * P:(j + 1) * P], c16(KF[0])[:, 4 * u + j, :], ident)
                    m.then_inc(E12["t"], 1)
                pe.wait_ge(E12["te"], 4)
                pe.wait_ge(E12["qe"], 1)
                pe.wait_ge(E12["sc"], 4 * NL + 4)
                for c in range(NT):
                    if c:
                        pe.wait_ge(E12["S"], c)
                    for h in range(4):
                        a_ = 4 * h + c
                        o = PS[c % 2][:, h * P:(h + 1) * P]
                        pe.matmul(o, vtok[:, c, h * P:(h + 1) * P], sco[:, a_, :], start=True, stop=(c == 0))
                        if c:
                            m = pe.matmul(o, Sb[:, h, :], QE[:, a_, :], start=False, stop=True)
                    if c:
                        m.then_inc(E12["o"], 1)
                    for h in range(4):
                        m = pe.matmul(PS[2 + c % 2][:, h * P:(h + 1) * P], KDt[:, 4 * h + c, :], vtok[:, c, h * P:(h + 1) * P], start=True, stop=True)
                    m.then_inc(E12["u"], 1)
                pe.wait_ge(E12["oe"], NT)
                for h in range(4):
                    pe.wait_ge(E12["sq"], h + 1)
                    if h >= 2:
                        pe.wait_ge(E12["rs"], h - 1)
                    pe.matmul(PS[h % 2][:, :], ones, sq12[h % 2], start=True, stop=True).then_inc(E12["ss"], 1)

            @block.vector
            def _(dve):
                v = V()
                tt = nc.vector.tensor_tensor
                dve.wait_ge(E12["reset"], 1)
                v(nc.vector.tensor_tensor_scan(FB[0], resets, bb, 0.0, ALU.mult, ALU.add))
                v(nc.vector.tensor_copy(bb, FB[0]), E12["b"])

                def diff(i):
                    s = LEVELS[i - 1]
                    blocks = lambda ap: ap.rearrange("p (n w) -> p n w", w=2 * s)
                    mid = blocks(bb)[:, :, s - 1:s].to_broadcast([P, 2048 // (2 * s), 2 * s])
                    v(tt(blocks(FB[i % 2]), blocks(bb), mid, ALU.subtract), E12["diff"])

                def add(i):
                    mask = ident if i == 0 else up[i - 1]
                    for u in range(4):
                        dve.wait_ge(E12["s"], 4 * i + u + 1)
                        ps, dst = PS[u][:, :].rearrange("p (a t) -> p a t", a=4), sco[:, 4 * u:4 * u + 4, :]
                        if i == 0:
                            v(tt(dst, ps, all4(mask), ALU.mult), E12["sc"])
                        else:
                            tmp = R[1][:, 512:1024].rearrange("p (a t) -> p a t", a=4)
                            v(tt(tmp, ps, all4(mask), ALU.mult))
                            v(tt(dst, dst, tmp, ALU.add), E12["sc"])

                diff(1)
                add(0)
                for i in range(1, NL + 1):
                    dve.wait_ge(E12["F"], i)
                    v(tt(QF[i % 2], bq, FB[i % 2], ALU.mult), E12["Q"])
                    if i < NL:
                        if i >= 2:
                            dve.wait_ge(E12["K"], i - 1)
                        diff(i + 1)
                    add(i)
                dve.wait_ge(E12["K"], NL)
                last = c16(bb)[:, :, P - 1:P].to_broadcast([P, 16, P])
                v(tt(c16(FB[1]), c16(bb), last, ALU.subtract), E12["diff"])
                dve.wait_ge(E12["el"], 1)
                for c in range(NT):
                    if c:
                        dve.wait_ge(E12["o"], c)
                    dve.wait_ge(E12["u"], c + 1)
                    v(nc.vector.tensor_copy(oT[:, 4:8, c * P:(c + 1) * P], PS[c % 2][:, :].rearrange("p (h t) -> p h t", h=4)), E12["oe"])
                    for h in range(4):
                        ps = PS[2 + c % 2][:, h * P:(h + 1) * P]
                        sem_ = E12["S"] if h == 3 else None
                        if c == 0:
                            v(nc.vector.tensor_copy(Sb[:, h, :], ps), sem_)
                        else:
                            v(nc.vector.scalar_tensor_tensor(Sb[:, h, :], Sb[:, h, :], eL[:, 4 * h + c:4 * h + c + 1], ps, ALU.mult, ALU.add), sem_)
                for h in range(4):
                    dve.wait_ge(E12["rs"], h + 1)
                    o = oT[:, 4 + h, :]
                    v(nc.vector.scalar_tensor_tensor(o, o, hgc[:, h:h + 1], rs12[h % 2], ALU.mult, ALU.mult), E12["n"])
                    v(tt(o, o, bgT[:, h, :], ALU.mult))
        lgrow, lbrow = SL[2][:, 0:D], SL[2][:, D:2 * D]
        sqr = R[3][:, 0:D]
        E13 = {n: sem("l_" + n) for n in ("rows", "y", "x", "sum", "nm", "var", "out", "st")}
        with nc.Block() as block:
            @block.sync
            def _(sp):
                sp.dma_start(lgrow, io["ln_g_2"].to_broadcast([P, D])).then_inc(E13["rows"], 16)
                sp.dma_start(lbrow, io["ln_b_2"].to_broadcast([P, D])).then_inc(E13["rows"], 16)
                for t in range(NT):
                    sp.wait_ge(E13["out"], t + 1)
                    sp.dma_start(io["out"][0, t * P:(t + 1) * P, :], x3[:, t, :]).then_inc(E13["st"], 16)
                sp.wait_ge(E13["st"], 16 * NT)

            @block.tensor
            def _(pe):
                pe.wait_ge(wo_in, 32)
                for t in range(NT):
                    for n in range(2):
                        for k in range(KD):
                            m = pe.matmul(PS[2 * t + n][:, :], oT[:, k, t * P:(t + 1) * P], wo_half[n][:, k, :],
                                          start=(k == 0), stop=(k == KD - 1))
                        m.then_inc(E13["y"], 1)

            @block.scalar
            def _(act):
                a = A()
                for t in range(NT):
                    s = stat[:, 8 * t:8 * t + 8]
                    act.wait_ge(E13["x"], t + 1)
                    a(nc.scalar.activation(sqr, x3[:, t, :], ACT.Copy, accum_out=s[:, 0:1]), E13["sum"])
                    act.wait_ge(E13["nm"], t + 1)
                    a(nc.scalar.activation(sqr, x3[:, t, :], ACT.Square, bias=s[:, 1:2], accum_out=s[:, 2:3]))
                    rsqrt(a, s[:, 3:4], s[:, 2:3], 1.0 / D, E13["var"], eps=LN_EPS)

            @block.vector
            def _(dve):
                v = V()
                dve.wait_ge(E13["rows"], 32)

                def finish(t):
                    s = stat[:, 8 * t:8 * t + 8]
                    dve.wait_ge(E13["var"], t + 1)
                    v(nc.vector.tensor_scalar(x3[:, t, :], x3[:, t, :], s[:, 1:2], s[:, 3:4], ALU.add, ALU.mult))
                    v(nc.vector.tensor_tensor(x3[:, t, :], x3[:, t, :], lgrow, ALU.mult))
                    v(nc.vector.tensor_tensor(x3[:, t, :], x3[:, t, :], lbrow, ALU.add), E13["out"])

                for t in range(NT):
                    for n in range(2):
                        xs = x3[:, t, n * 512:(n + 1) * 512]
                        dve.wait_ge(E13["y"], 2 * t + n + 1)
                        v(nc.vector.scalar_tensor_tensor(xs, xs, ALPHA, PS[2 * t + n][:, :], ALU.mult, ALU.add), E13["x"] if n else None)
                    dve.wait_ge(E13["sum"], t + 1)
                    v(nc.vector.tensor_scalar(stat[:, 8 * t + 1:8 * t + 2], stat[:, 8 * t:8 * t + 1], -1.0 / D, None, ALU.mult), E13["nm"])
                    if t:
                        finish(t - 1)
                finish(NT - 1)


def kernel(**inputs):
    import concourse.bacc as bacc
    from concourse.bass_utils import run_bass_kernel_spmd

    nc = bacc.Bacc("TRN2", target_bir_lowering=False, num_devices=1)
    arrays = {name: np.ascontiguousarray(a) for name, a in inputs.items()}
    arrays["table"] = shape_table()
    io = {name: nc.dram_tensor(name, a.shape, mybir.dt.from_np(a.dtype), kind="ExternalInput").ap()
          for name, a in arrays.items()}
    io["scratch"] = nc.dram_tensor("scratch", [4, P * REL], F32, kind="Internal").ap()
    io["out"] = nc.dram_tensor("y", [1, S, D], F32, kind="ExternalOutput").ap()
    build(nc, io)
    result = run_bass_kernel_spmd(nc, [arrays], core_ids=[0])
    return result.results[0]["y"]
```
